# Optimizing a Trainium2 kernel written in Bass

```python
import jax, jax.numpy as jnp
from jax import lax
import numpy as np

D_MODEL = 1024
BATCH = 1
SEQ = 128
DEPTH = 2
DEC_BATCH = 1
DEC_SEQ = 512
PAST_LEN = 256

GRID_W = 64
D_FF = 2816
FOUR_GROUPS = 4
FOUR_GROUP_DIM = 64
D_FOUR = FOUR_GROUPS * FOUR_GROUP_DIM
N_HEADS = 8
QK_NOPE = 64
QK_ROPE = 32
V_DIM = 64
Q_RANK = 384
KV_RANK = 256
N_BRANCH = 2
IN_W = D_FOUR + Q_RANK + KV_RANK + QK_ROPE + N_BRANCH * D_MODEL
N_MOD = 9
ROPE_BASE = 10000.0
EPS = 1e-6
Q_BLOCK = 128

kernel_name = "hybrid_fnet_mla_macaron_step"

def _rmsnorm(x, g):
    xf = x.astype(jnp.float32)
    y = xf * lax.rsqrt(jnp.mean(xf * xf, axis=-1, keepdims=True) + EPS)
    return (y * g.astype(jnp.float32)).astype(x.dtype)

def _swiglu(h, wg, wu, wd):
    return (jax.nn.silu(h @ wg) * (h @ wu)) @ wd

def _axial_tables(n_tok):
    rows = n_tok // GRID_W
    row = jnp.repeat(jnp.arange(rows), GRID_W).astype(jnp.float32)
    col = jnp.tile(jnp.arange(GRID_W), rows).astype(jnp.float32)
    axis_dim = QK_ROPE // 2
    inv = ROPE_BASE ** (-jnp.arange(0, axis_dim, 2, dtype=jnp.float32) / axis_dim)
    ar = row[:, None] * inv
    ac = col[:, None] * inv
    return (jnp.cos(ar), jnp.sin(ar), jnp.cos(ac), jnp.sin(ac))

def _rot_half(x, cos, sin):
    m = x.shape[-1] // 2
    x1, x2 = x[..., :m], x[..., m:]
    return jnp.concatenate([x1 * cos - x2 * sin, x2 * cos + x1 * sin], axis=-1)

def _axial_rope(x, tables):
    cr, sr, cc, sc = tables
    if x.ndim == 4:
        cr, sr, cc, sc = cr[:, None], sr[:, None], cc[:, None], sc[:, None]
    xf = x.astype(jnp.float32)
    half = QK_ROPE // 2
    out = jnp.concatenate([_rot_half(xf[..., :half], cr, sr), _rot_half(xf[..., half:], cc, sc)], axis=-1)
    return out.astype(x.dtype)

def _attend(q, k, v):
    B, N, H, Dh = q.shape
    scale = Dh ** -0.5
    nb = N // Q_BLOCK
    qb = q.reshape(B, nb, Q_BLOCK, H, Dh).swapaxes(0, 1)

    def one(qi):
        s = jnp.einsum("bqhd,bkhd->bhqk", qi, k).astype(jnp.float32) * scale
        p = jax.nn.softmax(s, axis=-1).astype(v.dtype)
        return jnp.einsum("bhqk,bkhd->bqhd", p, v)

    o = lax.map(one, qb)
    return o.swapaxes(0, 1).reshape(B, N, H, v.shape[-1])

def _mixer(h, p, tables, ctx_ckv, ctx_krope):
    B, N, _ = h.shape
    proj = h @ p["w_in"]
    cuts = [D_FOUR, D_FOUR + Q_RANK, D_FOUR + Q_RANK + KV_RANK, D_FOUR + Q_RANK + KV_RANK + QK_ROPE,
            D_FOUR + Q_RANK + KV_RANK + QK_ROPE + D_MODEL]
    f_in, q_lat, ckv, krope, g_f, g_a = jnp.split(proj, cuts, axis=-1)

    fg = f_in.reshape(B, N, FOUR_GROUPS, FOUR_GROUP_DIM).astype(jnp.float32)
    fr = jnp.real(jnp.fft.fft2(fg, axes=(1, 3), norm="ortho")).astype(h.dtype).reshape(B, N, D_FOUR)
    a_out = fr @ p["w_four"]

    q = (_rmsnorm(q_lat, p["q_norm"]) @ p["w_uq"]).reshape(B, N, N_HEADS, QK_NOPE + QK_ROPE)
    q_nope, q_rope = q[..., :QK_NOPE], q[..., QK_NOPE:]
    ckv_n = _rmsnorm(ckv, p["kv_norm"])
    if tables is not None:
        q_rope = _axial_rope(q_rope, tables)
        k_rope_own = _axial_rope(krope, tables)
    else:
        k_rope_own = krope
    key_ckv, key_rope = ckv_n, k_rope_own
    if ctx_ckv is not None:
        key_ckv = jnp.concatenate([ckv_n, ctx_ckv], axis=1)
        key_rope = jnp.concatenate([k_rope_own, ctx_krope], axis=1)
    M = key_ckv.shape[1]
    kv = (key_ckv @ p["w_ukv"]).reshape(B, M, N_HEADS, QK_NOPE + V_DIM)
    k_nope, v = kv[..., :QK_NOPE], kv[..., QK_NOPE:]
    q_full = jnp.concatenate([q_nope, q_rope], axis=-1)
    k_full = jnp.concatenate([k_nope, jnp.broadcast_to(key_rope[:, :, None, :], (B, M, N_HEADS, QK_ROPE))], axis=-1)
    o = _attend(q_full, k_full, v).reshape(B, N, N_HEADS * V_DIM) @ p["w_attn_proj"]

    merged = jax.nn.sigmoid(g_f) * a_out + jax.nn.sigmoid(g_a) * o
    return merged @ p["w_out"], ckv_n, krope

def _layer(x, mod, p, tables, ctx_ckv, ctx_krope):
    sh1, sc1, g1, sh2, sc2, g2, sh3, sc3, g3 = jnp.split(mod, N_MOD, axis=-1)
    h = _rmsnorm(x, p["norm_ffn1"]) * (1 + sc1) + sh1
    x = x + 0.5 * g1 * _swiglu(h, p["w_ffn1_gate"], p["w_ffn1_up"], p["w_ffn1_down"])
    h = _rmsnorm(x, p["norm_mix"]) * (1 + sc2) + sh2
    m, ckv_n, krope = _mixer(h, p, tables, ctx_ckv, ctx_krope)
    x = x + g2 * m
    h = _rmsnorm(x, p["norm_ffn2"]) * (1 + sc3) + sh3
    x = x + 0.5 * g3 * _swiglu(h, p["w_ffn2_gate"], p["w_ffn2_up"], p["w_ffn2_down"])
    return x, ckv_n, krope

def setup_inputs(seed: int = 0) -> dict:
    key = jax.random.key(seed)
    ks = iter(jax.random.split(key, 40))

    def nrm(shape, scale=1.0):
        return jax.random.normal(next(ks), shape, jnp.float32) * scale

    def gain(shape):
        return 1.0 + 0.05 * jax.random.normal(next(ks), shape, jnp.float32)

    L, D = DEPTH, D_MODEL
    return {
        "x_prompt": nrm((BATCH, SEQ, D)),
        "x_sample": nrm((DEC_BATCH, DEC_SEQ, D)),
        "cache_ckv": nrm((DEC_BATCH, DEPTH, PAST_LEN, KV_RANK)),
        "cache_krope": nrm((DEC_BATCH, DEPTH, PAST_LEN, QK_ROPE)),
        "c": nrm((DEC_BATCH, D)),
        "c_ctx": nrm((D,)),
        "w_mod": nrm((L, D, N_MOD * D), 0.5 * D ** -0.5),
        "b_mod": nrm((L, N_MOD * D), 0.01),
        "norm_ffn1": gain((L, D)),
        "w_ffn1_gate": nrm((L, D, D_FF), D ** -0.5),
        "w_ffn1_up": nrm((L, D, D_FF), D ** -0.5),
        "w_ffn1_down": nrm((L, D_FF, D), D_FF ** -0.5),
        "norm_mix": gain((L, D)),
        "w_in": nrm((L, D, IN_W), D ** -0.5),
        "w_four": nrm((L, D_FOUR, D), D_FOUR ** -0.5),
        "q_norm": gain((L, Q_RANK)),
        "w_uq": nrm((L, Q_RANK, N_HEADS * (QK_NOPE + QK_ROPE)), Q_RANK ** -0.5),
        "kv_norm": gain((L, KV_RANK)),
        "w_ukv": nrm((L, KV_RANK, N_HEADS * (QK_NOPE + V_DIM)), KV_RANK ** -0.5),
        "w_attn_proj": nrm((L, N_HEADS * V_DIM, D), (N_HEADS * V_DIM) ** -0.5),
        "w_out": nrm((L, D, D), D ** -0.5),
        "norm_ffn2": gain((L, D)),
        "w_ffn2_gate": nrm((L, D, D_FF), D ** -0.5),
        "w_ffn2_up": nrm((L, D, D_FF), D ** -0.5),
        "w_ffn2_down": nrm((L, D_FF, D), D_FF ** -0.5),
        "final_norm": gain((D,)),
    }

def reference(x_prompt, x_sample, cache_ckv, cache_krope, c, c_ctx, w_mod, b_mod, norm_ffn1, w_ffn1_gate,
              w_ffn1_up, w_ffn1_down, norm_mix, w_in, w_four, q_norm, w_uq, kv_norm, w_ukv, w_attn_proj,
              w_out, norm_ffn2, w_ffn2_gate, w_ffn2_up, w_ffn2_down, final_norm):
    tables = _axial_tables(x_sample.shape[1])
    xp, xs = x_prompt, x_sample
    ckvs, krs = [], []
    for l in range(DEPTH):
        p = {"norm_ffn1": norm_ffn1[l], "w_ffn1_gate": w_ffn1_gate[l], "w_ffn1_up": w_ffn1_up[l],
             "w_ffn1_down": w_ffn1_down[l], "norm_mix": norm_mix[l], "w_in": w_in[l], "w_four": w_four[l],
             "q_norm": q_norm[l], "w_uq": w_uq[l], "kv_norm": kv_norm[l], "w_ukv": w_ukv[l],
             "w_attn_proj": w_attn_proj[l], "w_out": w_out[l], "norm_ffn2": norm_ffn2[l],
             "w_ffn2_gate": w_ffn2_gate[l], "w_ffn2_up": w_ffn2_up[l], "w_ffn2_down": w_ffn2_down[l]}
        mod_ctx = (jax.nn.silu(c_ctx) @ w_mod[l] + b_mod[l])[None, None, :]
        mod_lat = (jax.nn.silu(c) @ w_mod[l] + b_mod[l])[:, None, :]
        xp, ckv_l, kr_l = _layer(xp, mod_ctx, p, None, None, None)
        ckvs.append(ckv_l)
        krs.append(kr_l)
        xs, _, _ = _layer(xs, mod_lat, p, tables, cache_ckv[:, l], cache_krope[:, l])
    y_prompt = _rmsnorm(xp, final_norm)
    y_sample = _rmsnorm(xs, final_norm)
    new_ckv = jnp.stack(ckvs, axis=1)
    new_krope = jnp.stack(krs, axis=1)
    return (y_prompt, y_sample, new_ckv, new_krope)


_drawn_inputs = setup_inputs


def setup_inputs(seed=0):
    import zlib

    import numpy as np

    out = dict(_drawn_inputs(seed))
    spreads = {}
    factors = {'cache_ckv': 7.291,
     'cache_krope': 8.0,
     'b_mod': 3.78,
     'norm_ffn1': 5.409,
     'q_norm': 8.0,
     'norm_ffn2': 5.074}
    for name, (base, spread) in spreads.items():
        noise = np.random.default_rng([zlib.crc32(name.encode()), seed]).standard_normal(out[name].shape)
        drawn = base * np.exp(spread * noise) if base else spread * noise
        out[name] = __import__('jax').numpy.asarray(drawn.astype(out[name].dtype))
    for name, factor in factors.items():
        out[name] = (out[name] * factor).astype(out[name].dtype)
    return out
```

```python
import numpy as np
import concourse.bass as bass
from concourse import mybir
from concourse.alu_op_type import AluOpType as ALU
from contextlib import ExitStack

F32 = mybir.dt.float32
F32R = mybir.dt.float32r
ACT = mybir.ActivationFunctionType
AX = mybir.AxisListType

P = 128
DEPTH = 2
D = 1024
KT = D // P
D_FF = 2816
FH = D_FF // P // 2
SAMPLE, PROMPT, PAST = 512, 128, 256
T = SAMPLE + PROMPT
HALF = T // 2
S2 = SAMPLE // 2
PRO = S2
STEP = S2 + PROMPT
TOK = [0, P, STEP, STEP + P, PRO]
KEYS = T + PAST
GRID_W = 64
HEADS, NOPE, ROPE, VD = 8, 64, 32, 64
QK = NOPE + ROPE
Q_RANK, KV_RANK = 384, 256
QT, CT = Q_RANK // P, KV_RANK // P
D_FOUR, FD = 256, 64
FT = D_FOUR // P
OT = HEADS * VD // P
EPS = 1e-6
SCALE = float(QK) ** -0.5
N_MOD = 9
MOD_BATCHES, MOD_COLS = 6, 384
MB = 4 * MOD_COLS

UP_W = KT * P
DOWN_W = FH * P
IN_W = KT * P
CHAN_W = 2 * P
PDFT_W = 2 * P
SDFT_W = 2 * SAMPLE
HEAD_W = QT * P + CT * (NOPE + VD)
MERGE_W = (2 * KT + OT + FT) * P // 2
OUT_W = KT * P
SLOT = DOWN_W

FFN_PAIRS = 2 * (FH + KT // 2)
IN_P, DFT_P, SEQ_P, HEAD_P, MERGE_P, OUT_P = 0, 4, 5, 7, 11, 19
MIX_PAIRS = OUT_P + KT // 2
LAYER_PAIRS = 2 * FFN_PAIRS + MIX_PAIRS
CREDIT = 2
UPD = 5 * KT
START = 1
XUPD0 = KT
UNITS = 5


def two(v):
    return bass.AP(v.tensor, v.offset, [v.ap[0], (STEP, 2), (1, S2)])


def pro(v):
    return v[:, PRO:PRO + PROMPT]


def groups(*views):
    return [(0, [two(v) for v in views]), (1, [pro(v) for v in views])]


def build(nc, i, o):
    ctx = ExitStack()
    with ctx:
        def sb(name, shape, dt=F32, where=ctx):
            return where.enter_context(nc.sbuf_tensor(name, shape, dt))

        def sem(name):
            return ctx.enter_context(nc.semaphore(name))

        x = sb("x", [P, KT, T])
        h_hi, h_lo = sb("h_hi", [P, KT, T], F32R), sb("h_lo", [P, KT, T], F32R)
        raw = [sb(f"raw{s}", [P, SLOT]) for s in range(2)]
        w_hi = [sb(f"w_hi{s}", [P, SLOT], F32R) for s in range(2)]
        w_lo = [sb(f"w_lo{s}", [P, SLOT], F32R) for s in range(2)]
        tmp = sb("tmp", [P, 6 * T])
        sq, std, ta, tb, rstd, acc = [tmp[:, n * T:(n + 1) * T] for n in range(6)]
        rope_tab = sb("rope_tab", [P, T])
        ones = sb("ones", [P, P])
        ident = sb("ident", [P, P])
        cond = sb("cond", [P, KT, 32])
        cond_in = sb("cond_in", [P, KT, 2])
        bmod = sb("bmod", [P, DEPTH, N_MOD * KT])
        gains = sb("gains", [P, DEPTH, 3, KT])
        lat_gain = sb("lat_gain", [P, DEPTH, QT + CT])
        fin_gain = sb("fin_gain", [P, KT])
        mod = sb("mod", [P, 2, N_MOD * KT])
        scale_a = sb("scale_a", [P, 2, KT])
        half_g = sb("half_g", [P, 2, KT])
        mod_row = sb("mod_row", [P, MOD_COLS])
        eps = sb("eps", [P, 1])
        mx, nmx, rsum, rinv = [sb(n, [P, UNITS]) for n in ("mx", "nmx", "rsum", "rinv")]

        with ExitStack() as ffn:
            a_hi, a_lo = sb("a_hi", [P, FH, T], F32R, ffn), sb("a_lo", [P, FH, T], F32R, ffn)
            wm = [sb(f"wm{s}", [P, MB], F32, ffn) for s in range(2)]
        with ExitStack() as mix:
            fr_hi, fr_lo = sb("fr_hi", [P, FT, T], F32R, mix), sb("fr_lo", [P, FT, T], F32R, mix)
            with ExitStack() as four:
                uv_hi = sb("uv_hi", [P, UNITS, 2 * FT * P], F32R, four)
                uv_lo = sb("uv_lo", [P, UNITS, 2 * FT * P], F32R, four)
            ot_hi, ot_lo = sb("ot_hi", [P, OT, T], F32R, mix), sb("ot_lo", [P, OT, T], F32R, mix)
            with ExitStack() as att:
                qn_hi, qn_lo = sb("qn_hi", [P, QT, T], F32R, att), sb("qn_lo", [P, QT, T], F32R, att)
                cn_hi, cn_lo = sb("cn_hi", [P, CT, KEYS], F32R, att), sb("cn_lo", [P, CT, KEYS], F32R, att)
                k_hi, k_lo = sb("k_hi", [P, KEYS], F32R, att), sb("k_lo", [P, KEYS], F32R, att)
                with ExitStack() as pre:
                    lat = sb("lat", [P, QT + CT, T], F32, pre)
                    f_hi, f_lo = sb("f_hi", [P, FT, T], F32R, pre), sb("f_lo", [P, FT, T], F32R, pre)
                    past_c = sb("past_c", [P, CT, PAST], F32, pre)
                    past_k = sb("past_k", [P, PAST], F32, pre)
                with ExitStack() as head:
                    q_hi, q_lo = sb("q_hi", [P, T], F32R, head), sb("q_lo", [P, T], F32R, head)
                    v_hi = sb("v_hi", [P, KEYS // P, VD], F32R, head)
                    v_lo = sb("v_lo", [P, KEYS // P, VD], F32R, head)
                    pt_hi = sb("pt_hi", [P, 2, SAMPLE + PAST], F32R, head)
                    pt_lo = sb("pt_lo", [P, 2, SAMPLE + PAST], F32R, head)
            with ExitStack() as mer:
                m_hi, m_lo = sb("m_hi", [P, KT, T], F32R, mer), sb("m_lo", [P, KT, T], F32R, mer)
        NK = SAMPLE + PAST
        probs = [tmp[:, u * NK:(u + 1) * NK] for u in range(2)]
        q32 = tmp[:, 2 * NK:2 * NK + T]
        rot = tmp[:, 2 * NK + T:2 * NK + 2 * T]
        kr32, kr_sin, kr_cos = sq, std, ta
        lat_sq, lat_std, lat_acc = tb, rstd, acc
        silu, prod = ta, tb
        sgf, sga, p1, p2 = sq, std, ta, tb

        ps = ctx.enter_context(nc.psum_tensor("ps", [P, 8 * 512], F32))

        def bank(b, n0=0, n1=512):
            return ps[:, b * 512 + n0:b * 512 + n1]

        def pair(j):
            return ps[:, j * 1024 + 512 - HALF:j * 1024 + 512 + HALF]

        def halves(v):
            return [v[:, 0:HALF], v[:, HALF:T]]

        s_raw = [sem(f"raw_loaded{s}") for s in range(2)]
        s_whi = sem("weight_hi_ready")
        s_split = sem("chunk_split")
        s_chunk = sem("chunk_used")
        s_wm = [sem(f"mod_weights_loaded{s}") for s in range(2)]
        s_wmused = sem("mod_weights_used")
        s_modmm, s_modrow, s_modt, s_mod = sem("mod_rows_summed"), sem("mod_rows_copied"), \
            sem("mod_transposed"), sem("mod_ready")
        s_const, s_fill, s_x = sem("constants_loaded"), sem("constants_filled"), sem("x_loaded")
        s_cond = sem("cond_ready")
        s_xupd, s_sq, s_acc = sem("x_updated"), sem("square_ready"), sem("squares_added")
        s_sum, s_std, s_rstd = sem("squares_summed"), sem("std_ready"), sem("rstd_ready")
        s_coef, s_half = sem("coefficients_ready"), sem("half_gates_ready")
        s_t, s_hhi, s_hlo = sem("scaled_ready"), sem("h_hi_ready"), sem("h_ready")
        s_silu, s_prod, s_ahi, s_alo = sem("silu_ready"), sem("product_ready"), sem("a_hi_ready"), sem("a_ready")
        s_lat, s_flo = sem("latent_copied"), sem("f_ready")
        s_lsq, s_lacc, s_lsum, s_lstd = sem("latent_square"), sem("latent_squares_added"), \
            sem("latent_summed"), sem("latent_std")
        s_lrstd, s_latn, s_nhi, s_nlo = sem("latent_rstd"), sem("latent_normed"), \
            sem("latent_hi_ready"), sem("latent_ready")
        s_past = sem("past_loaded")
        s_kr, s_krhi, s_krlo = sem("key_rope_step"), sem("key_rope_hi"), sem("key_rope_ready")
        s_pasthi, s_pastlo = sem("past_hi"), sem("past_ready")
        s_chan, s_uvhi, s_uvlo = sem("channel_dft"), sem("uv_hi"), sem("uv_ready")
        s_frhi, s_frlo = sem("fourier_hi"), sem("fourier_ready")
        s_qmm, s_kmm = sem("q_product"), sem("k_product")
        s_q32, s_rot, s_qhi, s_qlo = sem("q_copied"), sem("q_rotate_step"), sem("q_hi_ready"), sem("q_ready")
        s_khi, s_klo, s_vhi, s_vlo = sem("k_hi_ready"), sem("k_ready"), sem("v_hi_ready"), sem("v_ready")
        s_s, s_mx, s_nmx, s_exp = sem("scores_ready"), sem("max_ready"), sem("neg_max_ready"), sem("exp_ready")
        s_rinv, s_pn, s_pt, s_pthi, s_ptlo = sem("row_inverse"), sem("probs_ready"), \
            sem("probs_transposed"), sem("probs_t_hi"), sem("probs_t_ready")
        s_pv, s_ohi, s_olo = sem("values_mixed"), sem("o_hi_ready"), sem("o_ready")
        s_gf, s_op, s_ga = sem("gate_f_product"), sem("attn_out_product"), sem("gate_a_product")
        s_sgf, s_sga, s_p1, s_p2, s_m = sem("sigmoid_f"), sem("sigmoid_a"), sem("gated_fourier"), \
            sem("gated_attention"), sem("merged")
        s_mhi, s_mlo = sem("merged_hi"), sem("merged_ready")
        s_out, s_y = sem("outputs_written"), sem("y_ready")

        block = ctx.enter_context(nc.Block())

        def used(p, s):
            return (p * 2 + s) + 1 + CREDIT

        @block.sync
        def _(sp):
            for dst, src in ((cond_in, i["cond"]), (bmod, i["b_mod"]), (gains, i["gains"]),
                             (lat_gain, i["lat_gains"]), (fin_gain, i["fin_gain"])):
                sp.dma_start(dst[:], src).then_inc(s_const, 16)
            sp.dma_start(rope_tab[NOPE:P, :], i["rope"]).then_inc(s_const, 16)
            sp.dma_start(x[:], i["x"]).then_inc(s_x, 16)

            def load(p, s, width, src):
                sp.wait_ge(s_split, p * 2 + s + 1)
                sp.dma_start(raw[s][:, 0:width], src).then_inc(s_raw[s], 16)

            def ffn_chunks(l, f, base):
                for half in range(2):
                    up = base + half * (FH + KT // 2)
                    with sp.Fori(0, FH) as t:
                        for s in range(2):
                            load(up + t, s, UP_W, i["w_up"][l, f, t + half * FH, s])
                    with sp.Fori(0, KT // 2) as t:
                        for s in range(2):
                            load(up + FH + t, s, DOWN_W, i["w_down"][l, f, half, t * 2 + s])

            with sp.Fori(0, DEPTH) as l:
                base = l * LAYER_PAIRS
                ffn_chunks(l, 0, base)
                mixp = base + FFN_PAIRS
                with sp.Fori(0, 4) as t:
                    for s in range(2):
                        load(mixp + IN_P + t, s, IN_W, i["w_in"][l, t * 2 + s])
                load(mixp + DFT_P, 0, CHAN_W, i["dft_chan"])
                load(mixp + DFT_P, 1, PDFT_W, i["dft_prompt"])
                with sp.Fori(0, 2) as t:
                    for s in range(2):
                        load(mixp + SEQ_P + t, s, SDFT_W, i["dft_sample"][t * 2 + s])
                with sp.Fori(0, HEADS // 2) as t:
                    for s in range(2):
                        load(mixp + HEAD_P + t, s, HEAD_W, i["w_head"][l, t * 2 + s])
                with sp.Fori(0, KT) as t:
                    for s in range(2):
                        load(mixp + MERGE_P + t, s, MERGE_W, i["w_merge"][l, t, s])
                with sp.Fori(0, KT // 2) as t:
                    for s in range(2):
                        load(mixp + OUT_P + t, s, OUT_W, i["w_out"][l, t * 2 + s])
                ffn_chunks(l, 1, mixp + MIX_PAIRS)
            for k in range(KT):
                sp.wait_ge(s_y, k + 1)
                sp.dma_start(o["y"][:, k], x[:, k, :]).then_inc(s_out, 16)
            sp.wait_ge(s_out, 16 * (2 * DEPTH + KT))

        @block.gpsimd
        def _(pool):
            pool.sem_inc(s_split, CREDIT)
            nc.gpsimd.memset(ones[:], 1.0).then_inc(s_fill, 1)
            nc.gpsimd.memset(eps[:], EPS).then_inc(s_fill, 1)
            nc.gpsimd.memset(cond[:], 0.0).then_inc(s_fill, 1)
            nc.gpsimd.memset(ident[:], 0.0).then_inc(s_fill, 1)
            pool.wait_ge(s_fill, 4)
            nc.gpsimd.affine_select(out=ident[:], in_=ident[:], compare_op=ALU.not_equal, fill=1.0, base=0,
                                    pattern=[[-1, P]], channel_multiplier=1).then_inc(s_fill, 1)

            def split(p, s, width):
                r, hi, lo = raw[s][:, 0:width], w_hi[s][:, 0:width], w_lo[s][:, 0:width]
                pool.wait_ge(s_raw[s], (p + 1) * 16)
                pool.wait_ge(s_chunk, p * 2 + s + 1)
                nc.gpsimd.tensor_tensor(hi, r, ones[:, 0:1].to_broadcast([P, width]), ALU.mult).then_inc(s_whi, 1)
                pool.wait_ge(s_whi, p * 2 + s + 1)
                nc.gpsimd.tensor_tensor(lo, r, hi.bitcast(F32), ALU.subtract).then_inc(s_split, 1)

            def pairs(first, count, width):
                with pool.Fori(0, count) as t:
                    for s in range(2):
                        split(first + t, s, width)

            def ffn_chunks(base):
                for half in range(2):
                    up = base + half * (FH + KT // 2)
                    pairs(up, FH, UP_W)
                    pairs(up + FH, KT // 2, DOWN_W)

            with pool.Fori(0, DEPTH) as l:
                base = l * LAYER_PAIRS
                ffn_chunks(base)
                mixp = base + FFN_PAIRS
                pairs(mixp + IN_P, 4, IN_W)
                split(mixp + DFT_P, 0, CHAN_W)
                split(mixp + DFT_P, 1, PDFT_W)
                pairs(mixp + SEQ_P, 2, SDFT_W)
                pairs(mixp + HEAD_P, HEADS // 2, HEAD_W)
                pairs(mixp + MERGE_P, KT, MERGE_W)
                pairs(mixp + OUT_P, KT // 2, OUT_W)
                ffn_chunks(mixp + MIX_PAIRS)

        @block.tensor
        def _(pe):
            pe.sem_inc(s_chunk, CREDIT)
            pe.sem_inc(s_wmused, CREDIT)
            for started in (s_modt, s_pt, s_pv):
                pe.sem_inc(started, START)

            def product(outs, whi, wlo, xhi, xlo, first, last):
                for n, (out, v) in enumerate(zip(outs, xhi)):
                    nc.tensor.matmul(out, whi, v, start=first, stop=False)
                for out, v in zip(outs, xlo):
                    nc.tensor.matmul(out, whi, v, start=False, stop=False)
                for out, v in zip(outs, xhi):
                    mm = nc.tensor.matmul(out, wlo, v, start=False, stop=last)
                return mm

            def w_tile(s, n):
                return w_hi[s][:, n * P:(n + 1) * P], w_lo[s][:, n * P:(n + 1) * P]

            def dense(out, s, tiles, xhi, xlo, before=None, first=True, last=True):
                for n, (wt, k) in enumerate(tiles):
                    if before:
                        before(k)
                    mm = product(halves(out), *w_tile(s, wt), halves(xhi[:, k, :]), halves(xlo[:, k, :]),
                                 first and n == 0, last and n == len(tiles) - 1)
                return mm

            def chunk(p, s):
                pe.wait_ge(s_split, p * 2 + s + 1 + CREDIT)

            def norm_sum(nn):
                pe.wait_ge(s_acc, (nn + 1) * (KT + 1))
                for n in range(2):
                    mm = nc.tensor.matmul(halves(pair(3))[n], ones[:], halves(acc)[n], start=True, stop=True)
                mm.then_inc(s_sum, 1)

            def mod_step(e, k):
                pe.wait_ge(s_wm[k % 2], (e * (KT // 2) + k // 2 + 1) * 16)
                if k == 0:
                    pe.wait_ge(s_modrow, e + START)
                for j in range(4):
                    mm = nc.tensor.matmul(bank(4)[32 * j:32 * j + 32, 0:MOD_COLS], cond[:, k, :],
                                          wm[k % 2][:, j * MOD_COLS:(j + 1) * MOD_COLS],
                                          start=(k == 0), stop=(k == KT - 1))
                mm.then_inc(s_wmused, 1)

            def mod_turn(e):
                pe.wait_ge(s_modrow, e + 1 + START)
                pe.wait_ge(s_mod, e + START)
                for b in range(MOD_COLS // P):
                    mm = nc.tensor.transpose(bank(5)[:, b * P:(b + 1) * P], mod_row[:, b * P:(b + 1) * P], ident[:])
                mm.then_inc(s_modt, 1)

            def ffn_step(l, f, base, nn, mods):
                for half in range(2):
                    up = base + half * (FH + KT // 2)
                    g0 = (l * 2 + f) * 2 * FH + half * FH
                    with pe.Fori(0, FH) as t:
                        chunk(up + t, 0)
                        pe.wait_ge(s_silu, g0 + t + START)
                        if half:
                            pe.wait_ge(s_xupd, XUPD0 + l * UPD + f * 3 * KT + KT)
                        dense(pair(0), 0, [(k, k) for k in range(KT)], h_hi, h_lo,
                              lambda k: pe.wait_ge(s_hlo, nn * KT + k + 1 + START)).then_inc(s_chunk, 1)
                        chunk(up + t, 1)
                        pe.wait_ge(s_prod, g0 + t + START)
                        dense(pair(1), 1, [(k, k) for k in range(KT)], h_hi, h_lo).then_inc(s_chunk, 1)
                    upd0 = XUPD0 + l * UPD + f * 3 * KT + half * KT
                    with pe.Fori(0, 2) as t:
                        for m in range(4):
                            chunk(up + FH + t * 2 + m // 2, m % 2)
                            pe.wait_ge(s_xupd, upd0 + t * 4 + m - 1)
                            if m == 0:
                                pe.wait_ge(s_silu, g0 + FH + START)
                            dense(pair(m % 2), m % 2, [(k, k) for k in range(FH)], a_hi, a_lo,
                                  lambda k: pe.wait_ge(s_alo, g0 + k + 1 + START)).then_inc(s_chunk, 1)
                            if mods is not None and mods[half] is not None:
                                mod_step(mods[half] + t, 2 * m)
                                mod_step(mods[half] + t, 2 * m + 1)
                        if mods is not None and mods[half] is not None:
                            mod_turn(mods[half] + t)

            def mixer_step(l, mixp, nn):
                for t in range(8):
                    chunk(mixp + IN_P + t // 2, t % 2)
                    if t >= 2:
                        pe.wait_ge(s_lat, l * 8 + t - 1)
                    dense(pair(t % 2), t % 2, [(k, k) for k in range(KT)], h_hi, h_lo,
                          (lambda k: pe.wait_ge(s_hlo, nn * KT + k + 1 + START)) if t == 0 else None).then_inc(s_chunk, 1)
                    if t >= 6:
                        pe.wait_ge(s_lacc, l * (QT + CT) + (QT if t == 6 else QT + CT))
                        for n in range(2):
                            mm = nc.tensor.matmul(halves(pair(t - 4))[n], ones[:], halves(lat_acc)[n],
                                                  start=True, stop=True)
                        mm.then_inc(s_lsum, 1)
                chunk(mixp + DFT_P, 0)
                pe.wait_ge(s_flo, (l + 1) * FT)
                bd_hi, bd_lo = w_hi[0][:, 0:CHAN_W], w_lo[0][:, 0:CHAN_W]
                for t in range(UNITS):
                    if t == 4:
                        pe.wait_ge(s_uvlo, l * UNITS + 1)
                    for c in range(FT):
                        tok = slice(TOK[t], TOK[t] + P)
                        mm = product([bank(t % 4, c * CHAN_W, (c + 1) * CHAN_W)], f_hi[:, c, tok], f_lo[:, c, tok],
                                     [bd_hi], [bd_lo], True, True)
                    mm.then_inc(s_chan if t < 4 else s_chunk, 1)
                chunk(mixp + DFT_P, 1)
                pe.wait_ge(s_uvlo, (l + 1) * UNITS)
                for c in range(FT):
                    for n in range(2):
                        st = slice((2 * c + n) * P, (2 * c + n + 1) * P)
                        mm = product([bank(1, c * P, (c + 1) * P)], uv_hi[:, 4, st], uv_lo[:, 4, st],
                                     [w_hi[1][:, n * P:(n + 1) * P]], [w_lo[1][:, n * P:(n + 1) * P]], n == 0, n == 1)
                mm.then_inc(s_chunk, 1)
                for t in range(4):
                    chunk(mixp + SEQ_P + t // 2, t % 2)
                    for c in range(FT):
                        for n in range(2):
                            st = slice((2 * c + n) * P, (2 * c + n + 1) * P)
                            mv = slice(n * SAMPLE, (n + 1) * SAMPLE)
                            mm = product([bank(2 + c)], uv_hi[:, t, st], uv_lo[:, t, st],
                                         [w_hi[t % 2][:, mv]], [w_lo[t % 2][:, mv]],
                                         t == 0 and n == 0, t == 3 and n == 1)
                    mm.then_inc(s_chunk, 1)
                with pe.Fori(0, HEADS // 2) as t:
                    for s in range(2):
                        if s == 0:
                            pe.wait_ge(s_frlo, (l + 1) * 3)
                            pe.wait_ge(s_nlo, (l + 1) * (QT + CT))
                            pe.wait_ge(s_pastlo, (l + 1) * 2)
                            pe.wait_ge(s_krlo, l + 1)
                        attend(l * HEADS + t * 2 + s, mixp + HEAD_P + t, s)
                with pe.Fori(0, KT) as m:
                    n0 = l * KT + m
                    chunk(mixp + MERGE_P + m, 0)
                    pe.wait_ge(s_sgf, n0 + START)
                    dense(pair(0), 0, [(k, k) for k in range(KT)], h_hi, h_lo).then_inc(s_gf, 1)
                    pe.wait_ge(s_p2, n0 + START)
                    pe.wait_ge(s_olo, (l + 1) * 2 * HEADS + START)
                    dense(pair(1), 0, [(KT + k, k) for k in range(3)], ot_hi, ot_lo, last=False).then_inc(s_chunk, 1)
                    chunk(mixp + MERGE_P + m, 1)
                    dense(pair(1), 1, [(KT, 3)], ot_hi, ot_lo, first=False).then_inc(s_op, 1)
                    pe.wait_ge(s_sga, n0 + START)
                    dense(pair(2), 1, [(k, k) for k in range(KT)], h_hi, h_lo).then_inc(s_ga, 1)
                    pe.wait_ge(s_p1, n0 + START)
                    dense(pair(3), 1, [(KT + 1 + k, k) for k in range(FT)], fr_hi, fr_lo).then_inc(s_chunk, 1)
                upd0 = XUPD0 + l * UPD + 2 * KT
                with pe.Fori(0, KT // 2) as t:
                    for s in range(2):
                        chunk(mixp + OUT_P + t, s)
                        pe.wait_ge(s_xupd, upd0 + t * 2 + s - 1)
                        pe.wait_ge(s_p2 if s else s_sgf, (l + 1) * KT + START)
                        dense(pair(s), s, [(k, k) for k in range(KT)], m_hi, m_lo,
                              lambda k: pe.wait_ge(s_mlo, l * KT + k + 1 + START)).then_inc(s_chunk, 1)

            def attend(hd, p, s):
                u0 = hd * UNITS
                chunk(p, s)
                pe.wait_ge(s_exp, u0 + START)
                dense(pair(0), s, [(k, k) for k in range(QT)], qn_hi, qn_lo).then_inc(s_qmm, 1)
                k0, v0 = QT * P, QT * P + CT * NOPE
                for c in range(CT):
                    w = slice(k0 + c * NOPE, k0 + (c + 1) * NOPE)
                    mm = product([bank(2 + n, 0, KEYS // 2)[0:NOPE] for n in range(2)], w_hi[s][:, w], w_lo[s][:, w],
                                 [cn_hi[:, c, n * KEYS // 2:(n + 1) * KEYS // 2] for n in range(2)],
                                 [cn_lo[:, c, n * KEYS // 2:(n + 1) * KEYS // 2] for n in range(2)],
                                 c == 0, c == CT - 1)
                mm.then_inc(s_kmm, 1)
                for n, col in enumerate(TOK[0:4] + [T, T + P, PRO]):
                    for c in range(CT):
                        w = slice(v0 + c * VD, v0 + (c + 1) * VD)
                        mm = product([bank(4, n * VD, (n + 1) * VD)], cn_hi[:, c, col:col + P], cn_lo[:, c, col:col + P],
                                     [w_hi[s][:, w]], [w_lo[s][:, w]], c == 0, c == CT - 1)
                mm.then_inc(s_chunk, 1)

                def scores(u):
                    if u == 0:
                        pe.wait_ge(s_qlo, hd + 1)
                        pe.wait_ge(s_klo, hd + 1)
                    if u >= 2:
                        pe.wait_ge(s_exp, u0 + u - 1 + START)
                    st = slice(TOK[u], TOK[u] + P)
                    qh, ql = q_hi[0:QK, st], q_lo[0:QK, st]
                    b = 2 * (u % 2)
                    if u < 4:
                        product([bank(b)], qh, ql, [two(k_hi[0:QK, :])], [two(k_lo[0:QK, :])], True, True)
                        mm = product([bank(b + 1, 0, PAST)], qh, ql, [k_hi[0:QK, T:KEYS]], [k_lo[0:QK, T:KEYS]],
                                     True, True)
                    else:
                        mm = product([bank(b, 0, P)], qh, ql, [k_hi[0:QK, PRO:PRO + P]], [k_lo[0:QK, PRO:PRO + P]],
                                     True, True)
                    mm.then_inc(s_s, 1)

                def turn(u):
                    pe.wait_ge(s_pn, u0 + u + 1)
                    pe.wait_ge(s_ptlo, u0 + u + START)
                    for n in range(6 if u < 4 else 1):
                        mm = nc.tensor.transpose(bank(5 + n // 4, (n % 4) * P, (n % 4 + 1) * P),
                                                 probs[u % 2][:, n * P:(n + 1) * P], ident[:])
                    mm.then_inc(s_pt, 1)

                def values(u):
                    pe.wait_ge(s_ptlo, u0 + u + 1 + START)
                    if u == 0:
                        pe.wait_ge(s_vlo, hd + 1)
                        pe.wait_ge(s_olo, hd * 2 + START)
                    out = bank(7, u * P, (u + 1) * P) if u < 4 else bank(6, 384, 512)
                    tiles = range(6) if u < 4 else [6]
                    for n, kt in enumerate(tiles):
                        mm = product([out[0:VD]], v_hi[:, kt, :], v_lo[:, kt, :],
                                     [pt_hi[:, u % 2, n * P:(n + 1) * P]], [pt_lo[:, u % 2, n * P:(n + 1) * P]],
                                     n == 0, n == len(tiles) - 1)
                    mm.then_inc(s_pv, 1)

                scores(0)
                scores(1)
                for u in range(UNITS):
                    turn(u)
                    if u + 2 < UNITS:
                        scores(u + 2)
                    if u >= 1:
                        values(u - 1)
                values(UNITS - 1)

            pe.wait_ge(s_fill, 5)
            pe.wait_ge(s_cond, 1)
            norm_sum(0)
            with pe.Fori(0, 2) as e:
                for k in range(KT):
                    mod_step(e, k)
                mod_turn(e)
            with pe.Fori(0, DEPTH) as l:
                base = l * LAYER_PAIRS
                e0 = l * MOD_BATCHES + 2
                ffn_step(l, 0, base, l * 3, (e0, e0 + 2))
                norm_sum(l * 3 + 1)
                mixer_step(l, base + FFN_PAIRS, l * 3 + 1)
                norm_sum(l * 3 + 2)
                ffn_step(l, 1, base + FFN_PAIRS + MIX_PAIRS, l * 3 + 2, (None, e0 + 4))
                norm_sum(l * 3 + 3)

        @block.scalar
        def _(act):
            for started in (s_modrow, s_silu, s_exp, s_sgf, s_sga):
                act.sem_inc(started, START)

            def mod_load(e, le, b, k):
                act.wait_ge(s_wmused, e * KT + k + 1)
                act.dma_start(wm[k % 2][:], i["w_mod"][le, b, k]).then_inc(s_wm[k % 2], 16)

            def mod_copy(e):
                act.wait_ge(s_wmused, (e + 1) * KT + CREDIT)
                act.wait_ge(s_modt, e + START)
                nc.scalar.activation(mod_row[:], bank(4, 0, MOD_COLS), ACT.Copy).then_inc(s_modrow, 1)

            def norm(nn, l, j):
                act.wait_ge(s_sum, nn + 1)
                nc.scalar.activation(std, pair(3), ACT.Sqrt, scale=1.0 / D, bias=eps[:, 0:1]).then_inc(s_std, 1)
                with act.Fori(0, KT // 2) as t:
                    for n, src in enumerate((ta, tb)):
                        k = t * 2 + n
                        act.wait_ge(s_t, nn * KT + k + 1)
                        for g, (v, hi) in groups(src, h_hi[:, bass.ds(k, 1), :][:, 0, :]):
                            ins = nc.scalar.activation(hi, v, ACT.Identity, bias=mod[:, g, bass.ds(k + 3 * j * KT, 1)])
                        ins.then_inc(s_hhi, 1)

            def ffn_step(l, f, base, mods):
                for half in range(2):
                    up = base + half * (FH + KT // 2)
                    g0 = (l * 2 + f) * 2 * FH + half * FH
                    with act.Fori(0, FH) as t:
                        act.wait_ge(s_chunk, used(up + t, 0))
                        act.wait_ge(s_prod, g0 + t + START)
                        nc.scalar.activation(silu, pair(0), ACT.Silu).then_inc(s_silu, 1)
                        act.wait_ge(s_prod, g0 + t + 1 + START)
                        nc.scalar.activation(a_hi[:, bass.ds(t, 1), :], prod, ACT.Copy).then_inc(s_ahi, 1)
                    if mods is not None and mods[half] is not None:
                        e, le, b = mods[half]
                        with act.Fori(0, 2) as t:
                            for k in range(KT):
                                mod_load(e + t, le, b + t, k)
                            mod_copy(e + t)

            def mixer_step(l, mixp):
                act.wait_ge(s_chunk, used(mixp + IN_P, 0))
                act.dma_start(past_c[:], i["past_ckv"][l]).then_inc(s_past, 16)
                act.dma_start(past_k[NOPE:QK, :], i["past_krope"][l]).then_inc(s_past, 16)

                def latent(t0, t1, nsum, width):
                    act.wait_ge(s_lsum, l * 2 + nsum + 1)
                    if nsum:
                        act.wait_ge(s_latn, l * (QT + CT) + QT)
                    nc.scalar.activation(lat_std, pair(2 + nsum), ACT.Sqrt, scale=1.0 / width,
                                         bias=eps[:, 0:1]).then_inc(s_lstd, 1)
                    for t in range(t0, t1):
                        act.wait_ge(s_latn, l * (QT + CT) + t + 1)
                        hi = qn_hi[:, t, :] if t < QT else cn_hi[:, t - QT, 0:T]
                        nc.scalar.activation(hi, lat[:, t, :], ACT.Copy).then_inc(s_nhi, 1)

                for t in range(8):
                    p, s = mixp + IN_P + t // 2, t % 2
                    act.wait_ge(s_chunk, used(p, s))
                    if t < QT + CT:
                        nc.scalar.activation(lat[:, t, :], pair(s), ACT.Copy).then_inc(s_lat, 1)
                    elif t == QT + CT:
                        nc.scalar.activation(kr32[NOPE:P], pair(s)[NOPE:P], ACT.Copy).then_inc(s_lat, 1)
                        act.wait_ge(s_lat, l * 8 + t + 1)
                        act.dma_start(o["krope"][l], kr32[NOPE:QK, PRO:PRO + PROMPT]).then_inc(s_out, 16)
                        act.wait_ge(s_past, (l + 1) * 32)
                        nc.scalar.activation(cn_hi[:, :, T:KEYS], past_c[:], ACT.Copy).then_inc(s_pasthi, 1)
                        nc.scalar.activation(k_hi[NOPE:QK, T:KEYS], past_k[NOPE:QK, :], ACT.Copy).then_inc(s_pasthi, 1)
                        act.wait_ge(s_kr, (l + 1) * 3)
                        nc.scalar.activation(k_hi[NOPE:QK, 0:T], kr_cos[NOPE:QK], ACT.Copy).then_inc(s_krhi, 1)
                    else:
                        nc.scalar.activation(f_hi[:, t - 6, :], pair(s), ACT.Copy).then_inc(s_lat, 1)
                for t in range(UNITS):
                    if t < 4:
                        act.wait_ge(s_chan, l * 4 + t + 1)
                    else:
                        act.wait_ge(s_chunk, used(mixp + DFT_P, 0))
                    nc.scalar.activation(uv_hi[:, t, :], bank(t % 4), ACT.Copy).then_inc(s_uvhi, 1)
                latent(0, QT, 0, Q_RANK)
                latent(QT, QT + CT, 1, KV_RANK)
                act.dma_start(o["ckv"][l], lat[:, QT:QT + CT, PRO:PRO + PROMPT]).then_inc(s_out, 16)
                act.wait_ge(s_chunk, used(mixp + DFT_P, 1))
                nc.scalar.activation(fr_hi[:, :, PRO:PRO + PROMPT],
                                     bank(1, 0, FT * P).rearrange("p (c n) -> p c n", c=FT),
                                     ACT.Copy).then_inc(s_frhi, 1)
                act.wait_ge(s_chunk, used(mixp + SEQ_P + 1, 1))
                for c in range(FT):
                    nc.scalar.activation(two(fr_hi[:, c, :]), bank(2 + c).rearrange("p (a n) -> p a n", a=2),
                                         ACT.Copy).then_inc(s_frhi, 1)
                with act.Fori(0, HEADS // 2) as t:
                    for s in range(2):
                        if s == 0:
                            act.wait_ge(s_out, (l + 1) * 32)
                            act.wait_ge(s_frlo, (l + 1) * 3)
                        attend(l * HEADS + t * 2 + s, mixp + HEAD_P + t, s, t)
                with act.Fori(0, KT) as m:
                    n0 = l * KT + m
                    act.wait_ge(s_gf, n0 + 1)
                    act.wait_ge(s_p1, n0 + START)
                    nc.scalar.activation(sgf, pair(0), ACT.Sigmoid).then_inc(s_sgf, 1)
                    act.wait_ge(s_ga, n0 + 1)
                    act.wait_ge(s_p2, n0 + START)
                    nc.scalar.activation(sga, pair(2), ACT.Sigmoid).then_inc(s_sga, 1)
                    act.wait_ge(s_m, n0 + 1)
                    nc.scalar.activation(m_hi[:, bass.ds(m, 1), :], p1, ACT.Copy).then_inc(s_mhi, 1)

            def attend(hd, p, s, t):
                u0 = hd * UNITS
                act.wait_ge(s_qmm, hd + 1)
                nc.scalar.activation(q32, pair(0), ACT.Copy).then_inc(s_q32, 1)
                act.wait_ge(s_kmm, hd + 1)
                nc.scalar.activation(k_hi[0:NOPE, :].rearrange("p (a n) -> p a n", a=2),
                                     ps[0:NOPE, 2 * 512:4 * 512].rearrange("p (a n) -> p a n", a=2)[:, :, 0:KEYS // 2],
                                     ACT.Copy).then_inc(s_khi, 1)
                act.wait_ge(s_rot, (hd + 1) * 3 + START)
                nc.scalar.activation(q_hi[0:QK, :], q32[0:QK], ACT.Copy).then_inc(s_qhi, 1)
                act.wait_ge(s_chunk, used(p, s))
                nc.scalar.activation(v_hi[:], bank(4, 0, 7 * VD), ACT.Copy).then_inc(s_vhi, 1)

                def exponent(u):
                    n = NK if u < 4 else P
                    act.wait_ge(s_nmx, u0 + u + 1)
                    act.wait_ge(s_pt, u0 + (u - 1 if u >= 2 else 0) + START)
                    nc.scalar.activation(probs[u % 2][:, 0:n], bank(2 * (u % 2))[:, 0:n] if n == P else
                                         ps[:, u % 2 * 1024:u % 2 * 1024 + n], ACT.Exp,
                                         bias=nmx[:, u:u + 1], scale=SCALE,
                                         accum_out=rsum[:, u:u + 1]).then_inc(s_exp, 1)

                def spread(u):
                    n = NK if u < 4 else P
                    act.wait_ge(s_pt, u0 + u + 1 + START)
                    act.wait_ge(s_pv, u0 + (u - 1 if u >= 2 else 0) + START)
                    nc.scalar.activation(pt_hi[:, u % 2, 0:n], ps[:, 5 * 512:5 * 512 + n], ACT.Copy).then_inc(s_pthi, 1)

                exponent(0)
                for u in range(UNITS):
                    if u + 1 < UNITS:
                        exponent(u + 1)
                    spread(u)
                rows = slice(s * VD, (s + 1) * VD)
                act.wait_ge(s_pv, u0 + 4 + START)
                nc.scalar.activation(two(ot_hi[rows, bass.ds(t, 1), :][:, 0, :]),
                                     bank(7)[0:VD].rearrange("p (a n) -> p a n", a=2), ACT.Copy).then_inc(s_ohi, 1)
                act.wait_ge(s_pv, u0 + 5 + START)
                nc.scalar.activation(pro(ot_hi[rows, bass.ds(t, 1), :][:, 0, :]), bank(6, 384, 512)[0:VD],
                                     ACT.Copy).then_inc(s_ohi, 1)

            act.wait_ge(s_const, 16 * 6)
            act.wait_ge(s_fill, 5)
            nc.scalar.activation(cond[:, :, 0:2], cond_in[:], ACT.Silu).then_inc(s_cond, 1)
            with act.Fori(0, 2) as e:
                for k in range(KT):
                    mod_load(e, 0, e, k)
                mod_copy(e)
            with act.Fori(0, DEPTH) as l:
                base = l * LAYER_PAIRS
                e0 = l * MOD_BATCHES + 2
                norm(l * 3, l, 0)
                ffn_step(l, 0, base, ((e0, l, 2), (e0 + 2, l, 4)))
                norm(l * 3 + 1, l, 1)
                mixer_step(l, base + FFN_PAIRS)
                norm(l * 3 + 2, l, 2)
                ffn_step(l, 1, base + FFN_PAIRS + MIX_PAIRS, (None, (e0 + 4, 1, 0)))
            act.wait_ge(s_sum, 3 * DEPTH + 1)
            nc.scalar.activation(std, pair(3), ACT.Sqrt, scale=1.0 / D, bias=eps[:, 0:1]).then_inc(s_std, 1)

        @block.vector
        def _(dve):
            dve.sem_inc(s_xupd, XUPD0)
            for started in (s_mod, s_prod, s_alo, s_hlo, s_rot, s_ptlo, s_olo, s_p1, s_p2, s_mlo):
                dve.sem_inc(started, START)
            tt, stt = nc.vector.tensor_tensor, nc.vector.scalar_tensor_tensor

            def xk(k):
                return x[:, bass.ds(k, 1), :][:, 0, :]

            def add_square(nn, k):
                dve.wait_ge(s_acc, nn * (KT + 1) + k + 1)
                tt(sq, xk(k), xk(k), ALU.mult).then_inc(s_sq, 1)
                dve.wait_ge(s_sq, nn * KT + k + 1)
                tt(acc, acc, sq, ALU.add).then_inc(s_acc, 1)

            def clear_acc(nn):
                dve.wait_ge(s_sum, nn)
                nc.vector.memset(acc, 0.0).then_inc(s_acc, 1)

            def mod_add(e, lb, b):
                dve.wait_ge(s_modt, e + 1 + START)
                cols = bank(5, 0, MOD_COLS).rearrange("p (b j r) -> p j b r", b=MOD_COLS // P, j=4)
                for g in range(2):
                    n = MB // P
                    ins = tt(mod[:, g, bass.ds(b * n, n)].rearrange("p (j b) -> p j b", j=4), cols[:, :, :, g],
                             bmod[:, bass.ds(lb, 1), bass.ds(b * n, n)][:, 0, :].rearrange("p (j b) -> p j b", j=4), ALU.add)
                ins.then_inc(s_mod, 1)

            def norm(nn, l, j, e_need):
                dve.wait_ge(s_mod, e_need + START)
                dve.wait_ge(s_hlo, nn * KT + START)
                for g in range(2):
                    ins = stt(out=scale_a[:, g, :], in0=mod[:, g, (3 * j + 1) * KT:(3 * j + 2) * KT], scalar=1.0,
                              in1=gains[:, bass.ds(l, 1), j, :][:, 0, :], op0=ALU.add, op1=ALU.mult)
                ins.then_inc(s_coef, 1)
                dve.wait_ge(s_std, nn + 1)
                for n in range(2):
                    ins = nc.vector.reciprocal(halves(rstd)[n], halves(std)[n])
                ins.then_inc(s_rstd, 1)
                with dve.Fori(0, KT // 2) as t:
                    dve.wait_ge(s_coef, nn + 1)
                    dve.wait_ge(s_rstd, nn + 1)
                    dve.wait_ge(s_hlo, nn * KT + t * 2 + START)
                    for n, dst in enumerate((ta, tb)):
                        k = t * 2 + n
                        for g, (d, v, r) in groups(dst, xk(k), rstd):
                            ins = stt(out=d, in0=v, scalar=scale_a[:, g, bass.ds(k, 1)], in1=r,
                                      op0=ALU.mult, op1=ALU.mult)
                        ins.then_inc(s_t, 1)
                    for n, src in enumerate((ta, tb)):
                        k = t * 2 + n
                        dve.wait_ge(s_t, nn * KT + k + 1)
                        dve.wait_ge(s_hhi, nn * KT + k + 1)
                        for g, (v, hi, lo) in groups(src, h_hi[:, bass.ds(k, 1), :][:, 0, :],
                                                     h_lo[:, bass.ds(k, 1), :][:, 0, :]):
                            ins = stt(out=lo, in0=v, scalar=mod[:, g, bass.ds(k + 3 * j * KT, 1)],
                                      in1=hi.bitcast(F32), op0=ALU.add, op1=ALU.subtract)
                        ins.then_inc(s_hlo, 1)

            def update(k, src, gate, col):
                for g, (v, y) in groups(xk(k), src):
                    ins = stt(out=v, in0=y, scalar=gate[:, g, bass.ds(k + col, 1)], in1=v, op0=ALU.mult, op1=ALU.add)
                ins.then_inc(s_xupd, 1)

            def ffn_step(l, f, base, nn, mods):
                j = 2 * f
                for half in range(2):
                    up = base + half * (FH + KT // 2)
                    g0 = (l * 2 + f) * 2 * FH + half * FH
                    with dve.Fori(0, FH) as t:
                        dve.wait_ge(s_chunk, used(up + t, 1))
                        dve.wait_ge(s_silu, g0 + t + 1 + START)
                        dve.wait_ge(s_alo, g0 + t + START)
                        tt(prod, pair(1), silu, ALU.mult).then_inc(s_prod, 1)
                        dve.wait_ge(s_prod, g0 + t + 1 + START)
                        dve.wait_ge(s_ahi, g0 + t + 1)
                        tt(a_lo[:, bass.ds(t, 1), :][:, 0, :], prod, a_hi[:, bass.ds(t, 1), :][:, 0, :].bitcast(F32),
                           ALU.subtract).then_inc(s_alo, 1)
                    if half == 0:
                        dve.wait_ge(s_xupd, XUPD0 + l * UPD + f * 3 * KT)
                        nc.vector.tensor_scalar(half_g[:], mod[:, :, (3 * j + 2) * KT:(3 * j + 3) * KT], 0.5, None,
                                                ALU.mult).then_inc(s_half, 1)
                    else:
                        clear_acc(nn + 1)
                    upd0 = XUPD0 + l * UPD + f * 3 * KT + half * KT
                    with dve.Fori(0, 2) as t:
                        for m in range(4):
                            k = t * 4 + m
                            dve.wait_ge(s_chunk, used(up + FH + t * 2 + m // 2, m % 2))
                            dve.wait_ge(s_half, l * 2 + f + 1)
                            update(k, pair(m % 2), half_g, 0)
                            if half == 1:
                                dve.wait_ge(s_xupd, upd0 + k + 1)
                                add_square(nn + 1, k)
                        if mods is not None and mods[half] is not None:
                            e, lb, b = mods[half]
                            mod_add(e + t, lb, b + t)

            def mixer_step(l, mixp, nn):
                lo_of = lambda out, src, hi: tt(out, src, hi.bitcast(F32), ALU.subtract)
                n5 = l * (QT + CT)
                def square(t):
                    dve.wait_ge(s_lat, l * 8 + t + 1)
                    if t == QT:
                        dve.wait_ge(s_lsum, l * 2 + 1)
                    if t in (0, QT):
                        tt(lat_acc, lat[:, t, :], lat[:, t, :], ALU.mult).then_inc(s_lacc, 1)
                    else:
                        dve.wait_ge(s_lacc, n5 + t)
                        tt(lat_sq, lat[:, t, :], lat[:, t, :], ALU.mult).then_inc(s_lsq, 1)
                        dve.wait_ge(s_lsq, l * (QT + CT - 2) + (t if t < QT else t - 1))
                        tt(lat_acc, lat_acc, lat_sq, ALU.add).then_inc(s_lacc, 1)

                def latent(t0, t1, nsum):
                    dve.wait_ge(s_lstd, l * 2 + nsum + 1)
                    for n in range(2):
                        ins = nc.vector.reciprocal(halves(lat_std)[n], halves(lat_std)[n])
                    ins.then_inc(s_lrstd, 1)
                    dve.wait_ge(s_lrstd, l * 2 + nsum + 1)
                    for t in range(t0, t1):
                        stt(out=lat[:, t, :], in0=lat[:, t, :], scalar=lat_gain[:, bass.ds(l, 1), t],
                            in1=lat_std, op0=ALU.mult, op1=ALU.mult).then_inc(s_latn, 1)
                    for t in range(t0, t1):
                        dve.wait_ge(s_latn, n5 + t + 1)
                        dve.wait_ge(s_nhi, n5 + t + 1)
                        hi, lo = (qn_hi[:, t, :], qn_lo[:, t, :]) if t < QT else \
                            (cn_hi[:, t - QT, 0:T], cn_lo[:, t - QT, 0:T])
                        lo_of(lo, lat[:, t, :], hi).then_inc(s_nlo, 1)

                for t in range(QT):
                    square(t)
                dve.wait_ge(s_lat, l * 8 + 6)
                tt(kr_sin[NOPE:QK], kr32[QK:P], rope_tab[QK:P, :], ALU.mult).then_inc(s_kr, 1)
                tt(kr_cos[NOPE:QK], kr32[NOPE:QK], rope_tab[NOPE:QK, :], ALU.mult).then_inc(s_kr, 1)
                dve.wait_ge(s_kr, l * 3 + 2)
                tt(kr_cos[NOPE:QK], kr_cos[NOPE:QK], kr_sin[NOPE:QK], ALU.add).then_inc(s_kr, 1)
                dve.wait_ge(s_pasthi, (l + 1) * 2)
                lo_of(cn_lo[:, :, T:KEYS], past_c[:], cn_hi[:, :, T:KEYS]).then_inc(s_pastlo, 1)
                lo_of(k_lo[NOPE:QK, T:KEYS], past_k[NOPE:QK, :], k_hi[NOPE:QK, T:KEYS]).then_inc(s_pastlo, 1)
                dve.wait_ge(s_kr, (l + 1) * 3)
                dve.wait_ge(s_krhi, l + 1)
                lo_of(k_lo[NOPE:QK, 0:T], kr_cos[NOPE:QK], k_hi[NOPE:QK, 0:T]).then_inc(s_krlo, 1)
                for c in range(FT):
                    dve.wait_ge(s_lat, l * 8 + 7 + c)
                    lo_of(f_lo[:, c, :], pair(c), f_hi[:, c, :]).then_inc(s_flo, 1)
                for t in range(QT, QT + CT):
                    square(t)
                for t in range(UNITS):
                    dve.wait_ge(s_uvhi, l * UNITS + t + 1)
                    lo_of(uv_lo[:, t, :], bank(t % 4), uv_hi[:, t, :]).then_inc(s_uvlo, 1)
                latent(0, QT, 0)
                latent(QT, QT + CT, 1)
                dve.wait_ge(s_frhi, l * 3 + 1)
                lo_of(fr_lo[:, :, PRO:PRO + PROMPT], bank(1, 0, FT * P).rearrange("p (c n) -> p c n", c=FT),
                      fr_hi[:, :, PRO:PRO + PROMPT]).then_inc(s_frlo, 1)
                for c in range(FT):
                    dve.wait_ge(s_frhi, l * 3 + 2 + c)
                    lo_of(two(fr_lo[:, c, :]), bank(2 + c).rearrange("p (a n) -> p a n", a=2),
                          two(fr_hi[:, c, :])).then_inc(s_frlo, 1)
                with dve.Fori(0, HEADS // 2) as t:
                    for s in range(2):
                        if s == 0:
                            dve.wait_ge(s_out, (l + 1) * 32)
                        attend(l * HEADS + t * 2 + s, s, t, lo_of)
                with dve.Fori(0, KT) as m:
                    n0 = l * KT + m
                    dve.wait_ge(s_op, n0 + 1)
                    dve.wait_ge(s_sga, n0 + 1 + START)
                    dve.wait_ge(s_mlo, n0 + START)
                    tt(p2, pair(1), sga, ALU.mult).then_inc(s_p2, 1)
                    dve.wait_ge(s_chunk, used(mixp + MERGE_P + m, 1))
                    dve.wait_ge(s_sgf, n0 + 1 + START)
                    tt(p1, pair(3), sgf, ALU.mult).then_inc(s_p1, 1)
                    dve.wait_ge(s_p1, n0 + 1 + START)
                    dve.wait_ge(s_p2, n0 + 1 + START)
                    tt(p1, p1, p2, ALU.add).then_inc(s_m, 1)
                    dve.wait_ge(s_m, n0 + 1)
                    dve.wait_ge(s_mhi, n0 + 1)
                    lo_of(m_lo[:, bass.ds(m, 1), :][:, 0, :], p1, m_hi[:, bass.ds(m, 1), :][:, 0, :]).then_inc(s_mlo, 1)
                clear_acc(nn + 1)
                with dve.Fori(0, KT // 2) as t:
                    for s in range(2):
                        k = t * 2 + s
                        dve.wait_ge(s_chunk, used(mixp + OUT_P + t, s))
                        update(k, pair(s), mod, 5 * KT)
                        dve.wait_ge(s_xupd, XUPD0 + l * UPD + 2 * KT + k + 1)
                        add_square(nn + 1, k)

            def attend(hd, s, t, lo_of):
                u0 = hd * UNITS
                dve.wait_ge(s_q32, hd + 1)
                dve.wait_ge(s_rot, hd * 3 + START)
                tt(rot[NOPE:QK], q32[QK:P], rope_tab[QK:P, :], ALU.mult).then_inc(s_rot, 1)
                tt(q32[NOPE:QK], q32[NOPE:QK], rope_tab[NOPE:QK, :], ALU.mult).then_inc(s_rot, 1)
                dve.wait_ge(s_rot, hd * 3 + 2 + START)
                tt(q32[NOPE:QK], q32[NOPE:QK], rot[NOPE:QK], ALU.add).then_inc(s_rot, 1)
                dve.wait_ge(s_khi, hd + 1)
                lo_of(k_lo[0:NOPE, :].rearrange("p (a n) -> p a n", a=2),
                      ps[0:NOPE, 2 * 512:4 * 512].rearrange("p (a n) -> p a n", a=2)[:, :, 0:KEYS // 2],
                      k_hi[0:NOPE, :].rearrange("p (a n) -> p a n", a=2)).then_inc(s_klo, 1)
                dve.wait_ge(s_rot, (hd + 1) * 3 + START)
                dve.wait_ge(s_qhi, hd + 1)
                lo_of(q_lo[0:QK, :], q32[0:QK], q_hi[0:QK, :]).then_inc(s_qlo, 1)
                dve.wait_ge(s_vhi, hd + 1)
                lo_of(v_lo[:].rearrange("p a n -> p (a n)"), bank(4, 0, 7 * VD),
                      v_hi[:].rearrange("p a n -> p (a n)")).then_inc(s_vlo, 1)

                def maxima(u):
                    n = NK if u < 4 else P
                    dve.wait_ge(s_s, u0 + u + 1)
                    nc.vector.tensor_reduce(mx[:, u:u + 1], ps[:, u % 2 * 1024:u % 2 * 1024 + n], AX.X,
                                            ALU.max).then_inc(s_mx, 1)
                    dve.wait_ge(s_mx, u0 + u + 1)
                    nc.vector.tensor_scalar(nmx[:, u:u + 1], mx[:, u:u + 1], -SCALE, None, ALU.mult).then_inc(s_nmx, 1)

                def normal(u):
                    n = NK if u < 4 else P
                    dve.wait_ge(s_exp, u0 + u + 1 + START)
                    nc.vector.reciprocal(rinv[:, u:u + 1], rsum[:, u:u + 1]).then_inc(s_rinv, 1)
                    dve.wait_ge(s_rinv, u0 + u + 1)
                    pr = probs[u % 2][:, 0:n]
                    nc.vector.tensor_scalar(pr, pr, rinv[:, u:u + 1], None, ALU.mult).then_inc(s_pn, 1)

                def spread(u):
                    n = NK if u < 4 else P
                    dve.wait_ge(s_pthi, u0 + u + 1)
                    lo_of(pt_lo[:, u % 2, 0:n], ps[:, 5 * 512:5 * 512 + n], pt_hi[:, u % 2, 0:n]).then_inc(s_ptlo, 1)

                maxima(0)
                for u in range(UNITS):
                    if u + 1 < UNITS:
                        maxima(u + 1)
                    normal(u)
                    spread(u)
                rows = slice(s * VD, (s + 1) * VD)
                oh, ol = ot_hi[rows, bass.ds(t, 1), :][:, 0, :], ot_lo[rows, bass.ds(t, 1), :][:, 0, :]
                dve.wait_ge(s_ohi, hd * 2 + 1)
                lo_of(two(ol), bank(7)[0:VD].rearrange("p (a n) -> p a n", a=2), two(oh)).then_inc(s_olo, 1)
                dve.wait_ge(s_ohi, hd * 2 + 2)
                lo_of(pro(ol), bank(6, 384, 512)[0:VD], pro(oh)).then_inc(s_olo, 1)

            dve.wait_ge(s_x, 16)
            dve.wait_ge(s_const, 16 * 6)
            nc.vector.memset(acc, 0.0).then_inc(s_acc, 1)
            with dve.Fori(0, KT) as k:
                add_square(0, k)
            with dve.Fori(0, 2) as e:
                mod_add(e, 0, e)
            with dve.Fori(0, DEPTH) as l:
                base = l * LAYER_PAIRS
                e0 = l * MOD_BATCHES + 2
                norm(l * 3, l, 0, e0)
                ffn_step(l, 0, base, l * 3, ((e0, l, 2), (e0 + 2, l, 4)))
                norm(l * 3 + 1, l, 1, e0 + 4)
                mixer_step(l, base + FFN_PAIRS, l * 3 + 1)
                norm(l * 3 + 2, l, 2, e0 + 4)
                ffn_step(l, 1, base + FFN_PAIRS + MIX_PAIRS, l * 3 + 2, (None, (e0 + 4, 1, 0)))
            dve.wait_ge(s_std, 3 * DEPTH + 1)
            dve.wait_ge(s_hlo, 3 * DEPTH * KT + START)
            for n in range(2):
                ins = nc.vector.reciprocal(halves(rstd)[n], halves(std)[n])
            ins.then_inc(s_rstd, 1)
            dve.wait_ge(s_rstd, 3 * DEPTH + 1)
            for k in range(KT):
                stt(out=x[:, k, :], in0=x[:, k, :], scalar=fin_gain[:, k:k + 1], in1=rstd,
                    op0=ALU.mult, op1=ALU.mult).then_inc(s_y, 1)


def _tables():
    n = np.arange(SAMPLE)
    axis = ROPE // 2
    inv = 10000.0 ** (-np.arange(0, axis, 2, dtype=np.float32) / axis)
    ar = (n // GRID_W)[:, None].astype(np.float32) * inv.astype(np.float32)
    ac = (n % GRID_W)[:, None].astype(np.float32) * inv.astype(np.float32)
    cos = np.concatenate([np.cos(ar), np.cos(ar), np.cos(ac), np.cos(ac)], 1).T
    sin = np.concatenate([-np.sin(ar), np.sin(ar), -np.sin(ac), np.sin(ac)], 1).T
    rope = np.concatenate([np.ones((2 * ROPE, PROMPT)), np.concatenate([cos, sin], 0)], 1)
    rope[ROPE:, :PROMPT] = 0.0

    def dft(m, norm):
        a = 2 * np.pi * (np.outer(np.arange(m), np.arange(m)) % m) / m
        return np.cos(a) / norm, np.sin(a) / norm

    c, s = dft(FD, 8.0)
    per = P // FD
    chan = np.concatenate([np.kron(np.eye(per), c), -np.kron(np.eye(per), s)], 1)
    prompt = np.concatenate(dft(PROMPT, PROMPT ** 0.5), 1)
    sample = np.concatenate(dft(SAMPLE, SAMPLE ** 0.5), 1).reshape(SAMPLE // P, P, 2 * SAMPLE)
    return [np.ascontiguousarray(a, dtype=np.float32) for a in (rope, chan, prompt, sample)]


def _cols(sample, prompt):
    return np.concatenate([sample[..., :S2], prompt, sample[..., S2:]], -1)


def _tiles(w, width=P):
    *lead, k, n = w.shape
    w = w.reshape(*lead, k // P, P, n // width, width)
    w = np.moveaxis(w, -2, -4)
    w = np.swapaxes(w, -3, -2)
    return w.reshape(*w.shape[:-2], -1)


def _kernel_inputs(a):
    a = {k: np.asarray(v) for k, v in a.items()}
    L = DEPTH
    out = {}
    xs = _cols(a["x_sample"][0].T, a["x_prompt"][0].T)
    out["x"] = xs.reshape(KT, P, T).transpose(1, 0, 2)
    out["cond"] = np.stack([a["c"][0], a["c_ctx"]], -1).reshape(KT, P, 2).transpose(1, 0, 2)
    out["b_mod"] = a["b_mod"].reshape(L, N_MOD * KT, P).transpose(2, 0, 1)
    out["gains"] = np.stack([a["norm_ffn1"], a["norm_mix"], a["norm_ffn2"]], 1).reshape(L, 3, KT, P).transpose(3, 0, 1, 2)
    out["lat_gains"] = np.concatenate([a["q_norm"], a["kv_norm"]], 1).reshape(L, QT + CT, P).transpose(2, 0, 1)
    out["fin_gain"] = a["final_norm"].reshape(KT, P).T
    out["w_mod"] = a["w_mod"].reshape(L, KT, P, MOD_BATCHES, MB).transpose(0, 3, 1, 2, 4)
    gate = np.stack([_tiles(a["w_ffn1_gate"]), _tiles(a["w_ffn2_gate"])], 1)
    up = np.stack([_tiles(a["w_ffn1_up"]), _tiles(a["w_ffn2_up"])], 1)
    out["w_up"] = np.stack([gate, up], 3)
    down = np.stack([a["w_ffn1_down"], a["w_ffn2_down"]], 1).reshape(L, 2, 2, D_FF // 2, D)
    out["w_down"] = _tiles(down)
    w_in = a["w_in"]
    cut = np.cumsum([0, D_FOUR, Q_RANK, KV_RANK, ROPE, D, D])
    swap = np.concatenate([np.r_[8:16, 0:8], 16 + np.r_[8:16, 0:8]])
    rope_cols = w_in[..., cut[3]:cut[4]]
    parts = [w_in[..., cut[1]:cut[3]], w_in[..., cut[3] - NOPE:cut[3]], rope_cols, rope_cols[..., swap],
             w_in[..., 0:D_FOUR]]
    out["w_in"] = _tiles(np.concatenate(parts, -1))
    uq = a["w_uq"].reshape(L, Q_RANK, HEADS, QK)
    uq = np.concatenate([uq, uq[..., NOPE:][..., swap]], -1).reshape(L, Q_RANK, HEADS * P)
    ukv = a["w_ukv"].reshape(L, KV_RANK, HEADS, NOPE + VD)
    uk = ukv[..., :NOPE].reshape(L, KV_RANK, HEADS * NOPE)
    uv = ukv[..., NOPE:].reshape(L, KV_RANK, HEADS * VD)
    out["w_head"] = np.concatenate([_tiles(uq), _tiles(uk, NOPE), _tiles(uv, VD)], -1)
    gf, ga = _tiles(w_in[..., cut[4]:cut[5]]), _tiles(w_in[..., cut[5]:cut[6]])
    ap, fo = _tiles(a["w_attn_proj"]), _tiles(a["w_four"])
    out["w_merge"] = np.stack([np.concatenate([gf, ap[..., :3 * P]], -1),
                               np.concatenate([ga, ap[..., 3 * P:], fo], -1)], 2)
    out["w_out"] = _tiles(a["w_out"])
    out["past_ckv"] = a["cache_ckv"][0].transpose(0, 2, 1).reshape(L, CT, P, PAST).transpose(0, 2, 1, 3)
    out["past_krope"] = a["cache_krope"][0].transpose(0, 2, 1)
    rope, chan, prompt, sample = _tables()
    out["rope"] = _cols(rope[:, PROMPT:], rope[:, :PROMPT])
    out["dft_chan"], out["dft_prompt"], out["dft_sample"] = chan, prompt, sample
    return {k: np.ascontiguousarray(v) for k, v in out.items()}


def kernel(**inputs):
    import concourse.bacc as _bacc
    from concourse.bass_utils import run_bass_kernel_spmd as _run

    nc = _bacc.Bacc("TRN2", target_bir_lowering=False, num_devices=1)
    arrays, ins, outs = {}, {}, {}
    for name, a in _kernel_inputs(inputs).items():
        arrays[f"in_{name}"] = a
        ins[name] = nc.dram_tensor(f"in_{name}", a.shape, mybir.dt.from_np(a.dtype), kind="ExternalInput").ap()
    shapes = {"y": (P, KT, T), "ckv": (DEPTH, P, CT, PROMPT), "krope": (DEPTH, ROPE, PROMPT)}
    for name, shape in shapes.items():
        outs[name] = nc.dram_tensor(f"out_{name}", shape, F32, kind="ExternalOutput").ap()
    build(nc, ins, outs)
    r = _run(nc, [arrays], core_ids=[0]).results[0]
    y = r["out_y"].transpose(1, 0, 2).reshape(D, T)
    y_sample = np.concatenate([y[:, :S2], y[:, STEP:]], 1).T[None]
    y_prompt = y[:, PRO:PRO + PROMPT].T[None]
    ckv = r["out_ckv"].transpose(0, 3, 2, 1).reshape(1, DEPTH, PROMPT, KV_RANK)
    krope = r["out_krope"].transpose(0, 2, 1)[None]
    return tuple(np.ascontiguousarray(v) for v in (y_prompt, y_sample, ckv, krope))
```

```python
import numpy as np
import concourse.bass as bass
from concourse import mybir
from concourse.alu_op_type import AluOpType as ALU
from contextlib import ExitStack

F32 = mybir.dt.float32
F32R = mybir.dt.float32r
ACT = mybir.ActivationFunctionType
AX = mybir.AxisListType

P = 128
DEPTH = 2
D = 1024
KT = D // P
D_FF = 2816
FH = D_FF // P // 2
SAMPLE, PROMPT, PAST = 512, 128, 256
T = SAMPLE + PROMPT
HALF = T // 2
TB = T + 2
S2 = SAMPLE // 2
PRO = S2
STEP = S2 + PROMPT
TOK = [0, P, STEP, STEP + P, PRO]
KEYS = T + PAST
GRID_W = 64
HEADS, NOPE, ROPE, VD = 8, 64, 32, 64
QK = NOPE + ROPE
Q_RANK, KV_RANK = 384, 256
QT, CT = Q_RANK // P, KV_RANK // P
D_FOUR, FD = 256, 64
FT = D_FOUR // P
OT = HEADS * VD // P
EPS = 1e-6
SCALE = float(QK) ** -0.5
N_MOD = 9
MOD_BATCHES, MOD_COLS = 6, 384
MB = 4 * MOD_COLS

UP_W = KT * P
DOWN_W = FH * P
IN_W = KT * P
CHAN_W = 2 * P
PDFT_W = 2 * P
SDFT_W = 2 * SAMPLE
HEAD_W = QT * P + CT * (NOPE + VD)
MERGE_W = (2 * KT + OT + FT) * P // 2
OUT_W = KT * P
SLOT = DOWN_W

FFN_PAIRS = 2 * (FH + KT // 2)
IN_P, DFT_P, SEQ_P, HEAD_P, MERGE_P, OUT_P = 0, 4, 5, 7, 11, 19
MIX_PAIRS = OUT_P + KT // 2
LAYER_PAIRS = 2 * FFN_PAIRS + MIX_PAIRS
CREDIT = 2
UPD = 5 * KT
START = 1
XUPD0 = KT
UNITS = 5


def two(v):
    return bass.AP(v.tensor, v.offset, [v.ap[0], (STEP, 2), (1, S2)])


def pro(v):
    return v[:, PRO:PRO + PROMPT]


def groups(*views):
    return [(0, [two(v) for v in views]), (1, [pro(v) for v in views])]


def build(nc, i, o):
    ctx = ExitStack()
    with ctx:
        def sb(name, shape, dt=F32, where=ctx):
            return where.enter_context(nc.sbuf_tensor(name, shape, dt))

        def sem(name):
            return ctx.enter_context(nc.semaphore(name))

        x = sb("x", [P, KT, T])
        h_hi, h_lo = sb("h_hi", [P, KT, TB], F32R), sb("h_lo", [P, KT, TB], F32R)
        raw = [sb(f"raw{s}", [P, SLOT]) for s in range(2)]
        w_hi = [sb(f"w_hi{s}", [P, SLOT], F32R) for s in range(2)]
        w_lo = [sb(f"w_lo{s}", [P, SLOT], F32R) for s in range(2)]
        tmp = sb("tmp", [P, 6 * T])
        sq, std, ta, tb, lat_std, acc = [tmp[:, n * T:(n + 1) * T] for n in range(6)]
        rstd = sb("rstd", [P, T])[:]
        rope_tab = sb("rope_tab", [P, T])
        ones = sb("ones", [P, P])
        ident = sb("ident", [P, P])
        cond = sb("cond", [P, KT, 32])
        cond_in = sb("cond_in", [P, KT, 2])
        bmod = sb("bmod", [P, DEPTH, N_MOD * KT])
        gains = sb("gains", [P, DEPTH * 3 + 1, KT])
        lat_gain = sb("lat_gain", [P, DEPTH, QT + CT])
        mod = sb("mod", [P, 2, N_MOD * KT])
        scale_a = sb("scale_a", [P, 2, KT])
        half_g = sb("half_g", [P, 2, KT])
        mod_row = sb("mod_row", [P, MOD_COLS])
        eps = sb("eps", [P, 1])
        bias_a, bias_b = sb("bias_a", [P, 2]), sb("bias_b", [P, 2])
        nmx, rsum, rinv = [sb(n, [P, UNITS]) for n in ("nmx", "rsum", "rinv")]

        with ExitStack() as ffn:
            a_hi, a_lo = sb("a_hi", [P, FH, T], F32R, ffn), sb("a_lo", [P, FH, T], F32R, ffn)
            wm = [sb(f"wm{s}", [P, MB], F32, ffn) for s in range(2)]
        with ExitStack() as start:
            wm_start = [sb(f"wm_start{n}", [P, MB], F32, start) for n in range(2 * KT - 2)]
            wm_start += [wm_start[0], tmp[:, 2 * T:2 * T + MB]]
        with ExitStack() as mix:
            fr_hi, fr_lo = sb("fr_hi", [P, FT, T], F32R, mix), sb("fr_lo", [P, FT, T], F32R, mix)
            with ExitStack() as four:
                uv_hi = sb("uv_hi", [P, UNITS, 2 * FT * P], F32R, four)
                uv_lo = sb("uv_lo", [P, UNITS, 2 * FT * P], F32R, four)
            ot_hi, ot_lo = sb("ot_hi", [P, OT, T], F32R, mix), sb("ot_lo", [P, OT, T], F32R, mix)
            with ExitStack() as att:
                qn_hi, qn_lo = sb("qn_hi", [P, QT, T], F32R, att), sb("qn_lo", [P, QT, T], F32R, att)
                cn_hi, cn_lo = sb("cn_hi", [P, CT, KEYS], F32R, att), sb("cn_lo", [P, CT, KEYS], F32R, att)
                k_hi, k_lo = sb("k_hi", [P, KEYS], F32R, att), sb("k_lo", [P, KEYS], F32R, att)
                with ExitStack() as pre:
                    lat = sb("lat", [P, QT + CT, T], F32, pre)
                    f_hi, f_lo = sb("f_hi", [P, FT, T], F32R, pre), sb("f_lo", [P, FT, T], F32R, pre)
                with ExitStack() as head:
                    q_hi, q_lo = sb("q_hi", [P, T], F32R, head), sb("q_lo", [P, T], F32R, head)
                    v_hi = sb("v_hi", [P, KEYS // P, VD], F32R, head)
                    v_lo = sb("v_lo", [P, KEYS // P, VD], F32R, head)
                    pt_hi = sb("pt_hi", [P, 2, SAMPLE + PAST], F32R, head)
                    pt_lo = sb("pt_lo", [P, 2, SAMPLE + PAST], F32R, head)
            with ExitStack() as mer:
                m_hi, m_lo = sb("m_hi", [P, KT, T], F32R, mer), sb("m_lo", [P, KT, T], F32R, mer)
        NK = SAMPLE + PAST
        probs = [tmp[:, u * NK:(u + 1) * NK] for u in range(2)]
        q32 = tmp[:, 2 * NK:2 * NK + T]
        rot = tmp[:, 2 * NK + T:2 * NK + 2 * T]
        kr32, kr_sin, kr_cos = sq, std, ta
        lat_sq, lat_acc = tb, acc
        fourier_in = [std, ta]
        past_c = lat_std[:, 0:CT * PAST].rearrange("p (c n) -> p c n", c=CT)
        past_k = mod_row[:, 0:PAST]
        silu, prod = ta, tb
        sgf, sga, p1, p2 = sq, std, ta, tb

        ps = ctx.enter_context(nc.psum_tensor("ps", [P, 8 * 512], F32))

        def bank(b, n0=0, n1=512):
            return ps[:, b * 512 + n0:b * 512 + n1]

        def pair(j):
            return ps[:, j * 1024 + 512 - HALF:j * 1024 + 512 + HALF]

        def pairb(j):
            return ps[:, j * 1024 + 512 - HALF:j * 1024 + 512 - HALF + TB]

        def shifts(j, p0=0):
            return ps[p0:P, j * 1024 + 512 + HALF:j * 1024 + 512 - HALF + TB]

        def halves(v):
            return [v[:, 0:HALF], v[:, HALF:]]

        s_raw = [sem(f"raw_loaded{s}") for s in range(2)]
        s_whi = sem("weight_hi_ready")
        s_split = sem("chunk_split")
        s_chunk = sem("chunk_used")
        s_wm = [sem(f"mod_weights_loaded{s}") for s in range(2)]
        s_start = [sem(f"first_mod_weights_loaded{n}") for n in range(2 * KT)]
        s_wmused = sem("mod_weights_used")
        s_modmm, s_modrow, s_modt, s_mod = sem("mod_rows_summed"), sem("mod_rows_copied"), \
            sem("mod_transposed"), sem("mod_ready")
        s_condin = sem("conditioning_loaded")
        s_const, s_fill, s_x = sem("constants_loaded"), sem("constants_filled"), sem("x_loaded")
        s_cond = sem("cond_ready")
        s_xupd, s_sq, s_acc = sem("x_updated"), sem("square_ready"), sem("squares_added")
        s_sum, s_std, s_rstd = sem("squares_summed"), sem("std_ready"), sem("rstd_ready")
        s_coef, s_half = sem("coefficients_ready"), sem("half_gates_ready")
        s_hhi, s_hlo, s_bhi, s_blo = sem("h_hi_ready"), sem("h_ready"), sem("shift_hi_ready"), sem("shift_ready")
        s_gsc, s_usc, s_latsc = sem("gate_scaled"), sem("up_scaled"), sem("latent_scaled")
        s_gfsc, s_gasc = sem("gate_f_scaled"), sem("gate_a_scaled")
        s_silu, s_prod, s_ahi, s_alo = sem("silu_ready"), sem("product_ready"), sem("a_hi_ready"), sem("a_ready")
        s_lat, s_flo = sem("latent_copied"), sem("f_ready")
        s_lsq, s_lacc, s_lsum, s_lstd = sem("latent_square"), sem("latent_squares_added"), \
            sem("latent_summed"), sem("latent_std")
        s_lrstd, s_latn, s_nhi, s_nlo = sem("latent_rstd"), sem("latent_normed"), \
            sem("latent_hi_ready"), sem("latent_ready")
        s_past = sem("past_loaded")
        s_kr, s_krhi, s_krlo = sem("key_rope_step"), sem("key_rope_hi"), sem("key_rope_ready")
        s_pasthi, s_pastlo = sem("past_hi"), sem("past_ready")
        s_chan, s_uvhi, s_uvlo = sem("channel_dft"), sem("uv_hi"), sem("uv_ready")
        s_frhi, s_frlo = sem("fourier_hi"), sem("fourier_ready")
        s_qmm, s_kmm = sem("q_product"), sem("k_product")
        s_q32, s_rot, s_qhi, s_qlo = sem("q_copied"), sem("q_rotate_step"), sem("q_hi_ready"), sem("q_ready")
        s_khi, s_klo, s_vhi, s_vlo = sem("k_hi_ready"), sem("k_ready"), sem("v_hi_ready"), sem("v_ready")
        s_s, s_nmx, s_exp = sem("scores_ready"), sem("neg_max_ready"), sem("exp_ready")
        s_rinv, s_pn, s_pt, s_pthi, s_ptlo = sem("row_inverse"), sem("probs_ready"), \
            sem("probs_transposed"), sem("probs_t_hi"), sem("probs_t_ready")
        s_pv, s_ohi, s_olo = sem("values_mixed"), sem("o_hi_ready"), sem("o_ready")
        s_gf, s_op, s_ga = sem("gate_f_product"), sem("attn_out_product"), sem("gate_a_product")
        s_sgf, s_sga, s_p1, s_p2, s_m = sem("sigmoid_f"), sem("sigmoid_a"), sem("gated_fourier"), \
            sem("gated_attention"), sem("merged")
        s_mhi, s_mlo = sem("merged_hi"), sem("merged_ready")
        s_out, s_y = sem("outputs_written"), sem("y_ready")

        block = ctx.enter_context(nc.Block())

        def used(p, s):
            return (p * 2 + s) + 1 + CREDIT

        @block.sync
        def _(sp):
            sp.dma_start(cond_in[:], i["cond"]).then_inc(s_condin, 16)
            for dst, src in ((bmod, i["b_mod"]), (gains, i["gains"]),
                             (lat_gain, i["lat_gains"])):
                sp.dma_start(dst[:], src).then_inc(s_const, 16)
            sp.dma_start(rope_tab[NOPE:P, :], i["rope"]).then_inc(s_const, 16)
            sp.dma_start(x[:], i["x"]).then_inc(s_x, 16)

            def load(p, s, width, src):
                sp.wait_ge(s_split, p * 2 + s + 1)
                sp.dma_start(raw[s][:, 0:width], src).then_inc(s_raw[s], 16)

            def ffn_chunks(l, f, base):
                for half in range(2):
                    up = base + half * (FH + KT // 2)
                    with sp.Fori(0, FH) as t:
                        for s in range(2):
                            load(up + t, s, UP_W, i["w_up"][l, f, t + half * FH, s])
                    with sp.Fori(0, KT // 2) as t:
                        for s in range(2):
                            load(up + FH + t, s, DOWN_W, i["w_down"][l, f, half, t * 2 + s])

            with sp.Fori(0, DEPTH) as l:
                base = l * LAYER_PAIRS
                ffn_chunks(l, 0, base)
                mixp = base + FFN_PAIRS
                with sp.Fori(0, 4) as t:
                    for s in range(2):
                        load(mixp + IN_P + t, s, IN_W, i["w_in"][l, t * 2 + s])
                load(mixp + DFT_P, 0, CHAN_W, i["dft_chan"])
                load(mixp + DFT_P, 1, PDFT_W, i["dft_prompt"])
                with sp.Fori(0, 2) as t:
                    for s in range(2):
                        load(mixp + SEQ_P + t, s, SDFT_W, i["dft_sample"][t * 2 + s])
                with sp.Fori(0, HEADS // 2) as t:
                    for s in range(2):
                        load(mixp + HEAD_P + t, s, HEAD_W, i["w_head"][l, t * 2 + s])
                with sp.Fori(0, KT) as t:
                    for s in range(2):
                        load(mixp + MERGE_P + t, s, MERGE_W, i["w_merge"][l, t, s])
                with sp.Fori(0, KT // 2) as t:
                    for s in range(2):
                        load(mixp + OUT_P + t, s, OUT_W, i["w_out"][l, t * 2 + s])
                ffn_chunks(l, 1, mixp + MIX_PAIRS)
            for k in range(KT):
                sp.wait_ge(s_y, k + 1)
                sp.dma_start(o["y"][:, k], x[:, k, :]).then_inc(s_out, 16)
            sp.wait_ge(s_out, 16 * (2 * DEPTH + KT))

        @block.gpsimd
        def _(pool):
            pool.sem_inc(s_split, CREDIT)
            pool.sem_inc(s_rot, START)
            nc.gpsimd.memset(ones[:], 1.0).then_inc(s_fill, 1)
            nc.gpsimd.memset(eps[:], EPS).then_inc(s_fill, 1)
            nc.gpsimd.memset(cond[:], 0.0).then_inc(s_fill, 1)
            nc.gpsimd.memset(ident[:], 0.0).then_inc(s_fill, 1)
            pool.wait_ge(s_fill, 4)
            nc.gpsimd.affine_select(out=ident[:], in_=ident[:], compare_op=ALU.not_equal, fill=1.0, base=0,
                                    pattern=[[-1, P]], channel_multiplier=1).then_inc(s_fill, 1)

            def split(p, s, width, rotated=None):
                if rotated is not None:
                    pool.wait_ge(s_rot, rotated * 3 + START)
                r, hi, lo = raw[s][:, 0:width], w_hi[s][:, 0:width], w_lo[s][:, 0:width]
                pool.wait_ge(s_raw[s], (p + 1) * 16)
                pool.wait_ge(s_chunk, p * 2 + s + 1)
                nc.gpsimd.tensor_tensor(hi, r, ones[:, 0:1].to_broadcast([P, width]), ALU.mult).then_inc(s_whi, 1)
                pool.wait_ge(s_whi, p * 2 + s + 1)
                nc.gpsimd.tensor_tensor(lo, r, hi.bitcast(F32), ALU.subtract).then_inc(s_split, 1)

            def pairs(first, count, width, rotated=None):
                with pool.Fori(0, count) as t:
                    for s in range(2):
                        split(first + t, s, width, rotated)

            def ffn_chunks(base):
                for half in range(2):
                    up = base + half * (FH + KT // 2)
                    pairs(up, FH, UP_W)
                    pairs(up + FH, KT // 2, DOWN_W)

            def rotate(hd):
                pool.wait_ge(s_q32, hd + 1)
                nc.gpsimd.tensor_tensor(rot[NOPE:QK], q32[QK:P], rope_tab[QK:P, :], ALU.mult).then_inc(s_rot, 1)
                pool.wait_ge(s_rot, hd * 3 + 1 + START)
                nc.gpsimd.tensor_tensor(q32[NOPE:QK], q32[NOPE:QK], rope_tab[NOPE:QK, :], ALU.mult).then_inc(s_rot, 1)
                pool.wait_ge(s_rot, hd * 3 + 2 + START)
                nc.gpsimd.tensor_tensor(q32[NOPE:QK], q32[NOPE:QK], rot[NOPE:QK], ALU.add).then_inc(s_rot, 1)

            with pool.Fori(0, DEPTH) as l:
                base = l * LAYER_PAIRS
                ffn_chunks(base)
                mixp = base + FFN_PAIRS
                pairs(mixp + IN_P, 4, IN_W)
                split(mixp + DFT_P, 0, CHAN_W)
                split(mixp + DFT_P, 1, PDFT_W)
                pairs(mixp + SEQ_P, 2, SDFT_W)
                with pool.Fori(0, HEADS // 2) as t:
                    for s in range(2):
                        split(mixp + HEAD_P + t, s, HEAD_W, l * HEADS + t * 2 + s)
                        rotate(l * HEADS + t * 2 + s)
                pairs(mixp + MERGE_P, KT, MERGE_W, (l + 1) * HEADS)
                pairs(mixp + OUT_P, KT // 2, OUT_W)
                ffn_chunks(mixp + MIX_PAIRS)

        @block.tensor
        def _(pe):
            pe.sem_inc(s_chunk, CREDIT)
            pe.sem_inc(s_wmused, CREDIT)
            for started in (s_modt, s_pt, s_pv):
                pe.sem_inc(started, START)

            def product(outs, whi, wlo, xhi, xlo, first, last):
                for n, (out, v) in enumerate(zip(outs, xhi)):
                    nc.tensor.matmul(out, whi, v, start=first, stop=False)
                for out, v in zip(outs, xlo):
                    nc.tensor.matmul(out, whi, v, start=False, stop=False)
                for out, v in zip(outs, xhi):
                    mm = nc.tensor.matmul(out, wlo, v, start=False, stop=last)
                return mm

            def w_tile(s, n):
                return w_hi[s][:, n * P:(n + 1) * P], w_lo[s][:, n * P:(n + 1) * P]

            def dense(out, s, tiles, xhi, xlo, before=None, first=True, last=True):
                for n, (wt, k) in enumerate(tiles):
                    if before:
                        before(k)
                    mm = product(halves(out), *w_tile(s, wt), halves(xhi[:, k, :]), halves(xlo[:, k, :]),
                                 first and n == 0, last and n == len(tiles) - 1)
                return mm

            def chunk(p, s):
                pe.wait_ge(s_split, p * 2 + s + 1 + CREDIT)

            def norm_sum(nn):
                pe.wait_ge(s_acc, (nn + 1) * (KT + 1))
                for n in range(2):
                    mm = nc.tensor.matmul(halves(pair(3))[n], ones[:], halves(acc)[n], start=True, stop=True)
                mm.then_inc(s_sum, 1)

            def mod_step(e, k, start=None):
                if start is None:
                    weights = wm[k % 2]
                    pe.wait_ge(s_wm[k % 2], ((e - 2) * (KT // 2) + k // 2 + 1) * 16)
                else:
                    weights = wm_start[start]
                    pe.wait_ge(s_start[start], 16)
                if k == 0:
                    pe.wait_ge(s_modrow, e + START)
                for j in range(4):
                    mm = nc.tensor.matmul(bank(4)[32 * j:32 * j + 32, 0:MOD_COLS], cond[:, k, :],
                                          weights[:, j * MOD_COLS:(j + 1) * MOD_COLS],
                                          start=(k == 0), stop=(k == KT - 1))
                mm.then_inc(s_wmused, 1)

            def mod_turn(e):
                pe.wait_ge(s_modrow, e + 1 + START)
                pe.wait_ge(s_mod, e + START)
                for b in range(MOD_COLS // P):
                    mm = nc.tensor.transpose(bank(5)[:, b * P:(b + 1) * P], mod_row[:, b * P:(b + 1) * P], ident[:])
                mm.then_inc(s_modt, 1)

            def ffn_step(l, f, base, nn, mods):
                every = [(k, k) for k in range(KT)]
                for half in range(2):
                    up = base + half * (FH + KT // 2)
                    g0 = (l * 2 + f) * 2 * FH + half * FH

                    def hidden_tile(t, first):
                        chunk(up + t, 0)
                        pe.wait_ge(s_silu, g0 + t + START)
                        if first and not half:
                            pe.wait_ge(s_blo, nn + 1)
                            pe.wait_ge(s_xupd, XUPD0 + l * UPD + f * 3 * KT - 1)
                        if half:
                            pe.wait_ge(s_xupd, XUPD0 + l * UPD + f * 3 * KT + KT)
                        dense(pairb(0), 0, every, h_hi, h_lo,
                              (lambda k: pe.wait_ge(s_hlo, nn * KT + k + 1 + START)) if first and not half else None
                              ).then_inc(s_chunk, 1)
                        if first and not half:
                            norm_sum(nn)
                        chunk(up + t, 1)
                        pe.wait_ge(s_prod, g0 + t + START)
                        dense(pairb(1), 1, every, h_hi, h_lo).then_inc(s_chunk, 1)

                    if half == 0:
                        hidden_tile(0, True)
                    with pe.Fori(1 - half, FH) as t:
                        hidden_tile(t, False)
                    upd0 = XUPD0 + l * UPD + f * 3 * KT + half * KT
                    with pe.Fori(0, 2) as t:
                        for m in range(4):
                            chunk(up + FH + t * 2 + m // 2, m % 2)
                            pe.wait_ge(s_xupd, upd0 + t * 4 + m - 1)
                            if m == 0:
                                pe.wait_ge(s_silu, g0 + FH + START)
                            dense(pair(m % 2), m % 2, [(k, k) for k in range(FH)], a_hi, a_lo,
                                  lambda k: pe.wait_ge(s_alo, g0 + k + 1 + START)).then_inc(s_chunk, 1)
                            if mods[half] is not None:
                                mod_step(mods[half] + t, 2 * m)
                                mod_step(mods[half] + t, 2 * m + 1)
                        if mods[half] is not None:
                            mod_turn(mods[half] + t)

            def mixer_step(l, mixp, nn):
                for t in range(8):
                    chunk(mixp + IN_P + t // 2, t % 2)
                    if t >= 2:
                        pe.wait_ge(s_lat, l * 8 + t - 1)
                    if t == 0:
                        pe.wait_ge(s_blo, nn + 1)
                        pe.wait_ge(s_xupd, XUPD0 + l * UPD + 2 * KT - 1)
                    dense(pairb(t % 2), t % 2, [(k, k) for k in range(KT)], h_hi, h_lo,
                          (lambda k: pe.wait_ge(s_hlo, nn * KT + k + 1 + START)) if t == 0 else None).then_inc(s_chunk, 1)
                    if t == 0:
                        norm_sum(nn)
                    if t >= 6:
                        pe.wait_ge(s_lacc, l * (QT + CT) + (QT if t == 6 else QT + CT))
                        for n in range(2):
                            mm = nc.tensor.matmul(halves(pair(t - 4))[n], ones[:], halves(lat_acc)[n],
                                                  start=True, stop=True)
                        mm.then_inc(s_lsum, 1)
                chunk(mixp + DFT_P, 0)
                pe.wait_ge(s_flo, (l + 1) * FT + START)
                bd_hi, bd_lo = w_hi[0][:, 0:CHAN_W], w_lo[0][:, 0:CHAN_W]
                for t in range(UNITS):
                    if t == 4:
                        pe.wait_ge(s_uvlo, l * UNITS + 1)
                    for c in range(FT):
                        tok = slice(TOK[t], TOK[t] + P)
                        mm = product([bank(t % 4, c * CHAN_W, (c + 1) * CHAN_W)], f_hi[:, c, tok], f_lo[:, c, tok],
                                     [bd_hi], [bd_lo], True, True)
                    mm.then_inc(s_chan if t < 4 else s_chunk, 1)
                chunk(mixp + DFT_P, 1)
                pe.wait_ge(s_uvlo, (l + 1) * UNITS)
                for c in range(FT):
                    for n in range(2):
                        st = slice((2 * c + n) * P, (2 * c + n + 1) * P)
                        mm = product([bank(1, c * P, (c + 1) * P)], uv_hi[:, 4, st], uv_lo[:, 4, st],
                                     [w_hi[1][:, n * P:(n + 1) * P]], [w_lo[1][:, n * P:(n + 1) * P]], n == 0, n == 1)
                mm.then_inc(s_chunk, 1)
                for t in range(4):
                    chunk(mixp + SEQ_P + t // 2, t % 2)
                    for c in range(FT):
                        for n in range(2):
                            st = slice((2 * c + n) * P, (2 * c + n + 1) * P)
                            mv = slice(n * SAMPLE, (n + 1) * SAMPLE)
                            mm = product([bank(2 + c)], uv_hi[:, t, st], uv_lo[:, t, st],
                                         [w_hi[t % 2][:, mv]], [w_lo[t % 2][:, mv]],
                                         t == 0 and n == 0, t == 3 and n == 1)
                    mm.then_inc(s_chunk, 1)
                hd0, hp = l * HEADS, mixp + HEAD_P
                pe.wait_ge(s_nlo, (l + 1) * (QT + CT))
                pe.wait_ge(s_pastlo, (l + 1) * 2)
                pe.wait_ge(s_krlo, l + 1)
                pe.wait_ge(s_frlo, (l + 1) * 3)
                queries(hd0, hp, 0, False)
                keys(hd0, 0)
                values_of(hd0, 0, 0, 7)
                with pe.Fori(0, HEADS // 2 - 1) as t:
                    attend(hd0 + t * 2, (hp + t, 1))
                    attend(hd0 + t * 2 + 1, (hp + t + 1, 0))
                last = HEADS // 2 - 1
                attend(hd0 + last * 2, (hp + last, 1))
                attend(hd0 + last * 2 + 1, None)
                with pe.Fori(0, KT) as m:
                    n0 = l * KT + m
                    chunk(mixp + MERGE_P + m, 0)
                    pe.wait_ge(s_sgf, n0 + START)
                    dense(pairb(0), 0, [(k, k) for k in range(KT)], h_hi, h_lo).then_inc(s_gf, 1)
                    pe.wait_ge(s_p2, n0 + START)
                    pe.wait_ge(s_olo, (l + 1) * 2 * HEADS + START)
                    dense(pair(1), 0, [(KT + k, k) for k in range(3)], ot_hi, ot_lo, last=False).then_inc(s_chunk, 1)
                    chunk(mixp + MERGE_P + m, 1)
                    dense(pair(1), 1, [(KT, 3)], ot_hi, ot_lo, first=False).then_inc(s_op, 1)
                    pe.wait_ge(s_sga, n0 + START)
                    dense(pairb(2), 1, [(k, k) for k in range(KT)], h_hi, h_lo).then_inc(s_ga, 1)
                    pe.wait_ge(s_p1, n0 + START)
                    dense(pair(3), 1, [(KT + 1 + k, k) for k in range(FT)], fr_hi, fr_lo).then_inc(s_chunk, 1)
                upd0 = XUPD0 + l * UPD + 2 * KT
                with pe.Fori(0, KT // 2) as t:
                    for s in range(2):
                        chunk(mixp + OUT_P + t, s)
                        pe.wait_ge(s_xupd, upd0 + t * 2 + s - 1)
                        pe.wait_ge(s_p2 if s else s_sgf, (l + 1) * KT + START)
                        dense(pair(s), s, [(k, k) for k in range(KT)], m_hi, m_lo,
                              lambda k: pe.wait_ge(s_mlo, l * KT + k + 1 + START)).then_inc(s_chunk, 1)

            def queries(hd, p, s, inner=True):
                chunk(p, s)
                pe.wait_ge(s_vlo, hd + START)
                for out, cols in ((bank(4), slice(0, 512)), (bank(1, PAST, PAST + T - 512), slice(512, T))):
                    if cols.start:
                        pe.wait_ge(s_exp, (hd - 1) * UNITS + 1 + START if inner else hd * UNITS + START)
                    for k in range(QT):
                        mm = product([out], *w_tile(s, k), [qn_hi[:, k, cols]], [qn_lo[:, k, cols]], k == 0, k == QT - 1)
                mm.then_inc(s_qmm, 1)

            def keys(hd, s):
                k0 = QT * P
                for c in range(CT):
                    w = slice(k0 + c * NOPE, k0 + (c + 1) * NOPE)
                    mm = product([bank(2 + n, 0, KEYS // 2)[0:NOPE] for n in range(2)], w_hi[s][:, w], w_lo[s][:, w],
                                 [cn_hi[:, c, n * KEYS // 2:(n + 1) * KEYS // 2] for n in range(2)],
                                 [cn_lo[:, c, n * KEYS // 2:(n + 1) * KEYS // 2] for n in range(2)],
                                 c == 0, c == CT - 1)
                mm.then_inc(s_kmm, 1)

            def values_of(hd, s, n0, n1):
                v0 = QT * P + CT * NOPE
                if n0 == 0:
                    pe.wait_ge(s_q32, hd + 1)
                for n, col in list(enumerate(TOK[0:4] + [T, T + P, PRO]))[n0:n1]:
                    for c in range(CT):
                        w = slice(v0 + c * VD, v0 + (c + 1) * VD)
                        mm = product([bank(4, n * VD, (n + 1) * VD)], cn_hi[:, c, col:col + P], cn_lo[:, c, col:col + P],
                                     [w_hi[s][:, w]], [w_lo[s][:, w]], c == 0, c == CT - 1)
                if n1 == 7:
                    mm.then_inc(s_chunk, 1)

            def attend(hd, following):
                u0 = hd * UNITS

                def scores(u):
                    if u == 0:
                        pe.wait_ge(s_qlo, hd + 1)
                        pe.wait_ge(s_klo, hd + 1)
                    if u >= 2:
                        pe.wait_ge(s_exp, u0 + u - 1 + START)
                    if u == 2 and following:
                        pe.wait_ge(s_q32, hd + 2)
                    st = slice(TOK[u], TOK[u] + P)
                    qh, ql = q_hi[0:QK, st], q_lo[0:QK, st]
                    b = 2 * (u % 2)
                    if u < 4:
                        product([bank(b)], qh, ql, [two(k_hi[0:QK, :])], [two(k_lo[0:QK, :])], True, True)
                        mm = product([bank(b + 1, 0, PAST)], qh, ql, [k_hi[0:QK, T:KEYS]], [k_lo[0:QK, T:KEYS]],
                                     True, True)
                    else:
                        mm = product([bank(b, 0, P)], qh, ql, [k_hi[0:QK, PRO:PRO + P]], [k_lo[0:QK, PRO:PRO + P]],
                                     True, True)
                    mm.then_inc(s_s, 1)

                def turn(u):
                    pe.wait_ge(s_pn, u0 + u + 1)
                    pe.wait_ge(s_ptlo, u0 + u + START)
                    for n in range(6 if u < 4 else 1):
                        mm = nc.tensor.transpose(bank(5 + n // 4, (n % 4) * P, (n % 4 + 1) * P),
                                                 probs[u % 2][:, n * P:(n + 1) * P], ident[:])
                    mm.then_inc(s_pt, 1)

                def values(u):
                    pe.wait_ge(s_ptlo, u0 + u + 1 + START)
                    if u == 0:
                        pe.wait_ge(s_vlo, hd + 1 + START)
                        pe.wait_ge(s_olo, hd * 2 + START)
                    out = bank(7, u * P, (u + 1) * P) if u < 4 else bank(6, 384, 512)
                    tiles = range(6) if u < 4 else [6]
                    for n, kt in enumerate(tiles):
                        mm = product([out[0:VD]], v_hi[:, kt, :], v_lo[:, kt, :],
                                     [pt_hi[:, u % 2, n * P:(n + 1) * P]], [pt_lo[:, u % 2, n * P:(n + 1) * P]],
                                     n == 0, n == len(tiles) - 1)
                    mm.then_inc(s_pv, 1)

                scores(0)
                scores(1)
                if following:
                    queries(hd + 1, *following)
                for u in range(UNITS):
                    turn(u)
                    if u + 2 < UNITS:
                        scores(u + 2)
                    if following and u == 3:
                        keys(hd + 1, following[1])
                    if following and u <= 3:
                        values_of(hd + 1, following[1], 2 * u, min(2 * u + 2, 7))
                    if u >= 1:
                        values(u - 1)
                values(UNITS - 1)

            pe.wait_ge(s_fill, 5)
            pe.wait_ge(s_cond, 1)
            for e in range(2):
                for k in range(KT):
                    mod_step(e, k, e * KT + k)
                mod_turn(e)
            with pe.Fori(0, DEPTH) as l:
                base = l * LAYER_PAIRS
                e0 = l * MOD_BATCHES + 2
                ffn_step(l, 0, base, l * 3, (e0, e0 + 2))
                mixer_step(l, base + FFN_PAIRS, l * 3 + 1)
                ffn_step(l, 1, base + FFN_PAIRS + MIX_PAIRS, l * 3 + 2, (e0 + 4, None))
            norm_sum(3 * DEPTH)

        @block.scalar
        def _(act):
            for started in (s_modrow, s_silu, s_exp, s_sgf, s_sga):
                act.sem_inc(started, START)

            def mod_load(e, le, b, k):
                act.wait_ge(s_wmused, e * KT + k + 1)
                act.dma_start(wm[k % 2][:], i["w_mod"][le, b, k]).then_inc(s_wm[k % 2], 16)

            def mod_copy(e):
                act.wait_ge(s_wmused, (e + 1) * KT + CREDIT)
                act.wait_ge(s_modt, e + START)
                nc.scalar.activation(mod_row[:], bank(4, 0, MOD_COLS), ACT.Copy).then_inc(s_modrow, 1)

            def rms(nn):
                act.wait_ge(s_sum, nn + 1)
                nc.scalar.activation(std, pair(3), ACT.Sqrt, scale=1.0 / D, bias=eps[:, 0:1]).then_inc(s_std, 1)

            def split_shift(nn, j):
                act.wait_ge(s_coef, nn + 1)
                nc.scalar.activation(h_hi[:, :, T:TB], mod[:, :, 3 * j * KT:(3 * j + 1) * KT].rearrange("p g k -> p k g"),
                                     ACT.Copy).then_inc(s_bhi, 1)

            def prepare(nn, k, updates):
                act.wait_ge(s_coef, nn + 1)
                act.wait_ge(s_xupd, updates)
                act.wait_ge(s_acc, nn * (KT + 1) + k + 1)
                hi_part(k)
                nc.scalar.activation(sq, x[:, bass.ds(k, 1), :], ACT.Square).then_inc(s_sq, 1)

            def hi_part(k):
                for g, (v, hi) in groups(x[:, bass.ds(k, 1), :][:, 0, :], h_hi[:, bass.ds(k, 1), 0:T][:, 0, :]):
                    ins = nc.scalar.activation(hi, v, ACT.Copy, scale=scale_a[:, g, bass.ds(k, 1)])
                ins.then_inc(s_hhi, 1)

            def ffn_step(l, f, base, nn, mods):
                for half in range(2):
                    up = base + half * (FH + KT // 2)
                    g0 = (l * 2 + f) * 2 * FH + half * FH
                    if half == 0:
                        rms(nn)
                    with act.Fori(0, FH) as t:
                        act.wait_ge(s_gsc, g0 + t + 1)
                        for g, (v,) in groups(silu):
                            ins = nc.scalar.activation(v, v, ACT.Silu, bias=bias_a[:, g:g + 1])
                        ins.then_inc(s_silu, 1)
                        act.wait_ge(s_prod, g0 + t + 1 + START)
                        nc.scalar.activation(a_hi[:, bass.ds(t, 1), :], prod, ACT.Copy).then_inc(s_ahi, 1)
                    if half == 1:
                        split_shift(nn + 1, (2 * f + 1) % 3)
                    upd0 = XUPD0 + l * UPD + f * 3 * KT + half * KT
                    with act.Fori(0, 2) as t:
                        for m in range(4):
                            if mods[half] is not None:
                                e, le, b = mods[half]
                                mod_load(e + t, le, b + t, 2 * m)
                                mod_load(e + t, le, b + t, 2 * m + 1)
                            if half == 1:
                                prepare(nn + 1, t * 4 + m, upd0 + t * 4 + m + 1)
                        if mods[half] is not None:
                            mod_copy(e + t)

            def mixer_step(l, mixp, nn):
                act.wait_ge(s_chunk, used(mixp + IN_P, 0))
                act.dma_start(past_c, i["past_ckv"][l]).then_inc(s_past, 16)
                act.dma_start(past_k[NOPE:QK, :], i["past_krope"][l]).then_inc(s_past, 16)

                def latent(t0, t1, nsum, width):
                    act.wait_ge(s_lsum, l * 2 + nsum + 1)
                    if nsum:
                        act.wait_ge(s_latn, l * (QT + CT) + QT)
                    nc.scalar.activation(lat_std, pair(2 + nsum), ACT.Sqrt, scale=1.0 / width,
                                         bias=eps[:, 0:1]).then_inc(s_lstd, 1)
                    for t in range(t0, t1):
                        act.wait_ge(s_latn, l * (QT + CT) + t + 1)
                        hi = qn_hi[:, t, :] if t < QT else cn_hi[:, t - QT, 0:T]
                        nc.scalar.activation(hi, lat[:, t, :], ACT.Copy).then_inc(s_nhi, 1)

                rms(nn)
                for t in range(8):
                    p, s = mixp + IN_P + t // 2, t % 2
                    dst = lat[:, t, :] if t < QT + CT else kr32 if t == QT + CT else fourier_in[t - 6]
                    out = f_hi[:, t - 6, :] if t >= 6 else dst
                    p0 = NOPE if t == QT + CT else 0
                    b = (bias_a, bias_b)[s]
                    act.wait_ge(s_latsc, l * 8 + t + 1)
                    for g, (v, to) in groups(dst, out):
                        ins = nc.scalar.activation(to[p0:P], v[p0:P], ACT.Identity, bias=b[p0:P, g:g + 1])
                    ins.then_inc(s_lat, 1)
                    if t == QT + CT:
                        act.wait_ge(s_lat, l * 8 + t + 1)
                        act.dma_start(o["krope"][l], kr32[NOPE:QK, PRO:PRO + PROMPT]).then_inc(s_out, 16)
                        act.wait_ge(s_past, (l + 1) * 32)
                        nc.scalar.activation(cn_hi[:, :, T:KEYS], past_c, ACT.Copy).then_inc(s_pasthi, 1)
                        nc.scalar.activation(k_hi[NOPE:QK, T:KEYS], past_k[NOPE:QK, :], ACT.Copy).then_inc(s_pasthi, 1)
                        act.wait_ge(s_kr, (l + 1) * 3)
                        nc.scalar.activation(k_hi[NOPE:QK, 0:T], kr_cos[NOPE:QK], ACT.Copy).then_inc(s_krhi, 1)
                for t in range(UNITS):
                    if t < 4:
                        act.wait_ge(s_chan, l * 4 + t + 1)
                    else:
                        act.wait_ge(s_chunk, used(mixp + DFT_P, 0))
                    nc.scalar.activation(uv_hi[:, t, :], bank(t % 4), ACT.Copy).then_inc(s_uvhi, 1)
                latent(0, QT, 0, Q_RANK)
                latent(QT, QT + CT, 1, KV_RANK)
                act.dma_start(o["ckv"][l], lat[:, QT:QT + CT, PRO:PRO + PROMPT]).then_inc(s_out, 16)
                act.wait_ge(s_chunk, used(mixp + DFT_P, 1))
                nc.scalar.activation(fr_hi[:, :, PRO:PRO + PROMPT],
                                     bank(1, 0, FT * P).rearrange("p (c n) -> p c n", c=FT),
                                     ACT.Copy).then_inc(s_frhi, 1)
                act.wait_ge(s_chunk, used(mixp + SEQ_P + 1, 1))
                for c in range(FT):
                    nc.scalar.activation(two(fr_hi[:, c, :]), bank(2 + c).rearrange("p (a n) -> p a n", a=2),
                                         ACT.Copy).then_inc(s_frhi, 1)
                hd0, hp, last = l * HEADS, mixp + HEAD_P, HEADS // 2 - 1
                act.wait_ge(s_out, (l + 1) * 32)
                act.wait_ge(s_frlo, (l + 1) * 3)
                queries(hd0)
                keys(hd0)
                split_queries(hd0)
                values(hd0, hp, 0)
                with act.Fori(0, last) as t:
                    attend(hd0 + t * 2, 0, t, (hp + t, 1))
                    attend(hd0 + t * 2 + 1, 1, t, (hp + t + 1, 0))
                attend(hd0 + last * 2, 0, last, (hp + last, 1))
                attend(hd0 + last * 2 + 1, 1, last, None)
                with act.Fori(0, KT) as m:
                    n0 = l * KT + m
                    for scaled, buf, b, ready in ((s_gfsc, sgf, bias_a, s_sgf), (s_gasc, sga, bias_b, s_sga)):
                        act.wait_ge(scaled, n0 + 1)
                        for g, (v,) in groups(buf):
                            ins = nc.scalar.activation(v, v, ACT.Sigmoid, bias=b[:, g:g + 1])
                        ins.then_inc(ready, 1)
                    act.wait_ge(s_m, n0 + 1)
                    nc.scalar.activation(m_hi[:, bass.ds(m, 1), :], p1, ACT.Copy).then_inc(s_mhi, 1)
                split_shift(nn + 1, 2)
                upd0 = XUPD0 + l * UPD + 2 * KT
                with act.Fori(0, KT) as k:
                    prepare(nn + 1, k, upd0 + k + 1)

            def queries(hd):
                act.wait_ge(s_qmm, hd + 1)
                for v, n0, n1 in ((bank(4), 0, 512), (bank(1, PAST, PAST + T - 512), 512, T)):
                    ins = nc.scalar.activation(q32[:, n0:n1], v, ACT.Copy, scale=SCALE)
                ins.then_inc(s_q32, 1)

            def split_queries(hd):
                act.wait_ge(s_rot, (hd + 1) * 3 + START)
                nc.scalar.activation(q_hi[0:QK, :], q32[0:QK], ACT.Copy).then_inc(s_qhi, 1)

            def keys(hd):
                act.wait_ge(s_kmm, hd + 1)
                nc.scalar.activation(k_hi[0:NOPE, :].rearrange("p (a n) -> p a n", a=2),
                                     ps[0:NOPE, 2 * 512:4 * 512].rearrange("p (a n) -> p a n", a=2)[:, :, 0:KEYS // 2],
                                     ACT.Copy).then_inc(s_khi, 1)

            def values(hd, p, s):
                act.wait_ge(s_chunk, used(p, s))
                nc.scalar.activation(v_hi[:], bank(4, 0, 7 * VD), ACT.Copy).then_inc(s_vhi, 1)

            def attend(hd, s, t, following):
                u0 = hd * UNITS

                def exponent(u):
                    n = NK if u < 4 else P
                    act.wait_ge(s_nmx, u0 + u + 1)
                    act.wait_ge(s_pt, u0 + (u - 1 if u >= 2 else 0) + START)
                    nc.scalar.activation(probs[u % 2][:, 0:n], bank(2 * (u % 2))[:, 0:n] if n == P else
                                         ps[:, u % 2 * 1024:u % 2 * 1024 + n], ACT.Exp,
                                         bias=nmx[:, u:u + 1],
                                         accum_out=rsum[:, u:u + 1]).then_inc(s_exp, 1)

                def spread(u):
                    n = NK if u < 4 else P
                    act.wait_ge(s_pt, u0 + u + 1 + START)
                    act.wait_ge(s_pv, u0 + (u - 1 if u >= 2 else 0) + START)
                    nc.scalar.activation(pt_hi[:, u % 2, 0:n], ps[:, 5 * 512:5 * 512 + n], ACT.Copy).then_inc(s_pthi, 1)

                exponent(0)
                exponent(1)
                if following:
                    queries(hd + 1)
                for u in range(3):
                    spread(u)
                    exponent(u + 2)
                if following:
                    split_queries(hd + 1)
                spread(3)
                if following:
                    keys(hd + 1)
                spread(4)
                rows = slice(s * VD, (s + 1) * VD)
                act.wait_ge(s_pv, u0 + 4 + START)
                nc.scalar.activation(two(ot_hi[rows, bass.ds(t, 1), :][:, 0, :]),
                                     bank(7)[0:VD].rearrange("p (a n) -> p a n", a=2), ACT.Copy).then_inc(s_ohi, 1)
                act.wait_ge(s_pv, u0 + 5 + START)
                nc.scalar.activation(pro(ot_hi[rows, bass.ds(t, 1), :][:, 0, :]), bank(6, 384, 512)[0:VD],
                                     ACT.Copy).then_inc(s_ohi, 1)
                if following:
                    values(hd + 1, *following)

            for n in range(2 * KT):
                if n == KT:
                    act.wait_ge(s_condin, 16)
                    act.wait_ge(s_fill, 5)
                    nc.scalar.activation(cond[:, :, 0:2], cond_in[:], ACT.Silu).then_inc(s_cond, 1)
                if n == 2 * KT - 2:
                    act.wait_ge(s_wmused, CREDIT + 1)
                act.dma_start(wm_start[n][:], i["w_mod"][0, n // KT, n % KT]).then_inc(s_start[n], 16)
            act.wait_ge(s_x, 16)
            for k in range(KT):
                act.wait_ge(s_acc, k + 1)
                nc.scalar.activation(sq, x[:, k, :], ACT.Square).then_inc(s_sq, 1)
            for e in range(2):
                mod_copy(e)
            split_shift(0, 0)
            for k in range(KT):
                hi_part(k)
            with act.Fori(0, DEPTH) as l:
                base = l * LAYER_PAIRS
                e0 = l * MOD_BATCHES + 2
                ffn_step(l, 0, base, l * 3, ((e0, l, 2), (e0 + 2, l, 4)))
                mixer_step(l, base + FFN_PAIRS, l * 3 + 1)
                ffn_step(l, 1, base + FFN_PAIRS + MIX_PAIRS, l * 3 + 2, ((e0 + 4, 1, 0), None))
            rms(3 * DEPTH)

        @block.vector
        def _(dve):
            dve.sem_inc(s_xupd, XUPD0)
            for started in (s_mod, s_prod, s_alo, s_hlo, s_flo, s_ptlo, s_vlo, s_olo, s_p1, s_p2, s_mlo):
                dve.sem_inc(started, START)
            tt, stt = nc.vector.tensor_tensor, nc.vector.scalar_tensor_tensor

            def xk(k):
                return x[:, bass.ds(k, 1), :][:, 0, :]

            def prepare(nn, k, updates):
                dve.wait_ge(s_coef, nn + 1)
                dve.wait_ge(s_xupd, updates)
                lo_part(nn, k)
                add_square(nn, k)

            def lo_part(nn, k):
                dve.wait_ge(s_hhi, nn * KT + k + 1)
                for g, (v, hi, lo) in groups(xk(k), h_hi[:, bass.ds(k, 1), 0:T][:, 0, :], h_lo[:, bass.ds(k, 1), 0:T][:, 0, :]):
                    ins = stt(out=lo, in0=v, scalar=scale_a[:, g, bass.ds(k, 1)], in1=hi.bitcast(F32),
                              op0=ALU.mult, op1=ALU.subtract)
                ins.then_inc(s_hlo, 1)

            def add_square(nn, k):
                dve.wait_ge(s_sq, nn * KT + k + 1)
                dve.wait_ge(s_acc, nn * (KT + 1) + k + 1)
                tt(acc, acc, sq, ALU.add).then_inc(s_acc, 1)

            def clear_acc(nn):
                dve.wait_ge(s_sum, nn)
                nc.vector.memset(acc, 0.0).then_inc(s_acc, 1)

            def mod_add(e, lb, b):
                dve.wait_ge(s_modt, e + 1 + START)
                cols = bank(5, 0, MOD_COLS).rearrange("p (b j r) -> p j b r", b=MOD_COLS // P, j=4)
                for g in range(2):
                    n = MB // P
                    ins = tt(mod[:, g, bass.ds(b * n, n)].rearrange("p (j b) -> p j b", j=4), cols[:, :, :, g],
                             bmod[:, bass.ds(lb, 1), bass.ds(b * n, n)][:, 0, :].rearrange("p (j b) -> p j b", j=4), ALU.add)
                ins.then_inc(s_mod, 1)

            def coefficients(nn, j, e_need):
                dve.wait_ge(s_mod, e_need + START)
                dve.wait_ge(s_hlo, nn * KT + START)
                for g in range(2):
                    ins = stt(out=scale_a[:, g, :], in0=mod[:, g, (3 * j + 1) * KT:(3 * j + 2) * KT], scalar=1.0,
                              in1=gains[:, bass.ds(nn, 1), :][:, 0, :], op0=ALU.add, op1=ALU.mult)
                ins.then_inc(s_coef, 1)
                dve.wait_ge(s_bhi, nn + 1)
                tt(h_lo[:, :, T:TB], mod[:, :, 3 * j * KT:(3 * j + 1) * KT].rearrange("p g k -> p k g"),
                   h_hi[:, :, T:TB].bitcast(F32), ALU.subtract).then_inc(s_blo, 1)

            def inverse(nn):
                dve.wait_ge(s_std, nn + 1)
                for n in range(2):
                    ins = nc.vector.reciprocal(halves(rstd)[n], halves(std)[n])
                ins.then_inc(s_rstd, 1)

            def update(k, src, gate, col):
                for g, (v, y) in groups(xk(k), src):
                    ins = stt(out=v, in0=y, scalar=gate[:, g, bass.ds(k + col, 1)], in1=v, op0=ALU.mult, op1=ALU.add)
                ins.then_inc(s_xupd, 1)

            def ffn_step(l, f, base, nn, mods):
                j = 2 * f
                for half in range(2):
                    up = base + half * (FH + KT // 2)
                    g0 = (l * 2 + f) * 2 * FH + half * FH
                    if half == 0:
                        inverse(nn)
                    with dve.Fori(0, FH) as t:
                        dve.wait_ge(s_chunk, used(up + t, 0))
                        dve.wait_ge(s_alo, g0 + t + START)
                        dve.wait_ge(s_rstd, nn + 1)
                        nc.vector.tensor_copy(bias_a[:], shifts(0))
                        tt(silu, pair(0), rstd, ALU.mult).then_inc(s_gsc, 1)
                        dve.wait_ge(s_chunk, used(up + t, 1))
                        nc.vector.tensor_copy(bias_b[:], shifts(1))
                        tt(prod, pair(1), rstd, ALU.mult).then_inc(s_usc, 1)
                        dve.wait_ge(s_usc, g0 + t + 1)
                        dve.wait_ge(s_silu, g0 + t + 1 + START)
                        for g, (u, v) in groups(prod, silu):
                            ins = stt(out=u, in0=u, scalar=bias_b[:, g:g + 1], in1=v, op0=ALU.add, op1=ALU.mult)
                        ins.then_inc(s_prod, 1)
                        dve.wait_ge(s_prod, g0 + t + 1 + START)
                        dve.wait_ge(s_ahi, g0 + t + 1)
                        tt(a_lo[:, bass.ds(t, 1), :][:, 0, :], prod, a_hi[:, bass.ds(t, 1), :][:, 0, :].bitcast(F32),
                           ALU.subtract).then_inc(s_alo, 1)
                    if half == 0:
                        dve.wait_ge(s_xupd, XUPD0 + l * UPD + f * 3 * KT)
                        nc.vector.tensor_scalar(half_g[:], mod[:, :, (3 * j + 2) * KT:(3 * j + 3) * KT], 0.5, None,
                                                ALU.mult).then_inc(s_half, 1)
                    else:
                        clear_acc(nn + 1)
                        coefficients(nn + 1, (2 * f + 1) % 3, l * MOD_BATCHES + (4 if f == 0 else 8))
                    upd0 = XUPD0 + l * UPD + f * 3 * KT + half * KT
                    with dve.Fori(0, 2) as t:
                        for m in range(4):
                            k = t * 4 + m
                            dve.wait_ge(s_chunk, used(up + FH + t * 2 + m // 2, m % 2))
                            dve.wait_ge(s_half, l * 2 + f + 1)
                            update(k, pair(m % 2), half_g, 0)
                            if half == 1:
                                prepare(nn + 1, k, upd0 + k + 1)
                        if mods[half] is not None:
                            e, lb, b = mods[half]
                            mod_add(e + t, lb, b + t)

            def mixer_step(l, mixp, nn):
                lo_of = lambda out, src, hi: tt(out, src, hi.bitcast(F32), ALU.subtract)
                n5 = l * (QT + CT)
                def square(t):
                    dve.wait_ge(s_lat, l * 8 + t + 1)
                    if t == QT:
                        dve.wait_ge(s_lsum, l * 2 + 1)
                    if t in (0, QT):
                        tt(lat_acc, lat[:, t, :], lat[:, t, :], ALU.mult).then_inc(s_lacc, 1)
                    else:
                        dve.wait_ge(s_lacc, n5 + t)
                        tt(lat_sq, lat[:, t, :], lat[:, t, :], ALU.mult).then_inc(s_lsq, 1)
                        dve.wait_ge(s_lsq, l * (QT + CT - 2) + (t if t < QT else t - 1))
                        tt(lat_acc, lat_acc, lat_sq, ALU.add).then_inc(s_lacc, 1)

                def latent(t0, t1, nsum):
                    dve.wait_ge(s_lstd, l * 2 + nsum + 1)
                    for n in range(2):
                        ins = nc.vector.reciprocal(halves(lat_std)[n], halves(lat_std)[n])
                    ins.then_inc(s_lrstd, 1)
                    dve.wait_ge(s_lrstd, l * 2 + nsum + 1)
                    for t in range(t0, t1):
                        stt(out=lat[:, t, :], in0=lat[:, t, :], scalar=lat_gain[:, bass.ds(l, 1), t],
                            in1=lat_std, op0=ALU.mult, op1=ALU.mult).then_inc(s_latn, 1)
                    for t in range(t0, t1):
                        dve.wait_ge(s_latn, n5 + t + 1)
                        dve.wait_ge(s_nhi, n5 + t + 1)
                        hi, lo = (qn_hi[:, t, :], qn_lo[:, t, :]) if t < QT else \
                            (cn_hi[:, t - QT, 0:T], cn_lo[:, t - QT, 0:T])
                        lo_of(lo, lat[:, t, :], hi).then_inc(s_nlo, 1)

                inverse(nn)

                def scale(t):
                    dve.wait_ge(s_chunk, used(mixp + IN_P + t // 2, t % 2))
                    dst = lat[:, t, :] if t < QT + CT else kr32 if t == QT + CT else fourier_in[t - 6]
                    p0 = NOPE if t == QT + CT else 0
                    if t >= 6:
                        dve.wait_ge(s_krlo, l + 1)
                    dve.wait_ge(s_rstd, nn + 1)
                    nc.vector.tensor_copy((bias_a, bias_b)[t % 2][p0:P], shifts(t % 2, p0))
                    tt(dst[p0:P], pair(t % 2)[p0:P], rstd[p0:P], ALU.mult).then_inc(s_latsc, 1)

                for t in range(QT):
                    scale(t)
                    square(t)
                scale(3)
                scale(4)
                scale(5)
                dve.wait_ge(s_lat, l * 8 + 6)
                tt(kr_sin[NOPE:QK], kr32[QK:P], rope_tab[QK:P, :], ALU.mult).then_inc(s_kr, 1)
                tt(kr_cos[NOPE:QK], kr32[NOPE:QK], rope_tab[NOPE:QK, :], ALU.mult).then_inc(s_kr, 1)
                dve.wait_ge(s_kr, l * 3 + 2)
                tt(kr_cos[NOPE:QK], kr_cos[NOPE:QK], kr_sin[NOPE:QK], ALU.add).then_inc(s_kr, 1)
                dve.wait_ge(s_pasthi, (l + 1) * 2)
                lo_of(cn_lo[:, :, T:KEYS], past_c, cn_hi[:, :, T:KEYS]).then_inc(s_pastlo, 1)
                lo_of(k_lo[NOPE:QK, T:KEYS], past_k[NOPE:QK, :], k_hi[NOPE:QK, T:KEYS]).then_inc(s_pastlo, 1)
                dve.wait_ge(s_kr, (l + 1) * 3)
                dve.wait_ge(s_krhi, l + 1)
                lo_of(k_lo[NOPE:QK, 0:T], kr_cos[NOPE:QK], k_hi[NOPE:QK, 0:T]).then_inc(s_krlo, 1)
                for c in range(FT):
                    scale(6 + c)
                    dve.wait_ge(s_latsc, l * 8 + 7 + c)
                    dve.wait_ge(s_lat, l * 8 + 7 + c)
                    for g, (v, hi, lo) in groups(fourier_in[c], f_hi[:, c, :], f_lo[:, c, :]):
                        ins = stt(out=lo, in0=v, scalar=(bias_a, bias_b)[c][:, g:g + 1], in1=hi.bitcast(F32),
                                  op0=ALU.add, op1=ALU.subtract)
                    ins.then_inc(s_flo, 1)
                    if c == 0:
                        for t in range(QT, QT + CT):
                            square(t)
                for t in range(UNITS):
                    dve.wait_ge(s_uvhi, l * UNITS + t + 1)
                    lo_of(uv_lo[:, t, :], bank(t % 4), uv_hi[:, t, :]).then_inc(s_uvlo, 1)
                latent(0, QT, 0)
                latent(QT, QT + CT, 1)
                dve.wait_ge(s_frhi, l * 3 + 1)
                lo_of(fr_lo[:, :, PRO:PRO + PROMPT], bank(1, 0, FT * P).rearrange("p (c n) -> p c n", c=FT),
                      fr_hi[:, :, PRO:PRO + PROMPT]).then_inc(s_frlo, 1)
                for c in range(FT):
                    dve.wait_ge(s_frhi, l * 3 + 2 + c)
                    lo_of(two(fr_lo[:, c, :]), bank(2 + c).rearrange("p (a n) -> p a n", a=2),
                          two(fr_hi[:, c, :])).then_inc(s_frlo, 1)
                hd0, last = l * HEADS, HEADS // 2 - 1
                dve.wait_ge(s_out, (l + 1) * 32)
                split_keys(hd0, lo_of)
                split_queries(hd0, lo_of)
                split_values(hd0, lo_of)
                with dve.Fori(0, last) as t:
                    for s in range(2):
                        attend(hd0 + t * 2 + s, s, t, lo_of, True)
                attend(hd0 + last * 2, 0, last, lo_of, True)
                attend(hd0 + last * 2 + 1, 1, last, lo_of, False)
                with dve.Fori(0, KT) as m:
                    n0 = l * KT + m
                    dve.wait_ge(s_gf, n0 + 1)
                    dve.wait_ge(s_mlo, n0 + START)
                    nc.vector.tensor_copy(bias_a[:], shifts(0))
                    tt(sgf, pair(0), rstd, ALU.mult).then_inc(s_gfsc, 1)
                    dve.wait_ge(s_ga, n0 + 1)
                    nc.vector.tensor_copy(bias_b[:], shifts(2))
                    tt(sga, pair(2), rstd, ALU.mult).then_inc(s_gasc, 1)
                    dve.wait_ge(s_op, n0 + 1)
                    dve.wait_ge(s_sga, n0 + 1 + START)
                    tt(p2, pair(1), sga, ALU.mult).then_inc(s_p2, 1)
                    dve.wait_ge(s_chunk, used(mixp + MERGE_P + m, 1))
                    dve.wait_ge(s_sgf, n0 + 1 + START)
                    tt(p1, pair(3), sgf, ALU.mult).then_inc(s_p1, 1)
                    dve.wait_ge(s_p1, n0 + 1 + START)
                    dve.wait_ge(s_p2, n0 + 1 + START)
                    tt(p1, p1, p2, ALU.add).then_inc(s_m, 1)
                    dve.wait_ge(s_m, n0 + 1)
                    dve.wait_ge(s_mhi, n0 + 1)
                    lo_of(m_lo[:, bass.ds(m, 1), :][:, 0, :], p1, m_hi[:, bass.ds(m, 1), :][:, 0, :]).then_inc(s_mlo, 1)
                clear_acc(nn + 1)
                coefficients(nn + 1, 2, l * MOD_BATCHES + 6)
                with dve.Fori(0, KT // 2) as t:
                    for s in range(2):
                        k = t * 2 + s
                        dve.wait_ge(s_chunk, used(mixp + OUT_P + t, s))
                        update(k, pair(s), mod, 5 * KT)
                        prepare(nn + 1, k, XUPD0 + l * UPD + 2 * KT + k + 1)

            def split_keys(hd, lo_of):
                dve.wait_ge(s_khi, hd + 1)
                lo_of(k_lo[0:NOPE, :].rearrange("p (a n) -> p a n", a=2),
                      ps[0:NOPE, 2 * 512:4 * 512].rearrange("p (a n) -> p a n", a=2)[:, :, 0:KEYS // 2],
                      k_hi[0:NOPE, :].rearrange("p (a n) -> p a n", a=2)).then_inc(s_klo, 1)

            def split_queries(hd, lo_of):
                dve.wait_ge(s_qhi, hd + 1)
                lo_of(q_lo[0:QK, :], q32[0:QK], q_hi[0:QK, :]).then_inc(s_qlo, 1)

            def split_values(hd, lo_of):
                dve.wait_ge(s_vhi, hd + 1)
                lo_of(v_lo[:].rearrange("p a n -> p (a n)"), bank(4, 0, 7 * VD),
                      v_hi[:].rearrange("p a n -> p (a n)")).then_inc(s_vlo, 1)

            def attend(hd, s, t, lo_of, following):
                u0 = hd * UNITS

                def maxima(u):
                    n = NK if u < 4 else P
                    dve.wait_ge(s_s, u0 + u + 1)
                    nc.vector.tensor_reduce(nmx[:, u:u + 1], ps[:, u % 2 * 1024:u % 2 * 1024 + n], AX.X,
                                            ALU.max, negate=True).then_inc(s_nmx, 1)

                def normal(u):
                    n = NK if u < 4 else P
                    dve.wait_ge(s_exp, u0 + u + 1 + START)
                    nc.vector.reciprocal(rinv[:, u:u + 1], rsum[:, u:u + 1]).then_inc(s_rinv, 1)
                    dve.wait_ge(s_rinv, u0 + u + 1)
                    pr = probs[u % 2][:, 0:n]
                    nc.vector.tensor_scalar(pr, pr, rinv[:, u:u + 1], None, ALU.mult).then_inc(s_pn, 1)

                def spread(u):
                    n = NK if u < 4 else P
                    dve.wait_ge(s_pthi, u0 + u + 1)
                    lo_of(pt_lo[:, u % 2, 0:n], ps[:, 5 * 512:5 * 512 + n], pt_hi[:, u % 2, 0:n]).then_inc(s_ptlo, 1)

                maxima(0)
                maxima(1)
                normal(0)
                normal(1)
                for u in range(3):
                    spread(u)
                    maxima(u + 2)
                    normal(u + 2)
                if following:
                    split_queries(hd + 1, lo_of)
                spread(3)
                if following:
                    split_keys(hd + 1, lo_of)
                spread(4)
                rows = slice(s * VD, (s + 1) * VD)
                oh, ol = ot_hi[rows, bass.ds(t, 1), :][:, 0, :], ot_lo[rows, bass.ds(t, 1), :][:, 0, :]
                dve.wait_ge(s_ohi, hd * 2 + 1)
                lo_of(two(ol), bank(7)[0:VD].rearrange("p (a n) -> p a n", a=2), two(oh)).then_inc(s_olo, 1)
                dve.wait_ge(s_ohi, hd * 2 + 2)
                lo_of(pro(ol), bank(6, 384, 512)[0:VD], pro(oh)).then_inc(s_olo, 1)
                if following:
                    split_values(hd + 1, lo_of)

            nc.vector.memset(acc, 0.0).then_inc(s_acc, 1)
            dve.wait_ge(s_x, 16)
            for k in range(KT):
                add_square(0, k)
            dve.wait_ge(s_const, 16 * 4)
            for e in range(2):
                mod_add(e, 0, e)
            coefficients(0, 0, 2)
            for k in range(KT):
                lo_part(0, k)
            with dve.Fori(0, DEPTH) as l:
                base = l * LAYER_PAIRS
                e0 = l * MOD_BATCHES + 2
                ffn_step(l, 0, base, l * 3, ((e0, l, 2), (e0 + 2, l, 4)))
                mixer_step(l, base + FFN_PAIRS, l * 3 + 1)
                ffn_step(l, 1, base + FFN_PAIRS + MIX_PAIRS, l * 3 + 2, ((e0 + 4, 1, 0), None))
            inverse(3 * DEPTH)
            dve.wait_ge(s_rstd, 3 * DEPTH + 1)
            for k in range(KT):
                stt(out=x[:, k, :], in0=x[:, k, :], scalar=gains[:, 3 * DEPTH, k:k + 1], in1=rstd,
                    op0=ALU.mult, op1=ALU.mult).then_inc(s_y, 1)


def _tables():
    n = np.arange(SAMPLE)
    axis = ROPE // 2
    inv = 10000.0 ** (-np.arange(0, axis, 2, dtype=np.float32) / axis)
    ar = (n // GRID_W)[:, None].astype(np.float32) * inv.astype(np.float32)
    ac = (n % GRID_W)[:, None].astype(np.float32) * inv.astype(np.float32)
    cos = np.concatenate([np.cos(ar), np.cos(ar), np.cos(ac), np.cos(ac)], 1).T
    sin = np.concatenate([-np.sin(ar), np.sin(ar), -np.sin(ac), np.sin(ac)], 1).T
    rope = np.concatenate([np.ones((2 * ROPE, PROMPT)), np.concatenate([cos, sin], 0)], 1)
    rope[ROPE:, :PROMPT] = 0.0

    def dft(m, norm):
        a = 2 * np.pi * (np.outer(np.arange(m), np.arange(m)) % m) / m
        return np.cos(a) / norm, np.sin(a) / norm

    c, s = dft(FD, 8.0)
    per = P // FD
    chan = np.concatenate([np.kron(np.eye(per), c), -np.kron(np.eye(per), s)], 1)
    prompt = np.concatenate(dft(PROMPT, PROMPT ** 0.5), 1)
    sample = np.concatenate(dft(SAMPLE, SAMPLE ** 0.5), 1).reshape(SAMPLE // P, P, 2 * SAMPLE)
    return [np.ascontiguousarray(a, dtype=np.float32) for a in (rope, chan, prompt, sample)]


def _cols(sample, prompt):
    return np.concatenate([sample[..., :S2], prompt, sample[..., S2:]], -1)


def _tiles(w, width=P):
    *lead, k, n = w.shape
    w = w.reshape(*lead, k // P, P, n // width, width)
    w = np.moveaxis(w, -2, -4)
    w = np.swapaxes(w, -3, -2)
    return w.reshape(*w.shape[:-2], -1)


def _kernel_inputs(a):
    a = {k: np.asarray(v) for k, v in a.items()}
    L = DEPTH
    out = {}
    xs = _cols(a["x_sample"][0].T, a["x_prompt"][0].T)
    out["x"] = xs.reshape(KT, P, T).transpose(1, 0, 2)
    out["cond"] = np.stack([a["c"][0], a["c_ctx"]], -1).reshape(KT, P, 2).transpose(1, 0, 2)
    out["b_mod"] = a["b_mod"].reshape(L, N_MOD * KT, P).transpose(2, 0, 1)
    norms = np.stack([a["norm_ffn1"], a["norm_mix"], a["norm_ffn2"]], 1).reshape(3 * L, D)
    out["gains"] = np.concatenate([norms, a["final_norm"][None]]).reshape(3 * L + 1, KT, P).transpose(2, 0, 1)
    out["lat_gains"] = np.concatenate([a["q_norm"], a["kv_norm"]], 1).reshape(L, QT + CT, P).transpose(2, 0, 1)
    out["w_mod"] = a["w_mod"].reshape(L, KT, P, MOD_BATCHES, MB).transpose(0, 3, 1, 2, 4)
    gate = np.stack([_tiles(a["w_ffn1_gate"]), _tiles(a["w_ffn2_gate"])], 1)
    up = np.stack([_tiles(a["w_ffn1_up"]), _tiles(a["w_ffn2_up"])], 1)
    out["w_up"] = np.stack([gate, up], 3)
    down = np.stack([a["w_ffn1_down"], a["w_ffn2_down"]], 1).reshape(L, 2, 2, D_FF // 2, D)
    out["w_down"] = _tiles(down)
    w_in = a["w_in"]
    cut = np.cumsum([0, D_FOUR, Q_RANK, KV_RANK, ROPE, D, D])
    swap = np.concatenate([np.r_[8:16, 0:8], 16 + np.r_[8:16, 0:8]])
    rope_cols = w_in[..., cut[3]:cut[4]]
    parts = [w_in[..., cut[1]:cut[3]], w_in[..., cut[3] - NOPE:cut[3]], rope_cols, rope_cols[..., swap],
             w_in[..., 0:D_FOUR]]
    out["w_in"] = _tiles(np.concatenate(parts, -1))
    uq = a["w_uq"].reshape(L, Q_RANK, HEADS, QK)
    uq = np.concatenate([uq, uq[..., NOPE:][..., swap]], -1).reshape(L, Q_RANK, HEADS * P)
    ukv = a["w_ukv"].reshape(L, KV_RANK, HEADS, NOPE + VD)
    uk = ukv[..., :NOPE].reshape(L, KV_RANK, HEADS * NOPE)
    uv = ukv[..., NOPE:].reshape(L, KV_RANK, HEADS * VD)
    out["w_head"] = np.concatenate([_tiles(uq), _tiles(uk, NOPE), _tiles(uv, VD)], -1)
    gf, ga = _tiles(w_in[..., cut[4]:cut[5]]), _tiles(w_in[..., cut[5]:cut[6]])
    ap, fo = _tiles(a["w_attn_proj"]), _tiles(a["w_four"])
    out["w_merge"] = np.stack([np.concatenate([gf, ap[..., :3 * P]], -1),
                               np.concatenate([ga, ap[..., 3 * P:], fo], -1)], 2)
    out["w_out"] = _tiles(a["w_out"])
    out["past_ckv"] = a["cache_ckv"][0].transpose(0, 2, 1).reshape(L, CT, P, PAST).transpose(0, 2, 1, 3)
    out["past_krope"] = a["cache_krope"][0].transpose(0, 2, 1)
    rope, chan, prompt, sample = _tables()
    out["rope"] = _cols(rope[:, PROMPT:], rope[:, :PROMPT])
    out["dft_chan"], out["dft_prompt"], out["dft_sample"] = chan, prompt, sample
    return {k: np.ascontiguousarray(v) for k, v in out.items()}


def kernel(**inputs):
    import concourse.bacc as _bacc
    from concourse.bass_utils import run_bass_kernel_spmd as _run

    nc = _bacc.Bacc("TRN2", target_bir_lowering=False, num_devices=1)
    arrays, ins, outs = {}, {}, {}
    for name, a in _kernel_inputs(inputs).items():
        arrays[f"in_{name}"] = a
        ins[name] = nc.dram_tensor(f"in_{name}", a.shape, mybir.dt.from_np(a.dtype), kind="ExternalInput").ap()
    shapes = {"y": (P, KT, T), "ckv": (DEPTH, P, CT, PROMPT), "krope": (DEPTH, ROPE, PROMPT)}
    for name, shape in shapes.items():
        outs[name] = nc.dram_tensor(f"out_{name}", shape, F32, kind="ExternalOutput").ap()
    build(nc, ins, outs)
    r = _run(nc, [arrays], core_ids=[0]).results[0]
    y = r["out_y"].transpose(1, 0, 2).reshape(D, T)
    y_sample = np.concatenate([y[:, :S2], y[:, STEP:]], 1).T[None]
    y_prompt = y[:, PRO:PRO + PROMPT].T[None]
    ckv = r["out_ckv"].transpose(0, 3, 2, 1).reshape(1, DEPTH, PROMPT, KV_RANK)
    krope = r["out_krope"].transpose(0, 2, 1)[None]
    return tuple(np.ascontiguousarray(v) for v in (y_prompt, y_sample, ckv, krope))
```

```python
import numpy as np
import concourse.bass as bass
from concourse import mybir
from concourse.alu_op_type import AluOpType as ALU
from contextlib import ExitStack

F32 = mybir.dt.float32
F32R = mybir.dt.float32r
ACT = mybir.ActivationFunctionType
AX = mybir.AxisListType

P = 128
DEPTH = 2
D = 1024
KT = D // P
D_FF = 2816
FH = D_FF // P // 2
SAMPLE, PROMPT, PAST = 512, 128, 256
T = SAMPLE + PROMPT
HALF = T // 2
TB = T + 2
S2 = SAMPLE // 2
PRO = S2
STEP = S2 + PROMPT
TOK = [0, P, STEP, STEP + P, PRO]
KEYS = T + PAST
GRID_W = 64
HEADS, NOPE, ROPE, VD = 8, 64, 32, 64
QK = NOPE + ROPE
Q_RANK, KV_RANK = 384, 256
QT, CT = Q_RANK // P, KV_RANK // P
D_FOUR, FD = 256, 64
FT = D_FOUR // P
OT = HEADS * VD // P
EPS = 1e-6
SCALE = float(QK) ** -0.5
N_MOD = 9
MOD_BATCHES, MOD_COLS = 6, 384
MB = 4 * MOD_COLS

UP_W = KT * P
DOWN_W = FH * P
IN_W = KT * P
CHAN_W = 2 * P
PDFT_W = 2 * P
SDFT_W = 2 * SAMPLE
HEAD_W = QT * P + CT * (NOPE + VD)
MERGE_W = (2 * KT + OT + FT) * P // 2
OUT_W = KT * P
SLOT = DOWN_W

FFN_PAIRS = 2 * (FH + KT // 2)
IN_P, DFT_P, SEQ_P, HEAD_P, MERGE_P, OUT_P = 0, 4, 5, 7, 11, 19
MIX_PAIRS = OUT_P + KT // 2
LAYER_PAIRS = 2 * FFN_PAIRS + MIX_PAIRS
CREDIT = 2
UPD = 5 * KT
START = 1
XUPD0 = KT
UNITS = 5


def two(v):
    return bass.AP(v.tensor, v.offset, [v.ap[0], (STEP, 2), (1, S2)])


def pro(v):
    return v[:, PRO:PRO + PROMPT]


def groups(*views):
    return [(0, [two(v) for v in views]), (1, [pro(v) for v in views])]


def build(nc, i, o):
    ctx = ExitStack()
    with ctx:
        def sb(name, shape, dt=F32, where=ctx):
            return where.enter_context(nc.sbuf_tensor(name, shape, dt))

        def sem(name):
            return ctx.enter_context(nc.semaphore(name))

        x = sb("x", [P, KT, T])
        h_hi, h_lo = sb("h_hi", [P, KT, TB], F32R), sb("h_lo", [P, KT, TB], F32R)
        raw = [sb(f"raw{s}", [P, SLOT]) for s in range(2)]
        w_hi = [sb(f"w_hi{s}", [P, SLOT], F32R) for s in range(2)]
        w_lo = [sb(f"w_lo{s}", [P, SLOT], F32R) for s in range(2)]
        tmp = sb("tmp", [P, 6 * T])
        sq, std, ta, tb, lat_std, acc = [tmp[:, n * T:(n + 1) * T] for n in range(6)]
        rstd = sb("rstd", [P, T])[:]
        rope_tab = sb("rope_tab", [P, T])
        ones = sb("ones", [P, P])
        ident = sb("ident", [P, P])
        cond = sb("cond", [P, KT, 32])
        pick = sb("pick", [P, 2, 32])
        cond_in = sb("cond_in", [P, KT, 2])
        bmod = sb("bmod", [P, DEPTH, N_MOD * KT])
        gains = sb("gains", [P, DEPTH * 3 + 1, KT])
        lat_gain = sb("lat_gain", [P, DEPTH, QT + CT])
        mod = sb("mod", [P, 2, N_MOD * KT])
        scale_a = sb("scale_a", [P, 2, KT])
        half_g = sb("half_g", [P, 2, KT])
        mod_row = sb("mod_row", [P, MOD_COLS])
        eps = sb("eps", [P, 1])
        bias_a, bias_b = sb("bias_a", [P, 2]), sb("bias_b", [P, 2])
        nmx, rsum, rinv = [sb(n, [P, UNITS]) for n in ("nmx", "rsum", "rinv")]

        with ExitStack() as ffn:
            a_hi, a_lo = sb("a_hi", [P, FH, T], F32R, ffn), sb("a_lo", [P, FH, T], F32R, ffn)
            wm = [sb(f"wm{s}", [P, MB], F32, ffn) for s in range(2)]
            mod_acc = sb("mod_acc", [P, 2, MB], F32, ffn)
        with ExitStack() as start:
            wm_start = [sb(f"wm_start{n}", [P, MB], F32, start) for n in range(2 * KT - 2)]
            wm_start += [wm_start[0], tmp[:, 2 * T:2 * T + MB]]
        with ExitStack() as mix:
            fr_hi, fr_lo = sb("fr_hi", [P, FT, T], F32R, mix), sb("fr_lo", [P, FT, T], F32R, mix)
            with ExitStack() as four:
                uv_hi = sb("uv_hi", [P, UNITS, 2 * FT * P], F32R, four)
                uv_lo = sb("uv_lo", [P, UNITS, 2 * FT * P], F32R, four)
            ot_hi, ot_lo = sb("ot_hi", [P, OT, T], F32R, mix), sb("ot_lo", [P, OT, T], F32R, mix)
            with ExitStack() as att:
                qn_hi, qn_lo = sb("qn_hi", [P, QT, T], F32R, att), sb("qn_lo", [P, QT, T], F32R, att)
                cn_hi, cn_lo = sb("cn_hi", [P, CT, KEYS], F32R, att), sb("cn_lo", [P, CT, KEYS], F32R, att)
                k_hi, k_lo = sb("k_hi", [P, KEYS], F32R, att), sb("k_lo", [P, KEYS], F32R, att)
                with ExitStack() as pre:
                    lat = sb("lat", [P, QT + CT, T], F32, pre)
                    f_hi, f_lo = sb("f_hi", [P, FT, T], F32R, pre), sb("f_lo", [P, FT, T], F32R, pre)
                with ExitStack() as head:
                    q_hi, q_lo = sb("q_hi", [P, T], F32R, head), sb("q_lo", [P, T], F32R, head)
                    v_hi = sb("v_hi", [P, KEYS // P, VD], F32R, head)
                    v_lo = sb("v_lo", [P, KEYS // P, VD], F32R, head)
                    pt_hi = sb("pt_hi", [P, 2, SAMPLE + PAST], F32R, head)
                    pt_lo = sb("pt_lo", [P, 2, SAMPLE + PAST], F32R, head)
            with ExitStack() as mer:
                m_hi, m_lo = sb("m_hi", [P, KT, T], F32R, mer), sb("m_lo", [P, KT, T], F32R, mer)
        NK = SAMPLE + PAST
        probs = [tmp[:, u * NK:(u + 1) * NK] for u in range(2)]
        q32 = tmp[:, 2 * NK:2 * NK + T]
        rot = tmp[:, 2 * NK + T:2 * NK + 2 * T]
        vt = tmp[:, 2 * NK + 2 * T:2 * NK + 2 * T + KEYS]
        kr32, kr_sin, kr_cos = sq, std, ta
        lat_sq, lat_acc = tb, acc
        fourier_in = [std, ta]
        past_c = lat_std[:, 0:CT * PAST].rearrange("p (c n) -> p c n", c=CT)
        past_k = mod_row[:, 0:PAST]
        silu, prod = ta, tb
        sgf, sga, p1, p2 = sq, std, ta, tb

        ps = ctx.enter_context(nc.psum_tensor("ps", [P, 8 * 512], F32))

        def bank(b, n0=0, n1=512):
            return ps[:, b * 512 + n0:b * 512 + n1]

        def pair(j):
            return ps[:, j * 1024 + 512 - HALF:j * 1024 + 512 + HALF]

        def pairb(j):
            return ps[:, j * 1024 + 512 - HALF:j * 1024 + 512 - HALF + TB]

        def shifts(j, p0=0):
            return ps[p0:P, j * 1024 + 512 + HALF:j * 1024 + 512 - HALF + TB]

        def halves(v):
            return [v[:, 0:HALF], v[:, HALF:]]

        s_raw = [sem(f"raw_loaded{s}") for s in range(2)]
        s_whi = sem("weight_hi_ready")
        s_split = sem("chunk_split")
        s_chunk = sem("chunk_used")
        s_wm = [sem(f"mod_weights_loaded{s}") for s in range(2)]
        s_start = [sem(f"first_mod_weights_loaded{n}") for n in range(2 * KT)]
        s_wmused = sem("mod_weights_used")
        s_modacc = sem("mod_products_added")
        s_modmm, s_modrow, s_modt, s_mod = sem("mod_rows_summed"), sem("mod_rows_copied"), \
            sem("mod_transposed"), sem("mod_ready")
        s_condin = sem("conditioning_loaded")
        s_const, s_fill, s_x = sem("constants_loaded"), sem("constants_filled"), sem("x_loaded")
        s_cond = sem("cond_ready")
        s_xupd, s_sq, s_acc = sem("x_updated"), sem("square_ready"), sem("squares_added")
        s_sum, s_std, s_rstd = sem("squares_summed"), sem("std_ready"), sem("rstd_ready")
        s_coef, s_half = sem("coefficients_ready"), sem("half_gates_ready")
        s_hhi, s_hlo, s_bhi, s_blo = sem("h_hi_ready"), sem("h_ready"), sem("shift_hi_ready"), sem("shift_ready")
        s_gsc, s_usc, s_latsc = sem("gate_scaled"), sem("up_scaled"), sem("latent_scaled")
        s_gfsc, s_gasc = sem("gate_f_scaled"), sem("gate_a_scaled")
        s_silu, s_prod, s_ahi, s_alo = sem("silu_ready"), sem("product_ready"), sem("a_hi_ready"), sem("a_ready")
        s_lat, s_flo = sem("latent_copied"), sem("f_ready")
        s_lsq, s_lacc, s_lsum, s_lstd = sem("latent_square"), sem("latent_squares_added"), \
            sem("latent_summed"), sem("latent_std")
        s_lrstd, s_latn, s_nhi, s_nlo = sem("latent_rstd"), sem("latent_normed"), \
            sem("latent_hi_ready"), sem("latent_ready")
        s_past = sem("past_loaded")
        s_kr, s_krhi, s_krlo = sem("key_rope_step"), sem("key_rope_hi"), sem("key_rope_ready")
        s_pasthi, s_pastlo = sem("past_hi"), sem("past_ready")
        s_chan, s_uvhi, s_uvlo = sem("channel_dft"), sem("uv_hi"), sem("uv_ready")
        s_frhi, s_frlo = sem("fourier_hi"), sem("fourier_ready")
        s_qmm = sem("q_product")
        s_vt, s_vmm = sem("values_copied"), sem("values_turned")
        s_q32, s_rot, s_qhi, s_qlo = sem("q_copied"), sem("q_rotate_step"), sem("q_hi_ready"), sem("q_ready")
        s_khi, s_klo, s_vhi, s_vlo = sem("k_hi_ready"), sem("k_ready"), sem("v_hi_ready"), sem("v_ready")
        s_s, s_nmx, s_exp = sem("scores_ready"), sem("neg_max_ready"), sem("exp_ready")
        s_rinv, s_pn, s_pt, s_pthi, s_ptlo = sem("row_inverse"), sem("probs_ready"), \
            sem("probs_transposed"), sem("probs_t_hi"), sem("probs_t_ready")
        s_pv, s_ohi, s_olo = sem("values_mixed"), sem("o_hi_ready"), sem("o_ready")
        s_gf, s_op, s_ga = sem("gate_f_product"), sem("attn_out_product"), sem("gate_a_product")
        s_sgf, s_sga, s_p1, s_p2, s_m = sem("sigmoid_f"), sem("sigmoid_a"), sem("gated_fourier"), \
            sem("gated_attention"), sem("merged")
        s_mhi, s_mlo = sem("merged_hi"), sem("merged_ready")
        s_out, s_y = sem("outputs_written"), sem("y_ready")

        block = ctx.enter_context(nc.Block())

        def used(p, s):
            return (p * 2 + s) + 1 + CREDIT

        @block.sync
        def _(sp):
            sp.dma_start(cond_in[:], i["cond"]).then_inc(s_condin, 16)
            for dst, src in ((bmod, i["b_mod"]), (gains, i["gains"]),
                             (lat_gain, i["lat_gains"])):
                sp.dma_start(dst[:], src).then_inc(s_const, 16)
            sp.dma_start(rope_tab[NOPE:P, :], i["rope"]).then_inc(s_const, 16)
            sp.dma_start(x[:], i["x"]).then_inc(s_x, 16)

            def load(p, s, width, src):
                sp.wait_ge(s_split, p * 2 + s + 1)
                sp.dma_start(raw[s][:, 0:width], src).then_inc(s_raw[s], 16)

            def ffn_chunks(l, f, base):
                for half in range(2):
                    up = base + half * (FH + KT // 2)
                    with sp.Fori(0, FH) as t:
                        for s in range(2):
                            load(up + t, s, UP_W, i["w_up"][l, f, t + half * FH, s])
                    with sp.Fori(0, KT // 2) as t:
                        for s in range(2):
                            load(up + FH + t, s, DOWN_W, i["w_down"][l, f, half, t * 2 + s])

            with sp.Fori(0, DEPTH) as l:
                base = l * LAYER_PAIRS
                ffn_chunks(l, 0, base)
                mixp = base + FFN_PAIRS
                with sp.Fori(0, 4) as t:
                    for s in range(2):
                        load(mixp + IN_P + t, s, IN_W, i["w_in"][l, t * 2 + s])
                load(mixp + DFT_P, 0, CHAN_W, i["dft_chan"])
                load(mixp + DFT_P, 1, PDFT_W, i["dft_prompt"])
                with sp.Fori(0, 2) as t:
                    for s in range(2):
                        load(mixp + SEQ_P + t, s, SDFT_W, i["dft_sample"][t * 2 + s])
                with sp.Fori(0, HEADS // 2) as t:
                    for s in range(2):
                        load(mixp + HEAD_P + t, s, HEAD_W, i["w_head"][l, t * 2 + s])
                with sp.Fori(0, KT) as t:
                    for s in range(2):
                        load(mixp + MERGE_P + t, s, MERGE_W, i["w_merge"][l, t, s])
                with sp.Fori(0, KT // 2) as t:
                    for s in range(2):
                        load(mixp + OUT_P + t, s, OUT_W, i["w_out"][l, t * 2 + s])
                ffn_chunks(l, 1, mixp + MIX_PAIRS)
            for k in range(KT):
                sp.wait_ge(s_y, k + 1)
                sp.dma_start(o["y"][:, k], x[:, k, :]).then_inc(s_out, 16)
            sp.wait_ge(s_out, 16 * (2 * DEPTH + KT))

        @block.gpsimd
        def _(pool):
            pool.sem_inc(s_split, CREDIT)
            pool.sem_inc(s_rot, START)
            nc.gpsimd.memset(ones[:], 1.0).then_inc(s_fill, 1)
            nc.gpsimd.memset(eps[:], EPS).then_inc(s_fill, 1)
            nc.gpsimd.memset(cond[:], 0.0).then_inc(s_fill, 1)
            nc.gpsimd.memset(ident[:], 0.0).then_inc(s_fill, 1)
            nc.gpsimd.memset(pick[:], 0.0).then_inc(s_fill, 1)
            pool.wait_ge(s_fill, 5)
            for g in range(2):
                nc.gpsimd.memset(pick[:, g, g:g + 1], 1.0).then_inc(s_fill, 1)
            nc.gpsimd.affine_select(out=ident[:], in_=ident[:], compare_op=ALU.not_equal, fill=1.0, base=0,
                                    pattern=[[-1, P]], channel_multiplier=1).then_inc(s_fill, 1)

            def split(p, s, width, rotated=None):
                if rotated is not None:
                    pool.wait_ge(s_rot, rotated * 3 + START)
                r, hi, lo = raw[s][:, 0:width], w_hi[s][:, 0:width], w_lo[s][:, 0:width]
                pool.wait_ge(s_raw[s], (p + 1) * 16)
                pool.wait_ge(s_chunk, p * 2 + s + 1)
                nc.gpsimd.tensor_tensor(hi, r, ones[:, 0:1].to_broadcast([P, width]), ALU.mult).then_inc(s_whi, 1)
                pool.wait_ge(s_whi, p * 2 + s + 1)
                nc.gpsimd.tensor_tensor(lo, r, hi.bitcast(F32), ALU.subtract).then_inc(s_split, 1)

            def pairs(first, count, width, rotated=None):
                with pool.Fori(0, count) as t:
                    for s in range(2):
                        split(first + t, s, width, rotated)

            def ffn_chunks(base):
                for half in range(2):
                    up = base + half * (FH + KT // 2)
                    pairs(up, FH, UP_W)
                    pairs(up + FH, KT // 2, DOWN_W)

            def rotate(hd):
                pool.wait_ge(s_q32, hd + 1)
                nc.gpsimd.tensor_tensor(rot[NOPE:QK], q32[QK:P], rope_tab[QK:P, :], ALU.mult).then_inc(s_rot, 1)
                pool.wait_ge(s_rot, hd * 3 + 1 + START)
                nc.gpsimd.tensor_tensor(q32[NOPE:QK], q32[NOPE:QK], rope_tab[NOPE:QK, :], ALU.mult).then_inc(s_rot, 1)
                pool.wait_ge(s_rot, hd * 3 + 2 + START)
                nc.gpsimd.tensor_tensor(q32[NOPE:QK], q32[NOPE:QK], rot[NOPE:QK], ALU.add).then_inc(s_rot, 1)

            with pool.Fori(0, DEPTH) as l:
                base = l * LAYER_PAIRS
                ffn_chunks(base)
                mixp = base + FFN_PAIRS
                pairs(mixp + IN_P, 4, IN_W)
                split(mixp + DFT_P, 0, CHAN_W)
                split(mixp + DFT_P, 1, PDFT_W)
                pairs(mixp + SEQ_P, 2, SDFT_W)
                with pool.Fori(0, HEADS // 2) as t:
                    for s in range(2):
                        split(mixp + HEAD_P + t, s, HEAD_W, l * HEADS + t * 2 + s)
                        rotate(l * HEADS + t * 2 + s)
                pairs(mixp + MERGE_P, KT, MERGE_W, (l + 1) * HEADS)
                pairs(mixp + OUT_P, KT // 2, OUT_W)
                ffn_chunks(mixp + MIX_PAIRS)

        @block.tensor
        def _(pe):
            pe.sem_inc(s_chunk, CREDIT)
            pe.sem_inc(s_wmused, CREDIT)
            for started in (s_modmm, s_modt, s_pt, s_pv):
                pe.sem_inc(started, START)

            def product(outs, whi, wlo, xhi, xlo, first, last):
                for n, (out, v) in enumerate(zip(outs, xhi)):
                    nc.tensor.matmul(out, whi, v, start=first, stop=False)
                for out, v in zip(outs, xlo):
                    nc.tensor.matmul(out, whi, v, start=False, stop=False)
                for out, v in zip(outs, xhi):
                    mm = nc.tensor.matmul(out, wlo, v, start=False, stop=last)
                return mm

            def w_tile(s, n):
                return w_hi[s][:, n * P:(n + 1) * P], w_lo[s][:, n * P:(n + 1) * P]

            def dense(out, s, tiles, xhi, xlo, before=None, first=True, last=True):
                for n, (wt, k) in enumerate(tiles):
                    if before:
                        before(k)
                    mm = product(halves(out), *w_tile(s, wt), halves(xhi[:, k, :]), halves(xlo[:, k, :]),
                                 first and n == 0, last and n == len(tiles) - 1)
                return mm

            def chunk(p, s):
                pe.wait_ge(s_split, p * 2 + s + 1 + CREDIT)

            def norm_sum(nn):
                pe.wait_ge(s_acc, (nn + 1) * (KT + 1))
                for n in range(2):
                    mm = nc.tensor.matmul(halves(pair(3))[n], ones[:], halves(acc)[n], start=True, stop=True)
                mm.then_inc(s_sum, 1)

            def arriving(nn, k):
                if k == KT - 3:
                    norm_sum(nn)
                pe.wait_ge(s_hlo, nn * KT + k + 1 + START)

            def mod_step(e, k):
                n = e * KT + k
                pe.wait_ge(s_start[n], 16)
                if k == 0:
                    pe.wait_ge(s_modrow, e + START)
                for j in range(4):
                    mm = nc.tensor.matmul(bank(4)[32 * j:32 * j + 32, 0:MOD_COLS], cond[:, k, :],
                                          wm_start[n][:, j * MOD_COLS:(j + 1) * MOD_COLS],
                                          start=(k == 0), stop=(k == KT - 1))
                mm.then_inc(s_wmused, 1)

            def mod_sum(e):
                pe.wait_ge(s_modacc, (e - 1) * (KT + 1) + CREDIT)
                pe.wait_ge(s_modrow, e + START)
                for g in range(2):
                    for j in range(4):
                        mm = nc.tensor.matmul(bank(4)[32 * j:32 * j + 32, 0:MOD_COLS], pick[:, g, :],
                                              mod_acc[:, g, j * MOD_COLS:(j + 1) * MOD_COLS],
                                              start=(g == 0), stop=(g == 1))
                mm.then_inc(s_modmm, 1)

            def mod_turn(e):
                pe.wait_ge(s_modrow, e + 1 + START)
                pe.wait_ge(s_mod, e + START)
                for b in range(MOD_COLS // P):
                    mm = nc.tensor.transpose(bank(5)[:, b * P:(b + 1) * P], mod_row[:, b * P:(b + 1) * P], ident[:])
                mm.then_inc(s_modt, 1)

            def ffn_step(l, f, base, nn, hidden_mods, down_mods):
                every = [(k, k) for k in range(KT)]
                for half in range(2):
                    up = base + half * (FH + KT // 2)
                    g0 = (l * 2 + f) * 2 * FH + half * FH

                    def hidden_tile(t, first):
                        chunk(up + t, 0)
                        pe.wait_ge(s_silu, g0 + t + START)
                        if first and not half:
                            pe.wait_ge(s_blo, nn + 1)
                            pe.wait_ge(s_xupd, XUPD0 + l * UPD + f * 3 * KT - 1)
                        if half:
                            pe.wait_ge(s_xupd, XUPD0 + l * UPD + f * 3 * KT + KT - 1)
                        dense(pairb(0), 0, every, h_hi, h_lo,
                              (lambda k: arriving(nn, k)) if first and not half else None).then_inc(s_chunk, 1)
                        chunk(up + t, 1)
                        pe.wait_ge(s_prod, g0 + t + START)
                        if half:
                            pe.wait_ge(s_xupd, XUPD0 + l * UPD + f * 3 * KT + KT)
                        dense(pairb(1), 1, every, h_hi, h_lo).then_inc(s_chunk, 1)

                    if half == 0:
                        hidden_tile(0, True)
                    with pe.Fori(1 - half, FH - 1) as t:
                        hidden_tile(t, False)
                    mod_sum(hidden_mods[half])
                    hidden_tile(FH - 1, False)
                    mod_turn(hidden_mods[half])
                    upd0 = XUPD0 + l * UPD + f * 3 * KT + half * KT

                    def down_tile(p, s, tile, mods=None):
                        chunk(up + FH + p, s)
                        pe.wait_ge(s_xupd, upd0 + tile - 1)
                        if s == 0:
                            pe.wait_ge(s_silu, g0 + FH + START)

                        def before(k):
                            if mods is not None and k == FH - 2:
                                mod_sum(mods)
                            pe.wait_ge(s_alo, g0 + k + 1 + START)
                        dense(pair(s), s, [(k, k) for k in range(FH)], a_hi, a_lo, before).then_inc(s_chunk, 1)

                    last = KT // 2 - 1
                    with pe.Fori(0, last) as t:
                        for s in range(2):
                            down_tile(t, s, t * 2 + s)
                    down_tile(last, 0, last * 2)
                    down_tile(last, 1, last * 2 + 1, down_mods[half])
                    if down_mods[half] is not None:
                        mod_turn(down_mods[half])

            def mixer_step(l, mixp, nn):
                for t in range(8):
                    chunk(mixp + IN_P + t // 2, t % 2)
                    if t >= 2:
                        pe.wait_ge(s_lat, l * 8 + t - 1)
                    if t == 0:
                        pe.wait_ge(s_blo, nn + 1)
                        pe.wait_ge(s_xupd, XUPD0 + l * UPD + 2 * KT - 1)
                    dense(pairb(t % 2), t % 2, [(k, k) for k in range(KT)], h_hi, h_lo,
                          (lambda k: arriving(nn, k)) if t == 0 else None).then_inc(s_chunk, 1)
                    if t >= 6:
                        pe.wait_ge(s_lacc, l * (QT + CT) + (QT if t == 6 else QT + CT))
                        for n in range(2):
                            mm = nc.tensor.matmul(halves(pair(t - 4))[n], ones[:], halves(lat_acc)[n],
                                                  start=True, stop=True)
                        mm.then_inc(s_lsum, 1)
                chunk(mixp + DFT_P, 0)
                pe.wait_ge(s_flo, (l + 1) * FT + START)
                bd_hi, bd_lo = w_hi[0][:, 0:CHAN_W], w_lo[0][:, 0:CHAN_W]
                for t in range(UNITS):
                    if t in (0, 2):
                        pe.wait_ge(s_latsc, l * 8 + 7 + t // 2)
                    if t == 4:
                        pe.wait_ge(s_uvlo, l * UNITS + 1)
                    for c in range(FT):
                        tok = slice(TOK[t], TOK[t] + P)
                        mm = product([bank(t % 4, c * CHAN_W, (c + 1) * CHAN_W)], f_hi[:, c, tok], f_lo[:, c, tok],
                                     [bd_hi], [bd_lo], True, True)
                    mm.then_inc(s_chan if t < 4 else s_chunk, 1)
                chunk(mixp + DFT_P, 1)
                pe.wait_ge(s_uvlo, (l + 1) * UNITS)
                for c in range(FT):
                    for n in range(2):
                        st = slice((2 * c + n) * P, (2 * c + n + 1) * P)
                        mm = product([bank(1, c * P, (c + 1) * P)], uv_hi[:, 4, st], uv_lo[:, 4, st],
                                     [w_hi[1][:, n * P:(n + 1) * P]], [w_lo[1][:, n * P:(n + 1) * P]], n == 0, n == 1)
                mm.then_inc(s_chunk, 1)
                for t in range(4):
                    chunk(mixp + SEQ_P + t // 2, t % 2)
                    for c in range(FT):
                        for n in range(2):
                            st = slice((2 * c + n) * P, (2 * c + n + 1) * P)
                            mv = slice(n * SAMPLE, (n + 1) * SAMPLE)
                            mm = product([bank(2 + c)], uv_hi[:, t, st], uv_lo[:, t, st],
                                         [w_hi[t % 2][:, mv]], [w_lo[t % 2][:, mv]],
                                         t == 0 and n == 0, t == 3 and n == 1)
                    mm.then_inc(s_chunk, 1)
                hd0, hp = l * HEADS, mixp + HEAD_P
                pe.wait_ge(s_nlo, (l + 1) * (QT + CT))
                pe.wait_ge(s_pastlo, (l + 1) * 2)
                pe.wait_ge(s_krlo, l + 1)
                queries(hd0, hp, 0, False)
                pe.wait_ge(s_frlo, (l + 1) * 3)
                queries(hd0, hp, 0, True)
                pe.wait_ge(s_q32, hd0 + 1)
                keys_values(0)
                attend(hd0, (hp, 1), True)
                attend(hd0 + 1, (hp + 1, 0))
                with pe.Fori(1, HEADS // 2 - 1) as t:
                    attend(hd0 + t * 2, (hp + t, 1))
                    attend(hd0 + t * 2 + 1, (hp + t + 1, 0))
                last = HEADS // 2 - 1
                attend(hd0 + last * 2, (hp + last, 1))
                attend(hd0 + last * 2 + 1, None)
                with pe.Fori(0, KT) as m:
                    n0 = l * KT + m
                    chunk(mixp + MERGE_P + m, 0)
                    pe.wait_ge(s_sgf, n0 + START)
                    dense(pairb(0), 0, [(k, k) for k in range(KT)], h_hi, h_lo).then_inc(s_gf, 1)
                    pe.wait_ge(s_p2, n0 + START)
                    pe.wait_ge(s_olo, (l + 1) * 2 * HEADS + START)
                    dense(pair(1), 0, [(KT + k, k) for k in range(3)], ot_hi, ot_lo, last=False).then_inc(s_chunk, 1)
                    chunk(mixp + MERGE_P + m, 1)
                    dense(pair(1), 1, [(KT, 3)], ot_hi, ot_lo, first=False).then_inc(s_op, 1)
                    pe.wait_ge(s_sga, n0 + START)
                    dense(pairb(2), 1, [(k, k) for k in range(KT)], h_hi, h_lo).then_inc(s_ga, 1)
                    pe.wait_ge(s_p1, n0 + START)
                    dense(pair(3), 1, [(KT + 1 + k, k) for k in range(FT)], fr_hi, fr_lo).then_inc(s_chunk, 1)
                upd0 = XUPD0 + l * UPD + 2 * KT
                with pe.Fori(0, KT // 2) as t:
                    for s in range(2):
                        chunk(mixp + OUT_P + t, s)
                        pe.wait_ge(s_xupd, upd0 + t * 2 + s - 1)
                        pe.wait_ge(s_p2 if s else s_sgf, (l + 1) * KT + START)
                        dense(pair(s), s, [(k, k) for k in range(KT)], m_hi, m_lo,
                              lambda k: pe.wait_ge(s_mlo, l * KT + k + 1 + START)).then_inc(s_chunk, 1)

            def queries(hd, p, s, tail):
                if not tail:
                    chunk(p, s)
                    pe.wait_ge(s_vlo, hd + START)
                out, cols = (bank(3, PAST, PAST + T - 512), slice(512, T)) if tail else (bank(4), slice(0, 512))
                for k in range(QT):
                    mm = product([out], *w_tile(s, k), [qn_hi[:, k, cols]], [qn_lo[:, k, cols]], k == 0, k == QT - 1)
                mm.then_inc(s_qmm, 1)

            def keys_values(s, cs=range(CT)):
                n1 = KEYS // 2
                for c in cs:
                    mm = product([bank(2 + n, 0, n1) for n in range(2)], *w_tile(s, QT + c),
                                 [cn_hi[:, c, n * n1:(n + 1) * n1] for n in range(2)],
                                 [cn_lo[:, c, n * n1:(n + 1) * n1] for n in range(2)], c == 0, c == CT - 1)
                if CT - 1 in cs:
                    mm.then_inc(s_chunk, 1)

            def turn_values(b):
                for n, col in enumerate(TOK[0:4] + [T, T + P, PRO]):
                    mm = nc.tensor.transpose(bank(b, n * VD, (n + 1) * VD), vt[NOPE:P, col:col + P], ident[NOPE:P, NOPE:P])
                mm.then_inc(s_vmm, 1)

            def attend(hd, following, first=False):
                u0 = hd * UNITS

                def scores(u):
                    if u == 0:
                        pe.wait_ge(s_qlo, hd + 1)
                        pe.wait_ge(s_klo, hd + 1)
                    if u >= 2:
                        pe.wait_ge(s_exp, u0 + u - 1 + START)
                    if u == 3 and following:
                        pe.wait_ge(s_q32, hd + 2)
                    st = slice(TOK[u], TOK[u] + P)
                    qh, ql = q_hi[0:QK, st], q_lo[0:QK, st]
                    b = 2 * (u % 2)
                    if u < 4:
                        product([bank(b)], qh, ql, [two(k_hi[0:QK, :])], [two(k_lo[0:QK, :])], True, True)
                        mm = product([bank(b + 1, 0, PAST)], qh, ql, [k_hi[0:QK, T:KEYS]], [k_lo[0:QK, T:KEYS]],
                                     True, True)
                    else:
                        mm = product([bank(b, 0, P)], qh, ql, [k_hi[0:QK, PRO:PRO + P]], [k_lo[0:QK, PRO:PRO + P]],
                                     True, True)
                    mm.then_inc(s_s, 1)

                def turn(u):
                    pe.wait_ge(s_pn, u0 + u + 1)
                    pe.wait_ge(s_ptlo, u0 + u + START)
                    for n in range(6 if u < 4 else 1):
                        mm = nc.tensor.transpose(bank(5 + n // 4, (n % 4) * P, (n % 4 + 1) * P),
                                                 probs[u % 2][:, n * P:(n + 1) * P], ident[:])
                    mm.then_inc(s_pt, 1)

                def values(u):
                    pe.wait_ge(s_ptlo, u0 + u + 1 + START)
                    if u == 0:
                        pe.wait_ge(s_vlo, hd + 1 + START)
                        pe.wait_ge(s_olo, hd * 2 + START)
                    out = bank(7, u * P, (u + 1) * P) if u < 4 else bank(6, 384, 512)
                    tiles = range(6) if u < 4 else [6]
                    for n, kt in enumerate(tiles):
                        mm = product([out[0:VD]], v_hi[:, kt, :], v_lo[:, kt, :],
                                     [pt_hi[:, u % 2, n * P:(n + 1) * P]], [pt_lo[:, u % 2, n * P:(n + 1) * P]],
                                     n == 0, n == len(tiles) - 1)
                    mm.then_inc(s_pv, 1)

                scores(0)
                if first:
                    pe.wait_ge(s_vt, hd + 1)
                scores(1)
                if first:
                    turn_values(5)
                if following:
                    queries(hd + 1, *following, False)
                for u in range(UNITS):
                    if following and u == 3:
                        pe.wait_ge(s_exp, u0 + 4 + START)
                        keys_values(following[1], [0])
                    turn(u)
                    if following and u == 3:
                        keys_values(following[1], [1])
                    if u + 2 < UNITS:
                        scores(u + 2)
                    if following and u == 0:
                        pe.wait_ge(s_exp, u0 + 2 + START)
                        queries(hd + 1, *following, True)
                    if u >= 1:
                        values(u - 1)
                if following:
                    pe.wait_ge(s_vt, hd + 2)
                values(UNITS - 1)
                if following:
                    turn_values(4)

            pe.wait_ge(s_fill, 8)
            pe.wait_ge(s_cond, 1)
            for e in range(2):
                for k in range(KT):
                    mod_step(e, k)
                mod_turn(e)
            with pe.Fori(0, DEPTH) as l:
                base = l * LAYER_PAIRS
                e0 = l * MOD_BATCHES + 2
                ffn_step(l, 0, base, l * 3, (e0, e0 + 2), (e0 + 1, e0 + 3))
                mixer_step(l, base + FFN_PAIRS, l * 3 + 1)
                ffn_step(l, 1, base + FFN_PAIRS + MIX_PAIRS, l * 3 + 2, (e0 + 4, e0 + 5), (None, None))
            norm_sum(3 * DEPTH)

        @block.scalar
        def _(act):
            for started in (s_modrow, s_silu, s_exp, s_sgf, s_sga):
                act.sem_inc(started, START)

            def mod_load(batch, k, s):
                e, le, b = batch
                act.wait_ge(s_modacc, (e - 2) * (KT + 1) + k + 2)
                act.dma_start(wm[s][:], i["w_mod"][le, b, k]).then_inc(s_wm[s], 16)

            def mod_copy(e, first=False):
                if first:
                    act.wait_ge(s_wmused, (e + 1) * KT + CREDIT)
                else:
                    act.wait_ge(s_modmm, e - 1 + START)
                act.wait_ge(s_modt, e + START)
                nc.scalar.activation(mod_row[:], bank(4, 0, MOD_COLS), ACT.Copy).then_inc(s_modrow, 1)

            def rms(nn):
                act.wait_ge(s_sum, nn + 1)
                nc.scalar.activation(std, pair(3), ACT.Sqrt, scale=1.0 / D, bias=eps[:, 0:1]).then_inc(s_std, 1)

            def split_shift(nn, j):
                act.wait_ge(s_coef, nn + 1)
                nc.scalar.activation(h_hi[:, :, T:TB], mod[:, :, 3 * j * KT:(3 * j + 1) * KT].rearrange("p g k -> p k g"),
                                     ACT.Copy).then_inc(s_bhi, 1)

            def prepare(nn, k, updates):
                act.wait_ge(s_coef, nn + 1)
                act.wait_ge(s_xupd, updates)
                act.wait_ge(s_acc, nn * (KT + 1) + k + 1)
                hi_part(k)
                nc.scalar.activation(sq, x[:, bass.ds(k, 1), :], ACT.Square).then_inc(s_sq, 1)

            def hi_part(k):
                for g, (v, hi) in groups(x[:, bass.ds(k, 1), :][:, 0, :], h_hi[:, bass.ds(k, 1), 0:T][:, 0, :]):
                    ins = nc.scalar.activation(hi, v, ACT.Copy, scale=scale_a[:, g, bass.ds(k, 1)])
                ins.then_inc(s_hhi, 1)

            def ffn_step(l, f, base, nn, hidden_mods, down_mods):
                for half in range(2):
                    up = base + half * (FH + KT // 2)
                    g0 = (l * 2 + f) * 2 * FH + half * FH
                    if half == 0:
                        rms(nn)

                    def hidden_tile(t):
                        act.wait_ge(s_gsc, g0 + t + 1)
                        for g, (v,) in groups(silu):
                            ins = nc.scalar.activation(v, v, ACT.Silu, bias=bias_a[:, g:g + 1])
                        ins.then_inc(s_silu, 1)
                        act.wait_ge(s_prod, g0 + t + 1 + START)
                        nc.scalar.activation(a_hi[:, bass.ds(t, 1), :], prod, ACT.Copy).then_inc(s_ahi, 1)

                    with act.Fori(0, KT // 2) as t:
                        for s in range(2):
                            mod_load(hidden_mods[half], t * 2 + s, s)
                            hidden_tile(t * 2 + s)
                    for t in range(KT, FH - 1):
                        hidden_tile(t)
                    mod_copy(hidden_mods[half][0])
                    hidden_tile(FH - 1)
                    if half == 1:
                        split_shift(nn + 1, (2 * f + 1) % 3)
                    upd0 = XUPD0 + l * UPD + f * 3 * KT + half * KT
                    batch, last = down_mods[half], KT // 2 - 1
                    if batch is not None:
                        for s in range(2):
                            mod_load(batch, s, s)
                    if half == 0 and batch is None:
                        continue
                    with act.Fori(0, last) as t:
                        for s in range(2):
                            if half == 1:
                                prepare(nn + 1, t * 2 + s, upd0 + t * 2 + s + 1)
                            if batch is not None:
                                mod_load(batch, t * 2 + s + 2, s)
                    for s in range(2):
                        if s == 1 and batch is not None:
                            mod_copy(batch[0])
                        if half == 1:
                            prepare(nn + 1, last * 2 + s, upd0 + last * 2 + s + 1)

            def mixer_step(l, mixp, nn):
                rms(nn)
                act.wait_ge(s_chunk, used(mixp + IN_P, 0))
                act.dma_start(past_c, i["past_ckv"][l]).then_inc(s_past, 16)
                act.dma_start(past_k[NOPE:QK, :], i["past_krope"][l]).then_inc(s_past, 16)

                def latent(t0, t1, nsum, width):
                    act.wait_ge(s_lsum, l * 2 + nsum + 1)
                    if nsum:
                        act.wait_ge(s_latn, l * (QT + CT) + QT)
                    nc.scalar.activation(lat_std, pair(2 + nsum), ACT.Sqrt, scale=1.0 / width,
                                         bias=eps[:, 0:1]).then_inc(s_lstd, 1)
                    for t in range(t0, t1):
                        act.wait_ge(s_latn, l * (QT + CT) + t + 1)
                        hi = qn_hi[:, t, :] if t < QT else cn_hi[:, t - QT, 0:T]
                        nc.scalar.activation(hi, lat[:, t, :], ACT.Copy).then_inc(s_nhi, 1)

                for t in range(8):
                    p, s = mixp + IN_P + t // 2, t % 2
                    dst = fourier_in[t] if t < FT else lat[:, t - FT, :] if t < 7 else kr32
                    out = f_hi[:, t, :] if t < FT else dst
                    p0 = NOPE if t == 7 else 0
                    b = (bias_a, bias_b)[s]
                    act.wait_ge(s_latsc, l * 8 + t + 1)
                    for g, (v, to) in groups(dst, out):
                        ins = nc.scalar.activation(to[p0:P], v[p0:P], ACT.Identity, bias=b[p0:P, g:g + 1])
                    ins.then_inc(s_lat, 1)
                    if t == 2:
                        act.wait_ge(s_past, (l + 1) * 32)
                        nc.scalar.activation(cn_hi[:, :, T:KEYS], past_c, ACT.Copy).then_inc(s_pasthi, 1)
                        nc.scalar.activation(k_hi[NOPE:QK, T:KEYS], past_k[NOPE:QK, :], ACT.Copy).then_inc(s_pasthi, 1)
                act.wait_ge(s_lat, (l + 1) * 8)
                act.dma_start(o["krope"][l], kr32[NOPE:QK, PRO:PRO + PROMPT]).then_inc(s_out, 16)
                for t in range(UNITS):
                    if t < 4:
                        act.wait_ge(s_chan, l * 4 + t + 1)
                    else:
                        act.wait_ge(s_chunk, used(mixp + DFT_P, 0))
                    nc.scalar.activation(uv_hi[:, t, :], bank(t % 4), ACT.Copy).then_inc(s_uvhi, 1)
                act.wait_ge(s_kr, (l + 1) * 3)
                nc.scalar.activation(k_hi[NOPE:QK, 0:T], kr_cos[NOPE:QK], ACT.Copy).then_inc(s_krhi, 1)
                latent(0, QT, 0, Q_RANK)
                latent(QT, QT + CT, 1, KV_RANK)
                act.dma_start(o["ckv"][l], lat[:, QT:QT + CT, PRO:PRO + PROMPT]).then_inc(s_out, 16)
                act.wait_ge(s_chunk, used(mixp + DFT_P, 1))
                nc.scalar.activation(fr_hi[:, :, PRO:PRO + PROMPT],
                                     bank(1, 0, FT * P).rearrange("p (c n) -> p c n", c=FT),
                                     ACT.Copy).then_inc(s_frhi, 1)
                act.wait_ge(s_chunk, used(mixp + SEQ_P + 1, 1))
                for c in range(FT):
                    nc.scalar.activation(two(fr_hi[:, c, :]), bank(2 + c).rearrange("p (a n) -> p a n", a=2),
                                         ACT.Copy).then_inc(s_frhi, 1)
                hd0, hp, last = l * HEADS, mixp + HEAD_P, HEADS // 2 - 1
                act.wait_ge(s_out, (l + 1) * 32)
                act.wait_ge(s_frlo, (l + 1) * 3)
                queries(hd0, 0)
                queries(hd0, 1)
                keys(hd0, hp, 0)
                values_copy(hd0)
                split_queries(hd0)
                values(hd0, 5)
                with act.Fori(0, last) as t:
                    attend(hd0 + t * 2, 0, t, (hp + t, 1))
                    attend(hd0 + t * 2 + 1, 1, t, (hp + t + 1, 0))
                attend(hd0 + last * 2, 0, last, (hp + last, 1))
                attend(hd0 + last * 2 + 1, 1, last, None)
                with act.Fori(0, KT) as m:
                    n0 = l * KT + m
                    for scaled, buf, b, ready in ((s_gfsc, sgf, bias_a, s_sgf), (s_gasc, sga, bias_b, s_sga)):
                        act.wait_ge(scaled, n0 + 1)
                        for g, (v,) in groups(buf):
                            ins = nc.scalar.activation(v, v, ACT.Sigmoid, bias=b[:, g:g + 1])
                        ins.then_inc(ready, 1)
                    act.wait_ge(s_m, n0 + 1)
                    nc.scalar.activation(m_hi[:, bass.ds(m, 1), :], p1, ACT.Copy).then_inc(s_mhi, 1)
                split_shift(nn + 1, 2)
                upd0 = XUPD0 + l * UPD + 2 * KT
                with act.Fori(0, KT) as k:
                    prepare(nn + 1, k, upd0 + k + 1)

            def queries(hd, tail):
                act.wait_ge(s_qmm, hd * 2 + 1 + tail)
                v, cols = (bank(3, PAST, PAST + T - 512), slice(512, T)) if tail else (bank(4), slice(0, 512))
                ins = nc.scalar.activation(q32[:, cols], v, ACT.Copy, scale=SCALE)
                if tail:
                    ins.then_inc(s_q32, 1)

            def split_queries(hd):
                act.wait_ge(s_rot, (hd + 1) * 3 + START)
                nc.scalar.activation(q_hi[0:QK, :], q32[0:QK], ACT.Copy).then_inc(s_qhi, 1)

            def keys(hd, p, s):
                def both(v):
                    return v.rearrange("p (a n) -> p a n", a=2)

                act.wait_ge(s_chunk, used(p, s))
                kv = both(ps[:, 2 * 512:4 * 512])[:, :, 0:KEYS // 2]
                nc.scalar.activation(both(k_hi[0:NOPE, :]), kv[0:NOPE], ACT.Copy).then_inc(s_khi, 1)

            def values_copy(hd):
                for n in range(2):
                    ins = nc.scalar.activation(vt[NOPE:P, n * KEYS // 2:(n + 1) * KEYS // 2],
                                               bank(2 + n, 0, KEYS // 2)[NOPE:P], ACT.Copy)
                ins.then_inc(s_vt, 1)

            def values(hd, b):
                act.wait_ge(s_vmm, hd + 1)
                nc.scalar.activation(v_hi[:], bank(b, 0, 7 * VD), ACT.Copy).then_inc(s_vhi, 1)

            def attend(hd, s, t, following):
                u0 = hd * UNITS

                def exponent(u):
                    n = NK if u < 4 else P
                    act.wait_ge(s_nmx, u0 + u + 1)
                    act.wait_ge(s_pt, u0 + (u - 1 if u >= 2 else 0) + START)
                    nc.scalar.activation(probs[u % 2][:, 0:n], bank(2 * (u % 2))[:, 0:n] if n == P else
                                         ps[:, u % 2 * 1024:u % 2 * 1024 + n], ACT.Exp,
                                         bias=nmx[:, u:u + 1],
                                         accum_out=rsum[:, u:u + 1]).then_inc(s_exp, 1)

                def spread(u):
                    n = NK if u < 4 else P
                    act.wait_ge(s_pt, u0 + u + 1 + START)
                    act.wait_ge(s_pv, u0 + (u - 1 if u >= 2 else 0) + START)
                    nc.scalar.activation(pt_hi[:, u % 2, 0:n], ps[:, 5 * 512:5 * 512 + n], ACT.Copy).then_inc(s_pthi, 1)

                exponent(0)
                exponent(1)
                if following:
                    queries(hd + 1, 0)
                for u in range(3):
                    spread(u)
                    if following and u == 0:
                        queries(hd + 1, 1)
                    exponent(u + 2)
                if following:
                    split_queries(hd + 1)
                spread(3)
                if following:
                    keys(hd + 1, *following)
                    values_copy(hd + 1)
                spread(4)
                rows = slice(s * VD, (s + 1) * VD)
                act.wait_ge(s_pv, u0 + 4 + START)
                nc.scalar.activation(two(ot_hi[rows, bass.ds(t, 1), :][:, 0, :]),
                                     bank(7)[0:VD].rearrange("p (a n) -> p a n", a=2), ACT.Copy).then_inc(s_ohi, 1)
                act.wait_ge(s_pv, u0 + 5 + START)
                nc.scalar.activation(pro(ot_hi[rows, bass.ds(t, 1), :][:, 0, :]), bank(6, 384, 512)[0:VD],
                                     ACT.Copy).then_inc(s_ohi, 1)
                if following:
                    values(hd + 1, 4)

            for n in range(2 * KT):
                if n == KT:
                    act.wait_ge(s_condin, 16)
                    act.wait_ge(s_fill, 8)
                    nc.scalar.activation(cond[:, :, 0:2], cond_in[:], ACT.Silu).then_inc(s_cond, 1)
                if n == 2 * KT - 2:
                    act.wait_ge(s_wmused, CREDIT + 1)
                act.dma_start(wm_start[n][:], i["w_mod"][0, n // KT, n % KT]).then_inc(s_start[n], 16)
            act.wait_ge(s_x, 16)
            for k in range(KT):
                act.wait_ge(s_acc, k + 1)
                nc.scalar.activation(sq, x[:, k, :], ACT.Square).then_inc(s_sq, 1)
            for e in range(2):
                mod_copy(e, True)
            split_shift(0, 0)
            for k in range(KT):
                hi_part(k)
            with act.Fori(0, DEPTH) as l:
                base = l * LAYER_PAIRS
                e0 = l * MOD_BATCHES + 2
                ffn_step(l, 0, base, l * 3, ((e0, l, 2), (e0 + 2, l, 4)),
                         ((e0 + 1, l, 3), (e0 + 3, l, 5)))
                mixer_step(l, base + FFN_PAIRS, l * 3 + 1)
                ffn_step(l, 1, base + FFN_PAIRS + MIX_PAIRS, l * 3 + 2, ((e0 + 4, 1, 0), (e0 + 5, 1, 1)),
                         (None, None))
            rms(3 * DEPTH)

        @block.vector
        def _(dve):
            dve.sem_inc(s_xupd, XUPD0)
            for started in (s_mod, s_prod, s_alo, s_hlo, s_flo, s_ptlo, s_vlo, s_olo, s_p1, s_p2, s_mlo):
                dve.sem_inc(started, START)
            dve.sem_inc(s_modacc, CREDIT)
            tt, stt = nc.vector.tensor_tensor, nc.vector.scalar_tensor_tensor

            def xk(k):
                return x[:, bass.ds(k, 1), :][:, 0, :]

            def prepare(nn, k, updates):
                dve.wait_ge(s_coef, nn + 1)
                dve.wait_ge(s_xupd, updates)
                lo_part(nn, k)
                add_square(nn, k)

            def lo_part(nn, k):
                dve.wait_ge(s_hhi, nn * KT + k + 1)
                for g, (v, hi, lo) in groups(xk(k), h_hi[:, bass.ds(k, 1), 0:T][:, 0, :], h_lo[:, bass.ds(k, 1), 0:T][:, 0, :]):
                    ins = stt(out=lo, in0=v, scalar=scale_a[:, g, bass.ds(k, 1)], in1=hi.bitcast(F32),
                              op0=ALU.mult, op1=ALU.subtract)
                ins.then_inc(s_hlo, 1)

            def add_square(nn, k):
                dve.wait_ge(s_sq, nn * KT + k + 1)
                dve.wait_ge(s_acc, nn * (KT + 1) + k + 1)
                tt(acc, acc, sq, ALU.add).then_inc(s_acc, 1)

            def clear_acc(nn):
                dve.wait_ge(s_sum, nn)
                nc.vector.memset(acc, 0.0).then_inc(s_acc, 1)

            def mod_clear(e):
                dve.wait_ge(s_modmm, e - 2 + START)
                nc.vector.memset(mod_acc[:], 0.0).then_inc(s_modacc, 1)

            def mod_step(e, k, s):
                dve.wait_ge(s_wm[s], ((e - 2) * (KT // 2) + 1 + k[1]) * 16)
                dve.wait_ge(s_modacc, (e - 2) * (KT + 1) + 1 + k[0] + CREDIT)
                for g in range(2):
                    ins = stt(out=mod_acc[:, g, :], in0=wm[s][:], scalar=cond[:, bass.ds(k[0], 1), g],
                              in1=mod_acc[:, g, :], op0=ALU.mult, op1=ALU.add)
                ins.then_inc(s_modacc, 1)

            def mod_add(e, lb, b):
                dve.wait_ge(s_modt, e + 1 + START)
                cols = bank(5, 0, MOD_COLS).rearrange("p (b j r) -> p j b r", b=MOD_COLS // P, j=4)
                for g in range(2):
                    n = MB // P
                    ins = tt(mod[:, g, bass.ds(b * n, n)].rearrange("p (j b) -> p j b", j=4), cols[:, :, :, g],
                             bmod[:, bass.ds(lb, 1), bass.ds(b * n, n)][:, 0, :].rearrange("p (j b) -> p j b", j=4), ALU.add)
                ins.then_inc(s_mod, 1)

            def coefficients(nn, j, e_need):
                dve.wait_ge(s_mod, e_need + START)
                dve.wait_ge(s_hlo, nn * KT + START)
                for g in range(2):
                    ins = stt(out=scale_a[:, g, :], in0=mod[:, g, (3 * j + 1) * KT:(3 * j + 2) * KT], scalar=1.0,
                              in1=gains[:, bass.ds(nn, 1), :][:, 0, :], op0=ALU.add, op1=ALU.mult)
                ins.then_inc(s_coef, 1)
                dve.wait_ge(s_bhi, nn + 1)
                tt(h_lo[:, :, T:TB], mod[:, :, 3 * j * KT:(3 * j + 1) * KT].rearrange("p g k -> p k g"),
                   h_hi[:, :, T:TB].bitcast(F32), ALU.subtract).then_inc(s_blo, 1)

            def inverse(nn):
                dve.wait_ge(s_std, nn + 1)
                for n in range(2):
                    ins = nc.vector.reciprocal(halves(rstd)[n], halves(std)[n])
                ins.then_inc(s_rstd, 1)

            def update(k, src, gate, col):
                for g, (v, y) in groups(xk(k), src):
                    ins = stt(out=v, in0=y, scalar=gate[:, g, bass.ds(k + col, 1)], in1=v, op0=ALU.mult, op1=ALU.add)
                ins.then_inc(s_xupd, 1)

            def ffn_step(l, f, base, nn, hidden_mods, down_mods):
                j = 2 * f
                for half in range(2):
                    up = base + half * (FH + KT // 2)
                    g0 = (l * 2 + f) * 2 * FH + half * FH
                    mod_clear(hidden_mods[half][0])
                    if half == 0:
                        inverse(nn)

                    def hidden_tile(t):
                        dve.wait_ge(s_chunk, used(up + t, 0))
                        dve.wait_ge(s_alo, g0 + t + START)
                        dve.wait_ge(s_rstd, nn + 1)
                        nc.vector.tensor_copy(bias_a[:], shifts(0))
                        tt(silu, pair(0), rstd, ALU.mult).then_inc(s_gsc, 1)
                        dve.wait_ge(s_chunk, used(up + t, 1))
                        nc.vector.tensor_copy(bias_b[:], shifts(1))
                        tt(prod, pair(1), rstd, ALU.mult).then_inc(s_usc, 1)
                        dve.wait_ge(s_usc, g0 + t + 1)
                        dve.wait_ge(s_silu, g0 + t + 1 + START)
                        for g, (u, v) in groups(prod, silu):
                            ins = stt(out=u, in0=u, scalar=bias_b[:, g:g + 1], in1=v, op0=ALU.add, op1=ALU.mult)
                        ins.then_inc(s_prod, 1)
                        dve.wait_ge(s_prod, g0 + t + 1 + START)
                        dve.wait_ge(s_ahi, g0 + t + 1)
                        tt(a_lo[:, bass.ds(t, 1), :][:, 0, :], prod, a_hi[:, bass.ds(t, 1), :][:, 0, :].bitcast(F32),
                           ALU.subtract).then_inc(s_alo, 1)

                    with dve.Fori(0, KT // 2) as t:
                        for s in range(2):
                            hidden_tile(t * 2 + s)
                            mod_step(hidden_mods[half][0], (t * 2 + s, t), s)
                    for t in range(KT, FH):
                        hidden_tile(t)
                    mod_add(*hidden_mods[half])
                    if half == 0:
                        dve.wait_ge(s_xupd, XUPD0 + l * UPD + f * 3 * KT)
                        nc.vector.tensor_scalar(half_g[:], mod[:, :, (3 * j + 2) * KT:(3 * j + 3) * KT], 0.5, None,
                                                ALU.mult).then_inc(s_half, 1)
                    else:
                        clear_acc(nn + 1)
                        coefficients(nn + 1, (2 * f + 1) % 3, l * MOD_BATCHES + (4 if f == 0 else 8))
                    upd0 = XUPD0 + l * UPD + f * 3 * KT + half * KT
                    if down_mods[half] is not None:
                        mod_clear(down_mods[half][0])
                    with dve.Fori(0, 2) as t:
                        for m in range(4):
                            k = t * 4 + m
                            if down_mods[half] is not None:
                                mod_step(down_mods[half][0], (k, t * 2 + m // 2), m % 2)
                            dve.wait_ge(s_chunk, used(up + FH + t * 2 + m // 2, m % 2))
                            dve.wait_ge(s_half, l * 2 + f + 1)
                            update(k, pair(m % 2), half_g, 0)
                            if half == 1:
                                prepare(nn + 1, k, upd0 + k + 1)
                    if down_mods[half] is not None:
                        mod_add(*down_mods[half])

            def mixer_step(l, mixp, nn):
                lo_of = lambda out, src, hi: tt(out, src, hi.bitcast(F32), ALU.subtract)
                n5 = l * (QT + CT)
                def square(t):
                    dve.wait_ge(s_lat, l * 8 + FT + t + 1)
                    if t == QT:
                        dve.wait_ge(s_lsum, l * 2 + 1)
                    if t in (0, QT):
                        tt(lat_acc, lat[:, t, :], lat[:, t, :], ALU.mult).then_inc(s_lacc, 1)
                    else:
                        dve.wait_ge(s_lacc, n5 + t)
                        tt(lat_sq, lat[:, t, :], lat[:, t, :], ALU.mult).then_inc(s_lsq, 1)
                        dve.wait_ge(s_lsq, l * (QT + CT - 2) + (t if t < QT else t - 1))
                        tt(lat_acc, lat_acc, lat_sq, ALU.add).then_inc(s_lacc, 1)

                def latent(t0, t1, nsum):
                    dve.wait_ge(s_lstd, l * 2 + nsum + 1)
                    for n in range(2):
                        ins = nc.vector.reciprocal(halves(lat_std)[n], halves(lat_std)[n])
                    ins.then_inc(s_lrstd, 1)
                    dve.wait_ge(s_lrstd, l * 2 + nsum + 1)
                    for t in range(t0, t1):
                        stt(out=lat[:, t, :], in0=lat[:, t, :], scalar=lat_gain[:, bass.ds(l, 1), t],
                            in1=lat_std, op0=ALU.mult, op1=ALU.mult).then_inc(s_latn, 1)
                    for t in range(t0, t1):
                        dve.wait_ge(s_latn, n5 + t + 1)
                        dve.wait_ge(s_nhi, n5 + t + 1)
                        hi, lo = (qn_hi[:, t, :], qn_lo[:, t, :]) if t < QT else \
                            (cn_hi[:, t - QT, 0:T], cn_lo[:, t - QT, 0:T])
                        lo_of(lo, lat[:, t, :], hi).then_inc(s_nlo, 1)

                inverse(nn)

                def scale(t):
                    dve.wait_ge(s_chunk, used(mixp + IN_P + t // 2, t % 2))
                    dst = fourier_in[t] if t < FT else lat[:, t - FT, :] if t < 7 else kr32
                    p0 = NOPE if t == 7 else 0
                    dve.wait_ge(s_rstd, nn + 1)
                    if t in (2, 3):
                        dve.wait_ge(s_flo, l * FT + t - 1 + START)
                    nc.vector.tensor_copy((bias_a, bias_b)[t % 2][p0:P], shifts(t % 2, p0))
                    tt(dst[p0:P], pair(t % 2)[p0:P], rstd[p0:P], ALU.mult).then_inc(s_latsc, 1)

                for c in range(FT):
                    scale(c)
                    dve.wait_ge(s_latsc, l * 8 + c + 1)
                    dve.wait_ge(s_lat, l * 8 + c + 1)
                    for g, (v, hi, lo) in groups(fourier_in[c], f_hi[:, c, :], f_lo[:, c, :]):
                        ins = stt(out=lo, in0=v, scalar=(bias_a, bias_b)[c][:, g:g + 1], in1=hi.bitcast(F32),
                                  op0=ALU.add, op1=ALU.subtract)
                    ins.then_inc(s_flo, 1)
                for t in range(QT):
                    scale(FT + t)
                    square(t)
                    if t == 0:
                        dve.wait_ge(s_pasthi, (l + 1) * 2)
                        lo_of(cn_lo[:, :, T:KEYS], past_c, cn_hi[:, :, T:KEYS]).then_inc(s_pastlo, 1)
                        lo_of(k_lo[NOPE:QK, T:KEYS], past_k[NOPE:QK, :], k_hi[NOPE:QK, T:KEYS]).then_inc(s_pastlo, 1)
                for t in range(CT):
                    scale(FT + QT + t)
                for t in range(QT, QT + CT):
                    square(t)
                scale(7)
                for t in range(UNITS):
                    dve.wait_ge(s_uvhi, l * UNITS + t + 1)
                    lo_of(uv_lo[:, t, :], bank(t % 4), uv_hi[:, t, :]).then_inc(s_uvlo, 1)
                dve.wait_ge(s_lat, (l + 1) * 8)
                tt(kr_sin[NOPE:QK], kr32[QK:P], rope_tab[QK:P, :], ALU.mult).then_inc(s_kr, 1)
                tt(kr_cos[NOPE:QK], kr32[NOPE:QK], rope_tab[NOPE:QK, :], ALU.mult).then_inc(s_kr, 1)
                dve.wait_ge(s_kr, l * 3 + 2)
                tt(kr_cos[NOPE:QK], kr_cos[NOPE:QK], kr_sin[NOPE:QK], ALU.add).then_inc(s_kr, 1)
                dve.wait_ge(s_kr, (l + 1) * 3)
                dve.wait_ge(s_krhi, l + 1)
                lo_of(k_lo[NOPE:QK, 0:T], kr_cos[NOPE:QK], k_hi[NOPE:QK, 0:T]).then_inc(s_krlo, 1)
                latent(0, QT, 0)
                latent(QT, QT + CT, 1)
                dve.wait_ge(s_frhi, l * 3 + 1)
                lo_of(fr_lo[:, :, PRO:PRO + PROMPT], bank(1, 0, FT * P).rearrange("p (c n) -> p c n", c=FT),
                      fr_hi[:, :, PRO:PRO + PROMPT]).then_inc(s_frlo, 1)
                for c in range(FT):
                    dve.wait_ge(s_frhi, l * 3 + 2 + c)
                    lo_of(two(fr_lo[:, c, :]), bank(2 + c).rearrange("p (a n) -> p a n", a=2),
                          two(fr_hi[:, c, :])).then_inc(s_frlo, 1)
                hd0, last = l * HEADS, HEADS // 2 - 1
                dve.wait_ge(s_out, (l + 1) * 32)
                split_keys(hd0, lo_of)
                split_queries(hd0, lo_of)
                for s in range(2):
                    attend(hd0 + s, s, 0, lo_of, True, s == 0)
                with dve.Fori(1, last) as t:
                    for s in range(2):
                        attend(hd0 + t * 2 + s, s, t, lo_of, True)
                attend(hd0 + last * 2, 0, last, lo_of, True)
                attend(hd0 + last * 2 + 1, 1, last, lo_of, False)
                with dve.Fori(0, KT) as m:
                    n0 = l * KT + m
                    dve.wait_ge(s_gf, n0 + 1)
                    dve.wait_ge(s_mlo, n0 + START)
                    nc.vector.tensor_copy(bias_a[:], shifts(0))
                    tt(sgf, pair(0), rstd, ALU.mult).then_inc(s_gfsc, 1)
                    dve.wait_ge(s_ga, n0 + 1)
                    nc.vector.tensor_copy(bias_b[:], shifts(2))
                    tt(sga, pair(2), rstd, ALU.mult).then_inc(s_gasc, 1)
                    dve.wait_ge(s_op, n0 + 1)
                    dve.wait_ge(s_sga, n0 + 1 + START)
                    tt(p2, pair(1), sga, ALU.mult).then_inc(s_p2, 1)
                    dve.wait_ge(s_chunk, used(mixp + MERGE_P + m, 1))
                    dve.wait_ge(s_sgf, n0 + 1 + START)
                    tt(p1, pair(3), sgf, ALU.mult).then_inc(s_p1, 1)
                    dve.wait_ge(s_p1, n0 + 1 + START)
                    dve.wait_ge(s_p2, n0 + 1 + START)
                    tt(p1, p1, p2, ALU.add).then_inc(s_m, 1)
                    dve.wait_ge(s_m, n0 + 1)
                    dve.wait_ge(s_mhi, n0 + 1)
                    lo_of(m_lo[:, bass.ds(m, 1), :][:, 0, :], p1, m_hi[:, bass.ds(m, 1), :][:, 0, :]).then_inc(s_mlo, 1)
                clear_acc(nn + 1)
                coefficients(nn + 1, 2, l * MOD_BATCHES + 6)
                with dve.Fori(0, KT // 2) as t:
                    for s in range(2):
                        k = t * 2 + s
                        dve.wait_ge(s_chunk, used(mixp + OUT_P + t, s))
                        update(k, pair(s), mod, 5 * KT)
                        prepare(nn + 1, k, XUPD0 + l * UPD + 2 * KT + k + 1)

            def split_keys(hd, lo_of):
                dve.wait_ge(s_khi, hd + 1)
                lo_of(k_lo[0:NOPE, :].rearrange("p (a n) -> p a n", a=2),
                      ps[0:NOPE, 2 * 512:4 * 512].rearrange("p (a n) -> p a n", a=2)[:, :, 0:KEYS // 2],
                      k_hi[0:NOPE, :].rearrange("p (a n) -> p a n", a=2)).then_inc(s_klo, 1)

            def split_queries(hd, lo_of):
                dve.wait_ge(s_qhi, hd + 1)
                lo_of(q_lo[0:QK, :], q32[0:QK], q_hi[0:QK, :]).then_inc(s_qlo, 1)

            def split_values(hd, lo_of, b=4):
                dve.wait_ge(s_vhi, hd + 1)
                lo_of(v_lo[:].rearrange("p a n -> p (a n)"), bank(b, 0, 7 * VD),
                      v_hi[:].rearrange("p a n -> p (a n)")).then_inc(s_vlo, 1)

            def attend(hd, s, t, lo_of, following, first=False):
                u0 = hd * UNITS

                def maxima(u):
                    n = NK if u < 4 else P
                    dve.wait_ge(s_s, u0 + u + 1)
                    nc.vector.tensor_reduce(nmx[:, u:u + 1], ps[:, u % 2 * 1024:u % 2 * 1024 + n], AX.X,
                                            ALU.max, negate=True).then_inc(s_nmx, 1)

                def normal(u):
                    n = NK if u < 4 else P
                    dve.wait_ge(s_exp, u0 + u + 1 + START)
                    nc.vector.reciprocal(rinv[:, u:u + 1], rsum[:, u:u + 1]).then_inc(s_rinv, 1)
                    dve.wait_ge(s_rinv, u0 + u + 1)
                    pr = probs[u % 2][:, 0:n]
                    nc.vector.tensor_scalar(pr, pr, rinv[:, u:u + 1], None, ALU.mult).then_inc(s_pn, 1)

                def spread(u):
                    n = NK if u < 4 else P
                    dve.wait_ge(s_pthi, u0 + u + 1)
                    lo_of(pt_lo[:, u % 2, 0:n], ps[:, 5 * 512:5 * 512 + n], pt_hi[:, u % 2, 0:n]).then_inc(s_ptlo, 1)

                maxima(0)
                maxima(1)
                if first:
                    split_values(hd, lo_of, 5)
                normal(0)
                normal(1)
                for u in range(3):
                    spread(u)
                    maxima(u + 2)
                    normal(u + 2)
                if following:
                    split_queries(hd + 1, lo_of)
                spread(3)
                if following:
                    split_keys(hd + 1, lo_of)
                spread(4)
                rows = slice(s * VD, (s + 1) * VD)
                oh, ol = ot_hi[rows, bass.ds(t, 1), :][:, 0, :], ot_lo[rows, bass.ds(t, 1), :][:, 0, :]
                dve.wait_ge(s_ohi, hd * 2 + 1)
                lo_of(two(ol), bank(7)[0:VD].rearrange("p (a n) -> p a n", a=2), two(oh)).then_inc(s_olo, 1)
                dve.wait_ge(s_ohi, hd * 2 + 2)
                lo_of(pro(ol), bank(6, 384, 512)[0:VD], pro(oh)).then_inc(s_olo, 1)
                if following:
                    split_values(hd + 1, lo_of)

            nc.vector.memset(acc, 0.0).then_inc(s_acc, 1)
            dve.wait_ge(s_x, 16)
            for k in range(KT):
                add_square(0, k)
            dve.wait_ge(s_const, 16 * 4)
            for e in range(2):
                mod_add(e, 0, e)
            coefficients(0, 0, 2)
            for k in range(KT):
                lo_part(0, k)
            with dve.Fori(0, DEPTH) as l:
                base = l * LAYER_PAIRS
                e0 = l * MOD_BATCHES + 2
                ffn_step(l, 0, base, l * 3, ((e0, l, 2), (e0 + 2, l, 4)),
                         ((e0 + 1, l, 3), (e0 + 3, l, 5)))
                mixer_step(l, base + FFN_PAIRS, l * 3 + 1)
                ffn_step(l, 1, base + FFN_PAIRS + MIX_PAIRS, l * 3 + 2, ((e0 + 4, 1, 0), (e0 + 5, 1, 1)),
                         (None, None))
            inverse(3 * DEPTH)
            dve.wait_ge(s_rstd, 3 * DEPTH + 1)
            for k in range(KT):
                stt(out=x[:, k, :], in0=x[:, k, :], scalar=gains[:, 3 * DEPTH, k:k + 1], in1=rstd,
                    op0=ALU.mult, op1=ALU.mult).then_inc(s_y, 1)


def _tables():
    n = np.arange(SAMPLE)
    axis = ROPE // 2
    inv = 10000.0 ** (-np.arange(0, axis, 2, dtype=np.float32) / axis)
    ar = (n // GRID_W)[:, None].astype(np.float32) * inv.astype(np.float32)
    ac = (n % GRID_W)[:, None].astype(np.float32) * inv.astype(np.float32)
    cos = np.concatenate([np.cos(ar), np.cos(ar), np.cos(ac), np.cos(ac)], 1).T
    sin = np.concatenate([-np.sin(ar), np.sin(ar), -np.sin(ac), np.sin(ac)], 1).T
    rope = np.concatenate([np.ones((2 * ROPE, PROMPT)), np.concatenate([cos, sin], 0)], 1)
    rope[ROPE:, :PROMPT] = 0.0

    def dft(m, norm):
        a = 2 * np.pi * (np.outer(np.arange(m), np.arange(m)) % m) / m
        return np.cos(a) / norm, np.sin(a) / norm

    c, s = dft(FD, 8.0)
    per = P // FD
    chan = np.concatenate([np.kron(np.eye(per), c), -np.kron(np.eye(per), s)], 1)
    prompt = np.concatenate(dft(PROMPT, PROMPT ** 0.5), 1)
    sample = np.concatenate(dft(SAMPLE, SAMPLE ** 0.5), 1).reshape(SAMPLE // P, P, 2 * SAMPLE)
    return [np.ascontiguousarray(a, dtype=np.float32) for a in (rope, chan, prompt, sample)]


def _cols(sample, prompt):
    return np.concatenate([sample[..., :S2], prompt, sample[..., S2:]], -1)


def _tiles(w, width=P):
    *lead, k, n = w.shape
    w = w.reshape(*lead, k // P, P, n // width, width)
    w = np.moveaxis(w, -2, -4)
    w = np.swapaxes(w, -3, -2)
    return w.reshape(*w.shape[:-2], -1)


def _kernel_inputs(a):
    a = {k: np.asarray(v) for k, v in a.items()}
    L = DEPTH
    out = {}
    xs = _cols(a["x_sample"][0].T, a["x_prompt"][0].T)
    out["x"] = xs.reshape(KT, P, T).transpose(1, 0, 2)
    out["cond"] = np.stack([a["c"][0], a["c_ctx"]], -1).reshape(KT, P, 2).transpose(1, 0, 2)
    out["b_mod"] = a["b_mod"].reshape(L, N_MOD * KT, P).transpose(2, 0, 1)
    norms = np.stack([a["norm_ffn1"], a["norm_mix"], a["norm_ffn2"]], 1).reshape(3 * L, D)
    out["gains"] = np.concatenate([norms, a["final_norm"][None]]).reshape(3 * L + 1, KT, P).transpose(2, 0, 1)
    out["lat_gains"] = np.concatenate([a["q_norm"], a["kv_norm"]], 1).reshape(L, QT + CT, P).transpose(2, 0, 1)
    out["w_mod"] = a["w_mod"].reshape(L, KT, P, MOD_BATCHES, MB).transpose(0, 3, 1, 2, 4)
    gate = np.stack([_tiles(a["w_ffn1_gate"]), _tiles(a["w_ffn2_gate"])], 1)
    up = np.stack([_tiles(a["w_ffn1_up"]), _tiles(a["w_ffn2_up"])], 1)
    out["w_up"] = np.stack([gate, up], 3)
    down = np.stack([a["w_ffn1_down"], a["w_ffn2_down"]], 1).reshape(L, 2, 2, D_FF // 2, D)
    out["w_down"] = _tiles(down)
    w_in = a["w_in"]
    cut = np.cumsum([0, D_FOUR, Q_RANK, KV_RANK, ROPE, D, D])
    swap = np.concatenate([np.r_[8:16, 0:8], 16 + np.r_[8:16, 0:8]])
    rope_cols = w_in[..., cut[3]:cut[4]]
    parts = [w_in[..., 0:cut[3]], w_in[..., cut[3] - NOPE:cut[3]], rope_cols, rope_cols[..., swap]]
    out["w_in"] = _tiles(np.concatenate(parts, -1))
    uq = a["w_uq"].reshape(L, Q_RANK, HEADS, QK)
    uq = np.concatenate([uq, uq[..., NOPE:][..., swap]], -1).reshape(L, Q_RANK, HEADS * P)
    out["w_head"] = np.concatenate([_tiles(uq), _tiles(a["w_ukv"])], -1)
    gf, ga = _tiles(w_in[..., cut[4]:cut[5]]), _tiles(w_in[..., cut[5]:cut[6]])
    ap, fo = _tiles(a["w_attn_proj"]), _tiles(a["w_four"])
    out["w_merge"] = np.stack([np.concatenate([gf, ap[..., :3 * P]], -1),
                               np.concatenate([ga, ap[..., 3 * P:], fo], -1)], 2)
    out["w_out"] = _tiles(a["w_out"])
    out["past_ckv"] = a["cache_ckv"][0].transpose(0, 2, 1).reshape(L, CT, P, PAST).transpose(0, 2, 1, 3)
    out["past_krope"] = a["cache_krope"][0].transpose(0, 2, 1)
    rope, chan, prompt, sample = _tables()
    out["rope"] = _cols(rope[:, PROMPT:], rope[:, :PROMPT])
    out["dft_chan"], out["dft_prompt"], out["dft_sample"] = chan, prompt, sample
    return {k: np.ascontiguousarray(v) for k, v in out.items()}


def kernel(**inputs):
    import concourse.bacc as _bacc
    from concourse.bass_utils import run_bass_kernel_spmd as _run

    nc = _bacc.Bacc("TRN2", target_bir_lowering=False, num_devices=1)
    arrays, ins, outs = {}, {}, {}
    for name, a in _kernel_inputs(inputs).items():
        arrays[f"in_{name}"] = a
        ins[name] = nc.dram_tensor(f"in_{name}", a.shape, mybir.dt.from_np(a.dtype), kind="ExternalInput").ap()
    shapes = {"y": (P, KT, T), "ckv": (DEPTH, P, CT, PROMPT), "krope": (DEPTH, ROPE, PROMPT)}
    for name, shape in shapes.items():
        outs[name] = nc.dram_tensor(f"out_{name}", shape, F32, kind="ExternalOutput").ap()
    build(nc, ins, outs)
    r = _run(nc, [arrays], core_ids=[0]).results[0]
    y = r["out_y"].transpose(1, 0, 2).reshape(D, T)
    y_sample = np.concatenate([y[:, :S2], y[:, STEP:]], 1).T[None]
    y_prompt = y[:, PRO:PRO + PROMPT].T[None]
    ckv = r["out_ckv"].transpose(0, 3, 2, 1).reshape(1, DEPTH, PROMPT, KV_RANK)
    krope = r["out_krope"].transpose(0, 2, 1)[None]
    return tuple(np.ascontiguousarray(v) for v in (y_prompt, y_sample, ckv, krope))
```
